# Optimizing a Trainium2 kernel written in Bass

```python
import jax, jax.numpy as jnp
from jax import lax
import numpy as np

D_MODEL = 1024
BATCH = 1
SEQ = 512
DEPTH = 2

GRID_W = 64
CTX_LEN = 256

A_HEADS = 12
A_NOPE = 64
A_ROPE = 32
A_QK = A_NOPE + A_ROPE
A_V = 64
A_Q_RANK = 256
A_KV_RANK = 128
F_GROUPS = 4
F_CH = 64
F_WIDTH = F_GROUPS * F_CH
Q_END = A_Q_RANK
KV_END = Q_END + A_KV_RANK
R_END = KV_END + A_ROPE
A_IN = R_END + F_WIDTH
A_MIX = A_HEADS * A_V + F_WIDTH
C_HEADS = 16
C_DH = 64
C_WIDTH = C_HEADS * C_DH
WIN_R = 8
WIN_C = 16
D_FF = 2816
N_EXPERTS = 8
TOP_K = 2
D_FF_EXPERT = 1408

ROPE_THETA = 10000.0
EPS = 1e-6
Q_BLOCK = 128

kernel_name = "hybrid_mla_fourier_natten_moe_dit"

def rms_norm(x, g):
    x32 = x.astype(jnp.float32)
    y = x32 * lax.rsqrt(jnp.mean(x32 * x32, axis=-1, keepdims=True) + EPS)
    return (y * g.astype(jnp.float32)).astype(x.dtype)

def _axial_rope(t, rows, cols):
    n_pairs = A_ROPE // 2
    per_axis = n_pairs // 2
    inv = ROPE_THETA ** (-jnp.arange(per_axis, dtype=jnp.float32) / per_axis)
    ang = jnp.concatenate([rows.astype(jnp.float32)[:, None] * inv, cols.astype(jnp.float32)[:, None] * inv], axis=-1)
    cos = jnp.cos(ang)[:, None, :].astype(t.dtype)
    sin = jnp.sin(ang)[:, None, :].astype(t.dtype)
    tp = t.reshape(*t.shape[:-1], n_pairs, 2)
    t0, t1 = tp[..., 0], tp[..., 1]
    return jnp.stack([t0 * cos - t1 * sin, t0 * sin + t1 * cos], axis=-1).reshape(t.shape)

def _rope_tail(t, rows, cols):
    return jnp.concatenate([t[..., :A_NOPE], _axial_rope(t[..., A_NOPE:], rows, cols)], axis=-1)

def block_attention(q, k, v, scale):
    B, N, H, dq = q.shape
    nb = N // Q_BLOCK
    qb = q.reshape(B, nb, Q_BLOCK, H, dq).transpose(1, 0, 2, 3, 4)

    def one(qi):
        s = jnp.einsum('bqhd,bkhd->bhqk', qi, k).astype(jnp.float32) * scale
        p = jax.nn.softmax(s, axis=-1).astype(v.dtype)
        return jnp.einsum('bhqk,bkhd->bqhd', p, v)

    o = lax.map(one, qb)
    return o.transpose(1, 0, 2, 3, 4).reshape(B, N, H, v.shape[-1])

def _fourier(f):
    B, N, _ = f.shape
    f32 = f.astype(jnp.float32).reshape(B, N, F_GROUPS, F_CH)
    y = jnp.fft.fft2(f32, axes=(1, 3), norm='ortho').real
    return y.reshape(B, N, F_WIDTH).astype(f.dtype)

def _mla_q(q_lat, g_cq, w_uq, g_q):
    B, N, _ = q_lat.shape
    q = (rms_norm(q_lat, g_cq) @ w_uq).reshape(B, N, A_HEADS, A_QK)
    return rms_norm(q, g_q)

def _mla_kv(kv_lat, k_rope, g_ckv, w_ukv, g_k):
    B, N, _ = kv_lat.shape
    kv = (rms_norm(kv_lat, g_ckv) @ w_ukv).reshape(B, N, A_HEADS, A_NOPE + A_V)
    k_nope, v = kv[..., :A_NOPE], kv[..., A_NOPE:]
    k_r = jnp.broadcast_to(k_rope[:, :, None, :], (B, N, A_HEADS, A_ROPE))
    k = rms_norm(jnp.concatenate([k_nope, k_r], axis=-1), g_k)
    return k, v

def _mla_fourier_mixer(xn, cn, rows, cols, w_in, g_cq, g_ckv, w_uq, w_ukv, g_q, g_k, w_out, need_ctx):
    B, S, _ = xn.shape
    L = cn.shape[1]
    scale = A_QK ** -0.5
    px = xn @ w_in
    qx = _rope_tail(_mla_q(px[..., :Q_END], g_cq, w_uq, g_q), rows, cols)
    kx, vx = _mla_kv(px[..., Q_END:KV_END], px[..., KV_END:R_END], g_ckv, w_ukv, g_k)
    kx = _rope_tail(kx, rows, cols)
    if need_ctx:
        pc = cn @ w_in
        kc, vc = _mla_kv(pc[..., Q_END:KV_END], pc[..., KV_END:R_END], g_ckv, w_ukv, g_k)
    else:
        pc = cn @ w_in[:, Q_END:R_END]
        kc, vc = _mla_kv(pc[..., :A_KV_RANK], pc[..., A_KV_RANK:], g_ckv, w_ukv, g_k)
    k_all = jnp.concatenate([kx, kc], axis=1)
    v_all = jnp.concatenate([vx, vc], axis=1)
    ax = block_attention(qx, k_all, v_all, scale).reshape(B, S, A_HEADS * A_V)
    ox = jnp.concatenate([ax, _fourier(px[..., R_END:])], axis=-1) @ w_out
    if need_ctx:
        qc = _mla_q(pc[..., :Q_END], g_cq, w_uq, g_q)
        ac = block_attention(qc, kc, vc, scale).reshape(B, L, A_HEADS * A_V)
        oc = jnp.concatenate([ac, _fourier(pc[..., R_END:])], axis=-1) @ w_out
    else:
        oc = None
    return ox, oc

def _na_mixer(xn, cn, w_in, g_q, g_k, rpb, w_out, need_ctx):
    B, S, _ = xn.shape
    L = cn.shape[1]
    rows_n = S // GRID_W
    wr = min(WIN_R, rows_n)
    wc = min(WIN_C, GRID_W)
    scale = C_DH ** -0.5
    px = (xn @ w_in).reshape(B, S, 3, C_HEADS, C_DH)
    qx = rms_norm(px[:, :, 0], g_q)
    kx = rms_norm(px[:, :, 1], g_k)
    vx = px[:, :, 2]
    if need_ctx:
        pc = (cn @ w_in).reshape(B, L, 3, C_HEADS, C_DH)
        qc = rms_norm(pc[:, :, 0], g_q)
        kc = rms_norm(pc[:, :, 1], g_k)
        vc = pc[:, :, 2]
    else:
        pc = (cn @ w_in[:, C_WIDTH:]).reshape(B, L, 2, C_HEADS, C_DH)
        kc = rms_norm(pc[:, :, 0], g_k)
        vc = pc[:, :, 1]
    row_start = jnp.clip(jnp.arange(rows_n) - wr // 2, 0, rows_n - wr)
    col_pos = jnp.arange(GRID_W)
    col_idx = jnp.clip(col_pos - wc // 2, 0, GRID_W - wc)[:, None] + jnp.arange(wc)[None, :]
    rpb_c = rpb[:, :, col_idx - col_pos[:, None] + (WIN_C - 1)]
    k_grid = kx.reshape(B, rows_n, GRID_W, C_HEADS, C_DH)
    v_grid = vx.reshape(B, rows_n, GRID_W, C_HEADS, C_DH)
    q_rows = qx.reshape(B, rows_n, GRID_W, C_HEADS, C_DH).transpose(1, 0, 2, 3, 4)

    def one_row(args):
        r, qr = args
        start = row_start[r]
        kb = lax.dynamic_slice_in_dim(k_grid, start, wr, axis=1)
        vb = lax.dynamic_slice_in_dim(v_grid, start, wr, axis=1)
        ks = jnp.take(kb, col_idx, axis=2)
        vs = jnp.take(vb, col_idx, axis=2)
        dr = start + jnp.arange(wr) - r + (WIN_R - 1)
        bias = jnp.take(rpb_c, dr, axis=1).transpose(0, 2, 1, 3)
        s_loc = jnp.einsum('bqhd,baqchd->bhqac', qr, ks).astype(jnp.float32) * scale + bias[None].astype(jnp.float32)
        s_ctx = jnp.einsum('bqhd,blhd->bhql', qr, kc).astype(jnp.float32) * scale
        s = jnp.concatenate([s_loc.reshape(B, C_HEADS, GRID_W, wr * wc), s_ctx], axis=-1)
        p = jax.nn.softmax(s, axis=-1).astype(vs.dtype)
        p_loc = p[..., :wr * wc].reshape(B, C_HEADS, GRID_W, wr, wc)
        p_ctx = p[..., wr * wc:]
        return jnp.einsum('bhqac,baqchd->bqhd', p_loc, vs) + jnp.einsum('bhql,blhd->bqhd', p_ctx, vc)

    o = lax.map(one_row, (jnp.arange(rows_n), q_rows))
    ox = o.transpose(1, 0, 2, 3, 4).reshape(B, S, C_WIDTH) @ w_out
    if need_ctx:
        oc = block_attention(qc, kc, vc, scale).reshape(B, L, C_WIDTH) @ w_out
    else:
        oc = None
    return ox, oc

def _swiglu(h, wg, wu, wd):
    return (jax.nn.silu(h @ wg) * (h @ wu)) @ wd

def _moe(h, w_router, wg, wu, wd):
    logits = (h @ w_router).astype(jnp.float32)
    top_v, top_i = lax.top_k(logits, TOP_K)
    gates = jax.nn.softmax(top_v, axis=-1)
    combine = jnp.sum(jax.nn.one_hot(top_i, N_EXPERTS, dtype=jnp.float32) * gates[..., None], axis=-2).astype(h.dtype)
    out = jnp.zeros_like(h)
    for e in range(N_EXPERTS):
        out = out + combine[..., e, None] * _swiglu(h, wg[e], wu[e], wd[e])
    return out

def setup_inputs(seed: int = 0) -> dict:
    key = jax.random.key(seed)
    ks = iter(jax.random.split(key, 32))
    ne, no = (DEPTH + 1) // 2, DEPTH // 2

    def nrm(shape, scale):
        return jax.random.normal(next(ks), shape, jnp.float32) * scale

    def gain(shape):
        return 1.0 + nrm(shape, 0.05)

    D = D_MODEL
    return {
        "x": nrm((BATCH, SEQ, D), 1.0),
        "c": nrm((BATCH, D), 1.0),
        "ctx": nrm((BATCH, CTX_LEN, D), 1.0),
        "c_ctx": nrm((D,), 1.0),
        "w_mod": nrm((DEPTH, D, 6 * D), D ** -0.5),
        "b_mod": nrm((DEPTH, 6 * D), 0.01),
        "norm_g": gain((DEPTH, 2, D)),
        "a_w_in": nrm((ne, D, A_IN), D ** -0.5),
        "a_g_cq": gain((ne, A_Q_RANK)),
        "a_g_ckv": gain((ne, A_KV_RANK)),
        "a_w_uq": nrm((ne, A_Q_RANK, A_HEADS * A_QK), A_Q_RANK ** -0.5),
        "a_w_ukv": nrm((ne, A_KV_RANK, A_HEADS * (A_NOPE + A_V)), A_KV_RANK ** -0.5),
        "a_g_q": gain((ne, A_QK)),
        "a_g_k": gain((ne, A_QK)),
        "a_w_out": nrm((ne, A_MIX, D), A_MIX ** -0.5),
        "f_w_gate": nrm((ne, D, D_FF), D ** -0.5),
        "f_w_up": nrm((ne, D, D_FF), D ** -0.5),
        "f_w_down": nrm((ne, D_FF, D), D_FF ** -0.5),
        "c_w_in": nrm((no, D, 3 * C_WIDTH), D ** -0.5),
        "c_g_q": gain((no, C_DH)),
        "c_g_k": gain((no, C_DH)),
        "c_rpb": nrm((no, C_HEADS, 2 * WIN_R - 1, 2 * WIN_C - 1), 0.2),
        "c_w_out": nrm((no, C_WIDTH, D), C_WIDTH ** -0.5),
        "m_w_router": nrm((no, D, N_EXPERTS), D ** -0.5),
        "m_w_gate": nrm((no, N_EXPERTS, D, D_FF_EXPERT), D ** -0.5),
        "m_w_up": nrm((no, N_EXPERTS, D, D_FF_EXPERT), D ** -0.5),
        "m_w_down": nrm((no, N_EXPERTS, D_FF_EXPERT, D), D_FF_EXPERT ** -0.5),
    }

def reference(x, c, ctx, c_ctx, w_mod, b_mod, norm_g, a_w_in, a_g_cq, a_g_ckv, a_w_uq, a_w_ukv, a_g_q, a_g_k, a_w_out,
              f_w_gate, f_w_up, f_w_down, c_w_in, c_g_q, c_g_k, c_rpb, c_w_out, m_w_router, m_w_gate, m_w_up, m_w_down):
    B, S, D = x.shape
    L = ctx.shape[1]
    t = jnp.arange(S)
    rows = t // GRID_W
    cols = t % GRID_W
    sc = jax.nn.silu(c)
    scc = jax.nn.silu(c_ctx)[None]
    hx, hc = x, ctx
    for i in range(DEPTH):
        last = i == DEPTH - 1
        j = i // 2
        mx = (sc @ w_mod[i] + b_mod[i]).reshape(B, 6, D)
        mc = (scc @ w_mod[i] + b_mod[i]).reshape(1, 6, D)
        shx1, scx1, gx1, shx2, scx2, gx2 = [mx[:, k, None, :] for k in range(6)]
        shc1, scc1, gc1, shc2, scc2, gc2 = [mc[:, k, None, :] for k in range(6)]
        xn = rms_norm(hx, norm_g[i, 0]) * (1 + scx1) + shx1
        cn = rms_norm(hc, norm_g[i, 0]) * (1 + scc1) + shc1
        if i % 2 == 0:
            ox, oc = _mla_fourier_mixer(xn, cn, rows, cols, a_w_in[j], a_g_cq[j], a_g_ckv[j], a_w_uq[j], a_w_ukv[j],
                                        a_g_q[j], a_g_k[j], a_w_out[j], not last)
        else:
            ox, oc = _na_mixer(xn, cn, c_w_in[j], c_g_q[j], c_g_k[j], c_rpb[j], c_w_out[j], not last)
        hx = hx + gx1 * ox
        xn2 = rms_norm(hx, norm_g[i, 1]) * (1 + scx2) + shx2
        if last:
            h_all = xn2
        else:
            hc = hc + gc1 * oc
            cn2 = rms_norm(hc, norm_g[i, 1]) * (1 + scc2) + shc2
            h_all = jnp.concatenate([cn2, xn2], axis=1)
        if i % 2 == 0:
            y = _swiglu(h_all, f_w_gate[j], f_w_up[j], f_w_down[j])
        else:
            y = _moe(h_all, m_w_router[j], m_w_gate[j], m_w_up[j], m_w_down[j])
        if last:
            hx = hx + gx2 * y
        else:
            hc = hc + gc2 * y[:, :L]
            hx = hx + gx2 * y[:, L:]
    return hx


_drawn_inputs = setup_inputs


def setup_inputs(seed=0):
    import zlib

    import numpy as np

    out = dict(_drawn_inputs(seed))
    spreads = {}
    factors = {'a_g_cq': 8.0,
     'a_g_ckv': 2.822,
     'a_g_q': 4.584,
     'a_g_k': 3.912,
     'c_g_q': 3.952,
     'c_g_k': 8.0,
     'c_rpb': 3.691}
    for name, (base, spread) in spreads.items():
        noise = np.random.default_rng([zlib.crc32(name.encode()), seed]).standard_normal(out[name].shape)
        drawn = base * np.exp(spread * noise) if base else spread * noise
        out[name] = __import__('jax').numpy.asarray(drawn.astype(out[name].dtype))
    for name, factor in factors.items():
        out[name] = (out[name] * factor).astype(out[name].dtype)
    return out
```

```python
from contextlib import ExitStack

import numpy as np
import concourse.bass as bass
from concourse import mybir

F32 = mybir.dt.float32
F32R = mybir.dt.float32r
I32 = mybir.dt.int32
ALU = mybir.AluOpType
ACT = mybir.ActivationFunctionType
AX = mybir.AxisListType.X
ds = bass.ds

P = 128
D = 1024
KC = D // P
SEQ, CTX = 512, 256
T = SEQ + CTX
GRID_W, ROWS = 64, 8
EPS = 1e-6
A_HEADS, A_NOPE, A_ROPE, A_QK = 12, 64, 32, 96
A_QR, A_KVR = 256, 128
PAIRS0, PAIRS1 = A_HEADS // 2, 8
DH = 64
WIN_R, WIN_C = 8, 16
FF_CHUNKS = 22
EXPERTS, EX_CHUNKS = 8, 11
U = 1024
BIG = 1e30
BLK = 256
ITEMS = (2 * SEQ + EXPERTS * (BLK - 1)) // BLK
BIAS_TILES = 7
LOCAL = [([0, 1], 0), ([0, 1, 2], 2), ([1, 2, 3], 2), ([2, 3], 5)]

TR_MOD0, N_MOD = 0, 16
TR_AIN = TR_MOD0 + N_MOD
TR_PAIR0 = TR_AIN + 2
TR_OUT0 = TR_PAIR0 + PAIRS0
TR_MLP = TR_OUT0 + 3
TR_MOD1 = TR_MLP + FF_CHUNKS
TR_PAIR1 = TR_MOD1 + N_MOD
TR_OUT1 = TR_PAIR1 + PAIRS1
TR_EXP = TR_OUT1 + 3
TR_END = TR_EXP + EXPERTS * EX_CHUNKS


LO0, USED0 = 3, 1
NPT = [2, 2]


class At:

    def __init__(self, units, fills):
        self.u, self.f = units, fills


def plan():
    at, u, f = {}, [0, 0, 0], [0, 0, 0]
    for name, nu, nf in (("ain", (2, 2, 2), (1, 1, 0)), ("four", (2, 2, 2), (1, 1, 0)),
                         ("pr0", (PAIRS0,) * 3, (PAIRS0 // 2, PAIRS0 // 2, 0)),
                         ("out0", (3, 3, 2), (1, 1, 1)),
                         ("mlp", (3 * FF_CHUNKS,) * 3, (24, 24, 18)),
                         ("pr1", (PAIRS1,) * 3, (PAIRS1 // 2, PAIRS1 // 2, 0)),
                         ("out1", (3, 3, 2), (1, 1, 1)), ("exp", (0, 0, 0), (0, 0, 0))):
        at[name] = At(list(u), list(f))
        u = [x + y for x, y in zip(u, nu)]
        f = [x + y for x, y in zip(f, nf)]
    return at


AT = plan()
NORM_AT = {"n0": 0, "n1": 1, "n2": 4, "n3": 5}


def build(nc, io, stop_after=None):
    ctx = ExitStack()
    with ctx:
        _build(nc, io, ctx, stop_after)


def _build(nc, io, ctx, stop_after):
    def sem(name):
        return ctx.enter_context(nc.semaphore(name))

    at = [(nc.sbuf_base + 63) // 64 * 64]

    def place(name, shape, dt, offset=None):
        size = int(np.prod(shape[1:])) * 4
        off = at[0] if offset is None else offset
        t = nc.alloc_sbuf_tensor_at(name, shape, dt, offset=off)
        if offset is None:
            at[0] += (size + 31) // 32 * 32
        return t

    class Area:
        def __init__(self, start):
            self.at = start

        def __call__(self, name, shape, dt=F32):
            t = place(name, shape, dt, self.at)
            self.at += (int(np.prod(shape[1:])) * 4 + 31) // 32 * 32
            return t

        def pair(self, name, shape):
            return self(name + "_hi", shape, F32R), self(name + "_lo", shape, F32R)

    ones = place("ones", [P, P], F32)
    ident = place("ident", [P, P], F32)
    ones96 = place("ones96", [P, P], F32)
    ones64 = place("ones64", [P, P], F32)
    half2 = place("half2", [P, 2], F32)
    eps = place("eps", [P, 3], F32)
    cond = place("cond", [P, KC, 2], F32)
    scond = place("scond", [P, KC, 2], F32)
    bmod = place("bmod", [P, 2, 48], F32)
    mods = place("mods", [P, 2, 48, 2], F32)
    ng = place("ng", [P, 2, 2, KC], F32)
    nsc = place("nsc", [P, 2, 2, KC, 2], F32)
    gcol = place("gcol", [P, 8], F32)
    res = place("res", [P, KC, T], F32)
    raw = [place(f"raw{s}", [P, 3, U], F32) for s in range(3)]
    whi = [place(f"w_hi{r}", [P, U], F32R) for r in range(3)]
    wlo = [place(f"w_lo{r}", [P, U], F32R) for r in range(3)]
    x_start = at[0]
    att_start = x_start + 2 * KC * T * 4

    PS = ctx.enter_context(nc.psum_tensor("ps", [P, 8, 512], F32))

    def slot(s, a=0, b=1024):
        return PS[:, 2 * s:2 * s + 2, :].rearrange("p a b -> p (a b)")[:, a:b]

    def bank(b, a, n):
        return PS[:, b, a:a + n]

    ax = Area(x_start)
    xn = ax.pair("xn", [P, KC, T])
    an = Area(att_start)
    sqb = [an(f"sqb{i}", [P, T]) for i in range(2)]
    rstd = an("rstd", [P, T])
    zb = [an(f"zb{i}", [P, T]) for i in range(2)]
    xfb = [an(f"xfb{i}", [P, T]) for i in range(2)]

    ap_ = Area(att_start)
    plat = ap_("plat", [P, 6, T])
    ff_hl = ap_.pair("four_in", [P, 2, T])
    four_a = ap_.pair("four_a", [P, 6, 512])
    a0 = Area(x_start)
    cq = a0.pair("cq", [P, 2, T])
    ckv = a0.pair("ckv", [P, T])
    krope = a0("krope", [P, T])
    csg = a0("csg", [P, T])
    mix0 = a0("mix0", [P, KC, T])
    a0t = Area(att_start + 6 * T * 4)
    l0_sq = a0t("l0_sq", [P, 2, T])
    l0_rs = a0t("l0_rs", [P, 2, T])
    qtab = a0t("qtab", [P, T])
    ktab = a0t("ktab", [P, T])
    l0_t = a0t("l0_t", [P, 2, T])
    l0_x = a0t("l0_x", [P, 3, T])

    b0 = Area(att_start)
    q0 = b0.pair("q0", [P, 2, T])
    k0 = b0.pair("k0", [P, 2, T])
    v0 = b0.pair("v0", [P, 6, P])
    p0 = [b0(f"p0_{i}", [P, T]) for i in range(2)]
    pt0_start = b0.at
    pt0 = [b0.pair(f"pt0_{i}", [P, T]) for i in range(2)]
    b0.at = pt0_start
    qx0 = b0("qx0", [P, T])
    rk0 = b0("rk0", [P, T])
    kx0 = b0("kx0", [P, T])
    b0.at = pt0_start + 4 * T * 4
    sqq0 = b0("sqq0", [P, 2, T])
    sqk0 = b0("sqk0", [P, T])
    b1 = Area(att_start)
    mix1 = b1("mix1", [P, KC, SEQ])
    q1 = b1.pair("q1", [P, 2, SEQ])
    k1 = b1.pair("k1", [P, T])
    v1 = b1.pair("v1", [P, 6, P])
    p1 = [b1(f"p1_{i}", [P, 5 * P]) for i in range(2)]
    biasb = b1("biasb", [P, 2, BIAS_TILES * P])
    pt1_start = b1.at
    pt1 = [b1.pair(f"pt1_{i}", [P, 5 * P]) for i in range(2)]
    b1.at = pt1_start
    qx1 = b1("qx1", [P, SEQ])
    rk1 = b1("rk1", [P, T])
    b1.at = pt1_start + 4 * 5 * P * 4
    sq1 = b1("sq1", [P, T])
    asm = Area(max(b0.at, b1.at))
    rq = asm("rq", [P, 12])
    rqs = asm("rqs", [P, 12])
    nmax = asm("nmax", [P, 8])
    nneg = asm("nneg", [P, 8])
    rsum = asm("rsum", [P, 8])
    rinv = asm("rinv", [P, 8])
    o0 = Area(att_start)
    mix0_hl = o0.pair("mix0s", [P, KC, T])
    o1 = Area(x_start)
    mix1_hl = o1.pair("mix1s", [P, KC, SEQ])
    f_ = Area(x_start)
    xg = f_.pair("xg", [P, KC, BLK])
    hx = [f_(f"hx{i}", [P, BLK]) for i in range(3)]
    sg = [f_(f"sg{i}", [P, BLK]) for i in range(3)]
    hb = [f_.pair(f"hb{i}", [P, BLK]) for i in range(3)]
    fn_sq = [f_(f"fn_sq{i}", [P, SEQ]) for i in range(2)]
    fn_rs = f_("fn_rs", [P, SEQ])
    fn_z = [f_(f"fn_z{i}", [P, SEQ]) for i in range(2)]
    fn_x = [f_(f"fn_x{i}", [P, BLK]) for i in range(2)]
    nscr = f_("nscr", [P, KC, 3])
    nshr = f_("nshr", [P, KC, 3])
    ngtr = f_("ngtr", [P, KC, 3])
    xt = f_.pair("xt", [P, 4, D])
    xfm = [f_(f"xfm{i}", [P, SEQ]) for i in range(2)]
    wr = f_("wr", [P, KC, 8])
    tri = f_("tri", [P, P])
    iot = f_("iot", [P, BLK])
    ltj = f_("ltj", [P, 8, 8])
    itn = f_("itn", [P, ITEMS])
    lg = f_("lg", [P, 4, 8])
    r64 = f_("r64", [P, 4, 8, 8])
    r64b = f_("r64b", [P, 4, 8, 8])
    rank = f_("rank", [P, 4, 8])
    seltok = f_("seltok", [P, 4, 8])
    lmax = f_("lmax", [P, 4])
    wexp = f_("wexp", [P, 4, 8])
    comb = f_("comb", [P, 4, 8])
    wsum = f_("wsum", [P, 4])
    posn = f_("posn", [P, 4, 8])
    cnts = f_("cnts", [P, 8])
    nit = f_("nit", [P, 8])
    endi = f_("endi", [P, 8])
    starti = f_("starti", [P, 8])
    erow = f_("erow", [P, 8])
    oneh = f_("oneh", [P, ITEMS, 8])
    oneb = f_("oneb", [P, ITEMS, 8])
    tab = f_("tab", [P, 6, ITEMS])
    tabi = f_("tabi", [P, 6, ITEMS], I32)
    posi = f_("posi", [P, 4, ITEMS])
    cmbi = f_("cmbi", [P, 4, ITEMS])
    gm = f_("gm", [P, 4, BLK], F32R)
    gt = f_("gt", [P, 2, SEQ], F32R)
    wslot = f_("wslot", [P, 2])
    yx = [f_(f"yx{i}", [P, D]) for i in range(2)]
    yhl = f_.pair("yhl", [P, 2, D])
    assert max(f_.at, asm.at, o0.at, ap_.at, a0t.at) <= nc.sbuf_usable_end, (
        f_.at, asm.at, o0.at, ap_.at, a0t.at, nc.sbuf_usable_end)

    s_const = sem("s_const")
    s_fetch = sem("s_fetch")
    s_scond = sem("s_scond")
    s_phase = sem("s_phase")
    s_chain = sem("s_chain")
    m_full = [sem(f"m_raw_full{i}") for i in range(3)]
    m_used = sem("m_used")
    m_evac = sem("m_evac")
    raw_full = [sem(f"raw_full{i}") for i in range(3)]
    hi_ready = [sem(f"hi_ready{i}") for i in range(3)]
    lo_ready = [sem(f"lo_ready{i}") for i in range(3)]
    used = [sem(f"used{i}") for i in range(3)]
    nr = [sem(f"norm_{w}") for w in ("sq", "sum", "std", "rstd", "z", "x", "hi", "lo")]
    lin_evac = sem("lin_evac")
    mx_hi, mx_lo = sem("mix_hi"), sem("mix_lo")
    c_sem = [sem(f"c_{n}") for n in ("sq", "sum", "std", "x", "hi", "lo", "kr")]
    f_sem = [sem(f"f_{n}") for n in ("a", "ahi", "alo", "evac", "fhi", "flo")]
    at_names = ("qsq", "qx", "qhi", "qlo", "ksq", "ks", "kstd", "rk", "kx", "khi", "klo",
                "vhi", "vlo", "rq", "rqs", "rqd",
                "s", "max", "neg", "exp", "inv", "p", "t", "hi", "lo", "o", "oev")
    a_sem = [{n: sem(f"a{l}_{n}") for n in at_names} for l in range(2)]
    a_sem[1]["sadd"], a_sem[1]["bias"] = sem("a1_sadd"), sem("a1_bias")
    s_zero = sem("s_zero")
    ff = {n: {w: sem(f"{n}_{w}") for w in ("hm", "sg", "hh", "h")} for n in ("mlp", "exp")}
    y_evac = sem("y_evac")
    e_sem = {n: sem(f"e_{n}") for n in
             ("in", "xt", "xthi", "xtlo", "sel", "exps", "pos", "tab", "gm", "gmt", "gt", "xhi", "xlo",
              "sc", "ws", "wsc", "yx", "yhi", "ylo", "sct", "scev")}
    s_out = sem("s_out")

    block = ctx.enter_context(nc.Block())

    def mm3(pe, out, w, x, first, last, skip=False):
        for n, (a, b) in enumerate(((0, 0), (0, 1), (1, 0))):
            ins = pe.matmul(out, w[a], x[b], start=first and n == 0, stop=last and n == 2,
                            skip_group_check=skip)
        return ins

    def pieces(n):
        return [(0, n)] if n <= 512 else [(0, 512), (512, n)]

    PHASES = {n: k for k, n in enumerate((
        "mods0", "norm0", "ain", "lat", "four", "att0", "split0", "out0", "mlp", "mods1", "norm1",
        "att1", "split1", "out1", "router", "moe"))}

    def phase_end(eng, name):
        eng.drain().then_inc(s_phase, 1)
        eng.wait_ge(s_phase, 4 * (PHASES[name] + 1))

    def three(row):
        return row.rearrange("p (r u) -> p r u", r=3)

    def all_of(t):
        return t[tuple(slice(None) for _ in t.shape)]

    CONSTS = (("ident", ident), ("ones", ones), ("cond", cond), ("bmod", bmod), ("ng", ng), ("gcol", gcol),
              ("ones96", ones96), ("ones64", ones64), ("half2", half2), ("eps", eps), ("qtab", qtab),
              ("ktab", ktab), ("xT", res))
    E_CONSTS = (("wr", wr), ("tri", tri), ("iot", iot), ("ltj", ltj), ("itn", itn), ("erow", erow))

    @block.sync
    def _(sp):
        for name, tile in CONSTS:
            sp.dma_start(all_of(tile), io[name]).then_inc(s_const, 16)
        W = io["stream"]

        def slots_split(units):
            for r in range(3):
                sp.wait_ge(lo_ready[r], LO0 + units[r])

        def load(row, s, done):
            sp.dma_start(raw[s][:, :, :], three(row)).then_inc(done[s], 16)

        def load_dyn(row, s, done):
            sp.dma_start(raw[s][:, :, :], W[ds(row, 1)].rearrange("a p (r u) -> p (a r) u", r=3)
                         ).then_inc(done[s], 16)

        def load_mods(l):
            row0 = (TR_MOD0, TR_MOD1)[l]
            with sp.Fori(0, 5) as j:
                for s in range(3):
                    sp.wait_ge(m_used, j * 3 + (N_MOD * l + s + 1))
                    load_dyn(j * 3 + (row0 + s), s, m_full)
            sp.wait_ge(m_used, N_MOD * l + 16)
            load(W[row0 + 15], 0, m_full)

        def load_list(name, rows, slots):
            base = AT[name].u
            for n, row in enumerate(rows):
                if n >= slots:
                    for r in range(3):
                        sp.wait_ge(lo_ready[r], LO0 + base[r] + n - slots + 1)
                load(row, n % slots, raw_full)

        load_mods(0)
        sp.wait_ge(m_used, 3 + N_MOD)
        load_list("ain", [W[TR_AIN + n] for n in range(2)], 2)
        slots_split(AT["four"].u)
        load_list("four", [io["fourier"][n] for n in range(2)], 2)
        slots_split(AT["pr0"].u)
        load_list("pr0", [W[TR_PAIR0 + n] for n in range(PAIRS0)], 2)
        slots_split(AT["out0"].u)
        load_list("out0", [W[TR_OUT0 + n] for n in range(3)], 3)
        slots_split(AT["mlp"].u)

        def load_chunks(g0, row0, base):
            for c in range(EX_CHUNKS):
                sp.wait_ge(lo_ready[2], g0 + (base[2] + c + LO0 - (1 if c < 2 else 2)))
                sp.sem_inc(s_fetch, 1)
                load_dyn(row0 + c, c % 3, raw_full)

        with sp.Fori(0, 3) as t:
            with sp.Fori(0, 2) as half:
                load_chunks(t * 22 + half * 11, half * 11 + TR_MLP, AT["mlp"].u)
        slots_split(AT["pr1"].u)
        load_mods(1)
        sp.wait_ge(m_used, 3 + 2 * N_MOD)
        base = AT["pr1"].u
        for n in range(PAIRS1):
            if n >= 2:
                for r in range(3):
                    sp.wait_ge(lo_ready[r], LO0 + base[r] + n - 1)
            load(W[TR_PAIR1 + n], n % 2, raw_full)
            if n == 0:
                sp.wait_ge(s_phase, 4 * (PHASES["norm1"] + 1))
            else:
                sp.wait_ge(a_sem[1]["sadd"], 16 * n)
            sp.dma_start(biasb[:, :, :], io["bias"][n]).then_inc(a_sem[1]["bias"], 16)
        slots_split(AT["out1"].u)
        load_list("out1", [W[TR_OUT1 + n] for n in range(3)], 3)
        sp.wait_ge(s_phase, 4 * (PHASES["out1"] + 1))
        for name, tile in E_CONSTS:
            sp.dma_start(all_of(tile), io[name]).then_inc(e_sem["in"], 16)
        sp.wait_ge(e_sem["tab"], 1)
        slots_split(AT["exp"].u)
        with sp.Fori(0, ITEMS) as it:
            live = sp.value_load(tabi[0:1, 0, ds(it, 1)], min_val=0, max_val=1)
            row = sp.value_load(tabi[0:1, 1, ds(it, 1)], min_val=0, max_val=TR_END - EX_CHUNKS)
            with sp.If(live > 0):
                load_chunks(it * EX_CHUNKS, row, AT["exp"].u)
        sp.wait_ge(s_phase, 4 * (PHASES["moe"] + 1))
        sp.dma_start(io["out"], res[:, :, 0:SEQ]).then_inc(s_out, 16)
        sp.wait_ge(s_out, 16)

    def hi_unit(act, r, src, cols, s, n_full, n_used):
        act.wait_ge(raw_full[s], n_full * 16)
        act.wait_ge(used[r], n_used + USED0)
        act.activation(whi[r][:, 0:cols], src, ACT.Copy).then_inc(hi_ready[r], 1)

    def lo_unit(dve, r, src, cols, n):
        dve.wait_ge(hi_ready[r], n)
        dve.tensor_tensor(wlo[r][:, 0:cols], src, whi[r][:, 0:cols].bitcast(F32), ALU.subtract
                          ).then_inc(lo_ready[r], 1)

    def norm_pe(pe, nb, n, sq):
        SQ, SUM = nr[:2]
        for k in range(KC):
            pe.wait_ge(SQ, nb * 8 + (k + 1))
            for a, b in pieces(n):
                ins = pe.matmul(slot(3, a, b), ones[:, :], sq[k % 2][:, a:b], start=k == 0, stop=k == KC - 1)
            ins.then_inc(SUM, 1)

    def norm_act(act, nb, src, n, sq, rs, z, xf, cols, dst_hi):
        SQ, SUM, STD, RSTD, Z, X, HI, LO = nr
        for k in range(KC):
            if k >= 2:
                act.wait_ge(SUM, nb * 8 + (k - 1))
            act.activation(sq[k % 2][:, 0:n], src(k), ACT.Square).then_inc(SQ, 1)
        act.wait_ge(SUM, nb * 8 + 8)
        act.activation(rs[:, 0:n], slot(3, 0, n), ACT.Sqrt, bias=eps[:, 0:1], scale=1.0 / D).then_inc(STD, 1)
        for k in range(KC):
            act.wait_ge(Z, nb * 8 + (k + 1))
            if dst_hi is None:
                if k >= 2:
                    act.wait_ge(e_sem["xt"], k - 1)
            elif k >= 2:
                act.wait_ge(LO, nb * 8 + (k - 1))
            parts = cols(k)
            for a, b, scale, shift in parts:
                ins = act.activation(xf[k % 2][:, a:b], z[k % 2][:, a:b], ACT.Identity, bias=shift, scale=scale)
            ins.then_inc(X, 1)
            if dst_hi is not None:
                act.wait_ge(X, nb * 8 + (k + 1))
                act.activation(dst_hi(k), xf[k % 2][:, 0:n], ACT.Copy).then_inc(HI, 1)

    def norm_dve(dve, nb, src, n, rs, z, xf, dst_hi, dst_lo):
        SQ, SUM, STD, RSTD, Z, X, HI, LO = nr
        dve.wait_ge(STD, nb + 1)
        dve.reciprocal(rs[:, 0:n], rs[:, 0:n]).then_inc(RSTD, 1)
        dve.wait_ge(RSTD, nb + 1)
        for k in range(KC + 1):
            if k < KC:
                if k >= 2:
                    dve.wait_ge(X, nb * 8 + (k - 1))
                dve.tensor_tensor(z[k % 2][:, 0:n], src(k), rs[:, 0:n], ALU.mult).then_inc(Z, 1)
            if k >= 1 and dst_lo is not None:
                dve.wait_ge(HI, nb * 8 + k)
                dve.tensor_tensor(dst_lo(k - 1), xf[(k - 1) % 2][:, 0:n], dst_hi(k - 1).bitcast(F32),
                                  ALU.subtract).then_inc(LO, 1)

    def res_all(k):
        return res[:, k, :]

    def res_lat(k):
        return res[:, k, 0:SEQ]

    def res_block(t):
        return lambda k: res[:, k, ds(t * BLK, BLK)]

    def cols_all(l):
        return lambda k: [(0, SEQ, nsc[:, l, 0, k, 0:1], mods[:, l, k, 0:1]),
                          (SEQ, T, nsc[:, l, 0, k, 1:2], mods[:, l, k, 1:2])]

    def cols_block(t):
        return lambda k: [(0, BLK, nscr[:, k, ds(t, 1)], nshr[:, k, ds(t, 1)])]

    def cols_moe(k):
        return [(0, SEQ, nsc[:, 1, 1, k, 0:1], mods[:, 1, 3 * KC + k, 0:1])]

    def ffn_pe(pe, nm, g0, base, N, ymode, y_start, y_stop, y_wait):
        F = ff[nm]

        def down(c):
            pe.wait_ge(lo_ready[2], g0 + (base[2] + c + LO0 + 1))
            pe.wait_ge(F["h"], g0 + (c + 1))
            if c == 0:
                y_wait()
            first, last = y_start and c == 0, y_stop and c == EX_CHUNKS - 1
            if ymode == "channels":
                h = [t[:, 0:N] for t in hb[c % 3]]
                for m in range(KC):
                    o = bank(m // 2, (m % 2) * BLK, N)
                    for n, (a, b) in enumerate(((0, 0), (0, 1), (1, 0))):
                        ins = pe.matmul(o, (whi, wlo)[a][2][:, m * P:(m + 1) * P], h[b],
                                        start=first and n == 0 and m % 2 == 0, stop=last and n == 2,
                                        skip_group_check=True)
            else:
                for j in range(N // P):
                    for q in range(2):
                        ins = mm3(pe, bank(2 * j + q, 0, 512), [t[:, j * P:(j + 1) * P] for t in hb[c % 3]],
                                  [t[2][:, q * 512:(q + 1) * 512] for t in (whi, wlo)], first, last)
            ins.then_inc(used[2], 1)

        for c in range(EX_CHUNKS):
            pe.wait_ge(F["hm"], g0 + (c + 1))
            for r in range(2):
                pe.wait_ge(lo_ready[r], g0 + (base[r] + c + LO0 + 1))
                for k in range(KC):
                    ins = mm3(pe, bank(4 + c % 3, r * BLK, N),
                              [t[r][:, k * P:(k + 1) * P] for t in (whi, wlo)],
                              [t[:, k, 0:N] for t in xg], k == 0, k == KC - 1)
                ins.then_inc(used[r], 1)
            if c:
                down(c - 1)
        down(EX_CHUNKS - 1)

    def ffn_act(act, nm, g0, item, at_, N):
        F = ff[nm]

        def hi(r, c):
            hi_unit(act, r, raw[c % 3][:, r, :], U, c % 3,
                    item * [4, 4, 3][c % 3] + (at_.f[c % 3] + c // 3 + 1), g0 + (at_.u[r] + c))

        hi(0, 0)
        hi(1, 0)
        for c in range(EX_CHUNKS):
            if c < EX_CHUNKS - 1:
                hi(0, c + 1)
            act.wait_ge(used[1], g0 + (at_.u[1] + c + 1 + USED0))
            act.activation(sg[c % 3][:, 0:N], bank(4 + c % 3, 0, N), ACT.Silu).then_inc(F["sg"], 1)
            if c < EX_CHUNKS - 1:
                hi(1, c + 1)
            act.wait_ge(F["hm"], g0 + (c + 3))
            act.activation(hb[c % 3][0][:, 0:N], hx[c % 3][:, 0:N], ACT.Copy).then_inc(F["hh"], 1)
            hi(2, c)

    def ffn_dve(dve, nm, g0, at_, N):
        F = ff[nm]

        def lo(r, c):
            lo_unit(dve, r, raw[c % 3][:, r, :], U, g0 + (at_.u[r] + c + 1))

        lo(0, 0)
        lo(1, 0)
        for c in range(EX_CHUNKS):
            if c < EX_CHUNKS - 1:
                lo(0, c + 1)
            dve.wait_ge(F["sg"], g0 + (c + 1))
            dve.tensor_tensor(hx[c % 3][:, 0:N], sg[c % 3][:, 0:N], bank(4 + c % 3, BLK, N), ALU.mult
                              ).then_inc(F["hm"], 1)
            if c < EX_CHUNKS - 1:
                lo(1, c + 1)
            dve.wait_ge(F["hh"], g0 + (c + 1))
            dve.tensor_tensor(hb[c % 3][1][:, 0:N], hx[c % 3][:, 0:N], hb[c % 3][0][:, 0:N].bitcast(F32),
                              ALU.subtract).then_inc(F["h"], 1)
            lo(2, c)

    def steps_of(l):
        out = []
        for h in range(2):
            if l == 0:
                out += [(h, b, list(range(6)), 512, None) for b in range(4)]
                out += [(h, b, [4, 5], 0, None) for b in (4, 5)]
            else:
                out += [(h, b, LOCAL[b][0] + [4, 5], len(LOCAL[b][0]) * P, LOCAL[b][1]) for b in range(4)]
        return out

    def operands(l):
        return (q0, k0, v0, p0, pt0, mix0) if l == 0 else (q1, k1, v1, p1, pt1, mix1)

    def att_pe(pe, l, i):
        A = a_sem[l]
        q, k, v, p, pt, mix = operands(l)
        steps = steps_of(l)
        J = len(steps)

        def scores(j):
            h, b, tiles, nl, _ = steps[j]
            pe.wait_ge(A["oev"], i * J + (j + 1))
            s = j % 4
            qs = [t[:, h, b * P:(b + 1) * P] for t in q]
            if l == 0:
                runs = [(0, 0, 512), (512, 512, T)] if b < 4 else [(512, 512, T)]
                kk = [[t[:, h, x:y] for t in k] for _, x, y in runs]
            else:
                runs = [(0, tiles[0] * P, tiles[0] * P + nl), (512, 512, T)]
                kk = [[t[:, x:y] for t in k] for _, x, y in runs]
            for (o, x, y), ks in zip(runs, kk):
                ins = mm3(pe, slot(s, o, o + y - x), qs, ks, True, True)
            ins.then_inc(A["s"], 1)

        def turn(j):
            tiles = steps[j][2]
            pe.wait_ge(A["p"], i * J + (j + 1))
            for n in range(len(tiles)):
                ins = pe.transpose(slot(j % 4, n * P, (n + 1) * P), p[j % 2][:, n * P:(n + 1) * P], ident[:, :])
            ins.then_inc(A["t"], 1)

        def values(j):
            tiles = steps[j][2]
            pe.wait_ge(A["lo"], i * J + (j + 1))
            for n, kt in enumerate(tiles):
                ins = mm3(pe, slot(j % 4, 768, 896), [t[:, kt, :] for t in v],
                          [t[:, n * P:(n + 1) * P] for t in pt[j % len(pt)]], n == 0, n == len(tiles) - 1)
            ins.then_inc(A["o"], 1)

        for j in range(J + 3):
            if j < J:
                scores(j)
            if j >= 3:
                values(j - 3)
            if 1 <= j <= J:
                turn(j - 1)

    def att_act(act, l, i):
        A = a_sem[l]
        q, k, v, p, pt, mix = operands(l)
        steps = steps_of(l)
        J = len(steps)
        npt = NPT[l]

        def out(j):
            h, b = steps[j][:2]
            act.wait_ge(A["o"], i * J + (j + 1 + npt))
            act.activation(mix[h * 64:(h + 1) * 64, ds(i, 1), b * P:(b + 1) * P],
                           slot(j % 4, 768, 896)[h * 64:(h + 1) * 64, :], ACT.Copy).then_inc(A["oev"], 1)

        for j in range(J + 3):
            if j < J:
                h, b, tiles, nl, _ = steps[j]
                n = len(tiles) * P
                c = j % 8
                act.wait_ge(A["neg"], i * J + (j + 1))
                act.wait_ge(A["t"], i * J + (j + 1))
                if l == 0:
                    a = 0 if b < 4 else 512
                    act.activation(p[j % 2][:, 0:n], slot(j % 4, a, a + n), ACT.Exp, bias=nneg[:, c:c + 1],
                                   scale=rq[:, h * 6 + b:h * 6 + b + 1], accum_out=rsum[:, c:c + 1]
                                   ).then_inc(A["exp"], 1)
                else:
                    act.activation(p[j % 2][:, 0:n], p[j % 2][:, 0:n], ACT.Exp, bias=nneg[:, c:c + 1],
                                   accum_out=rsum[:, c:c + 1]).then_inc(A["exp"], 1)
            if j >= 3:
                out(j - 3)
            if 1 <= j <= J:
                n = len(steps[j - 1][2]) * P
                act.wait_ge(A["t"], i * J + (j + 2))
                act.wait_ge(A["o"], i * J + j)
                act.activation(pt[(j - 1) % npt][0][:, 0:n], slot((j - 1) % 4, 0, n), ACT.Copy
                               ).then_inc(A["hi"], 1)

    def att_dve(dve, l, i):
        A = a_sem[l]
        q, k, v, p, pt, mix = operands(l)
        steps = steps_of(l)
        J = len(steps)
        npt = NPT[l]
        for j in range(J + 1):
            if j < J:
                h, b, tiles, nl, bt = steps[j]
                n = len(tiles) * P
                c = j % 8
                dve.wait_ge(A["s"], i * J + (j + 1))
                if l == 0:
                    a = 0 if b < 4 else 512
                    dve.reduce_max(nmax[:, c:c + 1], slot(j % 4, a, a + n), AX).then_inc(A["max"], 1)
                    dve.wait_ge(A["max"], i * J + (j + 1))
                    dve.tensor_scalar(nneg[:, c:c + 1], nmax[:, c:c + 1], rq[:, h * 6 + b:h * 6 + b + 1], -1.0,
                                      ALU.mult, ALU.mult).then_inc(A["neg"], 1)
                else:
                    if j == 0:
                        dve.wait_ge(A["bias"], i * 16 + 16)
                    dve.wait_ge(A["t"], i * J + (j + 1))
                    r = rq[:, b * 2 + h:b * 2 + h + 1]
                    dve.scalar_tensor_tensor(out=p[j % 2][:, 0:nl], in0=slot(j % 4, 0, nl), scalar=r,
                                             in1=biasb[:, h, bt * P:bt * P + nl], op0=ALU.mult, op1=ALU.add
                                             ).then_inc(A["sadd"], 1)
                    dve.tensor_scalar(p[j % 2][:, nl:n], slot(j % 4, 512, T), r, None, ALU.mult
                                      ).then_inc(A["sadd"], 1)
                    dve.wait_ge(A["sadd"], i * (2 * J) + (2 * j + 2))
                    dve.reduce_max(nmax[:, c:c + 1], p[j % 2][:, 0:n], AX).then_inc(A["max"], 1)
                    dve.wait_ge(A["max"], i * J + (j + 1))
                    dve.tensor_scalar(nneg[:, c:c + 1], nmax[:, c:c + 1], -1.0, None, ALU.mult
                                      ).then_inc(A["neg"], 1)
                dve.wait_ge(A["exp"], i * J + (j + 1))
                dve.reciprocal(rinv[:, c:c + 1], rsum[:, c:c + 1]).then_inc(A["inv"], 1)
            if j:
                n = len(steps[j - 1][2]) * P
                dve.wait_ge(A["hi"], i * J + j)
                dve.tensor_tensor(pt[(j - 1) % npt][1][:, 0:n], slot((j - 1) % 4, 0, n),
                                  pt[(j - 1) % npt][0][:, 0:n].bitcast(F32), ALU.subtract
                                  ).then_inc(A["lo"], 1)

    def att_pool(pool, l, i):
        A = a_sem[l]
        p = operands(l)[3]
        steps = steps_of(l)
        J = len(steps)
        for j in range(J):
            n = len(steps[j][2]) * P
            pool.wait_ge(A["inv"], i * J + (j + 1))
            pool.tensor_tensor(p[j % 2][:, 0:n], p[j % 2][:, 0:n],
                               rinv[:, j % 8:j % 8 + 1].broadcast_to([P, n]), ALU.mult).then_inc(A["p"], 1)

    def pairs(eng, l, body):
        name, n = ("pr0", PAIRS0) if l == 0 else ("pr1", PAIRS1)
        with eng.Fori(0, n // 2) as ii:
            for u in range(2):
                body(ii * 2 + u, u, ii + AT[name].f[u])

    def items(eng, body):
        eng.wait_ge(e_sem["tab"], 1)
        with eng.Fori(0, ITEMS) as it:
            live = eng.value_load(tabi[0:1, 0, ds(it, 1)], min_val=0, max_val=1)
            wide = eng.value_load(tabi[0:1, 2, ds(it, 1)], min_val=0, max_val=1)
            with eng.If(live > 0):
                with eng.If(wide > 0):
                    body(it, BLK)
                with eng.Else():
                    body(it, P)
                eng.nop()
            eng.nop()

    def norm_act_first(act, nb):
        for k in range(KC):
            if k >= 2:
                act.wait_ge(nr[1], nb * 8 + (k - 1))
            act.activation(fn_sq[k % 2][:, :], res_lat(k), ACT.Square).then_inc(nr[0], 1)
        act.wait_ge(nr[1], nb * 8 + 8)
        act.activation(fn_rs[:, :], slot(3, 0, SEQ), ACT.Sqrt, bias=eps[:, 0:1], scale=1.0 / D).then_inc(nr[2], 1)

    def turned_hi(act, k):
        act.wait_ge(e_sem["xt"], k + 1)
        act.activation(xt[0][:, :, k * P:(k + 1) * P], bank(k % 4, 0, 512).rearrange("p (b c) -> p b c", b=4),
                       ACT.Copy).then_inc(e_sem["xthi"], 1)

    def y_part(J, part):
        if J == 2:
            return slot(part), part, 0, D
        return bank(part, 0, 512), 0, part * 512, part * 512 + 512

    UNITS = [[512, 256, 128], [U, U, U]]

    @block.tensor
    def _(pe):
        pe.sem_inc(m_used, 3)
        for r in range(3):
            pe.sem_inc(used[r], USED0)
        for l in range(2):
            pe.sem_inc(a_sem[l]["t"], 2)
            pe.sem_inc(a_sem[l]["o"], NPT[l])
        pe.sem_inc(e_sem["ws"], 1)

        def mods_pe(l):
            def subs(j, which):
                pe.wait_ge(m_evac, j + (6 * l + 1))
                for s in which:
                    pe.wait_ge(m_full[s], j * 16 + (1 + (6 if s == 0 else 5) * l) * 16)
                    for r in range(3):
                        for k in range(KC):
                            ins = pe.matmul(bank(7, (s * 3 + r) * 2, 2), raw[s][:, r, k * P:(k + 1) * P],
                                            scond[:, k, :], start=k == 0, stop=k == KC - 1)
                    ins.then_inc(m_used, 1)
            with pe.Fori(0, 5) as j:
                subs(j, range(3))
            subs(5, range(1))

        def linear(nm, subs, x, n, before):
            for m in range(subs):
                r, t = m % 3, m // 3
                pe.wait_ge(lin_evac, before + m + 1)
                pe.wait_ge(lo_ready[r], LO0 + AT[nm].u[r] + t + 1)
                for k in range(KC):
                    for a, b in pieces(n):
                        ins = mm3(pe, slot(m % 4, a, b), [w[r][:, k * P:(k + 1) * P] for w in (whi, wlo)],
                                  [h[:, k, a:b] for h in x], k == 0, k == KC - 1)
                ins.then_inc(used[r], 1)

        pe.wait_ge(s_const, 16 * len(CONSTS))
        pe.wait_ge(s_scond, 1)
        mods_pe(0)
        phase_end(pe, "mods0")
        norm_pe(pe, 0, T, sqb)
        phase_end(pe, "norm0")
        linear("ain", 6, xn, T, 0)
        phase_end(pe, "ain")
        SQ, SUM = c_sem[0], c_sem[1]
        pe.wait_ge(SQ, 2)
        for kc in range(2):
            for a, b in pieces(T):
                ins = pe.matmul(slot(0, a, b), ones[:, :], l0_sq[:, kc, a:b], start=kc == 0, stop=kc == 1)
        ins.then_inc(SUM, 1)
        pe.wait_ge(SQ, 3)
        for a, b in pieces(T):
            ins = pe.matmul(slot(1, a, b), ones[:, :], l0_x[:, 0, a:b], start=True, stop=True)
        ins.then_inc(SUM, 1)
        phase_end(pe, "lat")
        fa, fahi, falo, fev, fhi, flo = f_sem
        u4 = AT["four"].u
        pe.wait_ge(flo, 2)
        pe.wait_ge(lo_ready[0], LO0 + u4[0] + 1)
        for tb in range(6):
            if tb >= 4:
                pe.wait_ge(falo, tb - 3)
            for ch in range(2):
                ins = mm3(pe, slot(tb % 4, ch * 256, ch * 256 + 256), [t[:, ch, tb * P:(tb + 1) * P] for t in ff_hl],
                          [w[0][:, 0:256] for w in (whi, wlo)], True, True)
            ins.then_inc(fa, 1)
        pe.drain().then_inc(used[0], 1)
        pe.wait_ge(falo, 6)
        for u in range(4):
            r, t = (u + 1) % 3, (u + 1) // 3
            pe.wait_ge(lo_ready[r], LO0 + u4[r] + t + 1)
            for ch in range(2):
                for kb in range(2):
                    o = ch * 256 + (u // 2) * 128
                    ins = mm3(pe, slot(ch, 0, 512), [x[:, (u % 2) * 2 + kb, o:o + 128] for x in four_a],
                              [w[r][:, kb * 512:(kb + 1) * 512] for w in (whi, wlo)],
                              u == 0 and kb == 0, u == 3 and kb == 1)
            ins.then_inc(used[r], 1)
        pe.wait_ge(lo_ready[2], LO0 + u4[2] + 2)
        for ch in range(2):
            for u in range(2):
                for kb in range(2):
                    o = ch * 256 + u * 128
                    ins = mm3(pe, slot(ch, 512, 768), [x[:, 4 + kb, o:o + 128] for x in four_a],
                              [w[2][:, (u * 2 + kb) * 256:(u * 2 + kb + 1) * 256] for w in (whi, wlo)],
                              u == 0 and kb == 0, u == 1 and kb == 1)
        ins.then_inc(used[2], 1)
        phase_end(pe, "four")

        def pair0(i, s, fills):
            A, u = a_sem[0], AT["pr0"].u
            pe.wait_ge(A["oev"], i * 12 + 4)
            pe.wait_ge(lo_ready[0], i + (u[0] + LO0 + 1))
            for h in range(2):
                for a, b in pieces(T):
                    for kc in range(2):
                        o = (h * 2 + kc) * P
                        ins = mm3(pe, slot(h, a, b), [w[0][:, o:o + P] for w in (whi, wlo)],
                                  [x[:, kc, a:b] for x in cq], kc == 0, kc == 1)
            ins.then_inc(used[0], 1)
            pe.wait_ge(lo_ready[1], i + (u[1] + LO0 + 1))
            for h in range(2):
                for a, b in pieces(T):
                    ins = mm3(pe, slot(2 + h, a, b), [w[1][:, h * P:(h + 1) * P] for w in (whi, wlo)],
                              [x[:, a:b] for x in ckv], True, True)
            ins.then_inc(used[1], 1)
            for h in range(2):
                pe.wait_ge(A["qx"], i * 2 + (h + 1))
                pe.wait_ge(A["qsq"], i * 2 + (h + 1))
                pe.wait_ge(A["ksq"], i * 2 + (h + 1))
                for a, b in pieces(T):
                    ins = pe.matmul(slot(h, a, b), ones96[:, :], sqk0[:, a:b], start=True, stop=True)
                ins.then_inc(A["ks"], 1)
            pe.wait_ge(A["kx"], i * 2 + 1)
            for h in range(2):
                for b in range(6):
                    ins = pe.matmul(slot(2, 1000 + h * 6 + b, 1001 + h * 6 + b), sqq0[:, h, b * P:(b + 1) * P],
                                    ones96[:, 0:1], start=True, stop=True)
            ins.then_inc(A["rq"], 1)
            pe.wait_ge(lo_ready[2], i + (u[2] + LO0 + 1))
            pe.wait_ge(A["kx"], i * 2 + 2)
            for tb in range(6):
                ins = mm3(pe, slot(3, tb * P, (tb + 1) * P), [x[:, tb * P:(tb + 1) * P] for x in ckv],
                          [w[2][:, 0:P] for w in (whi, wlo)], True, True)
            ins.then_inc(used[2], 1)
            pe.wait_ge(A["klo"], i * 2 + 2)
            pe.wait_ge(A["qlo"], i * 2 + 2)
            pe.wait_ge(A["vlo"], i + 1)
            pe.wait_ge(A["rqd"], i + 1)
            att_pe(pe, 0, i)

        pairs(pe, 0, pair0)
        phase_end(pe, "att0")
        phase_end(pe, "split0")
        linear("out0", 8, mix0_hl, T, 6)
        phase_end(pe, "out0")

        with pe.Fori(0, 3) as t:
            norm_pe(pe, t + NORM_AT["n1"], BLK, fn_sq)
            pe.wait_ge(nr[7], t * 8 + (NORM_AT["n1"] + 1) * 8)
            ffn_pe(pe, "mlp", t * 22, AT["mlp"].u, BLK, "channels", True, False,
                   lambda: pe.wait_ge(y_evac, t + 1))
            ffn_pe(pe, "mlp", t * 22 + 11, AT["mlp"].u, BLK, "channels", False, True, lambda: None)
        phase_end(pe, "mlp")
        mods_pe(1)
        phase_end(pe, "mods1")
        norm_pe(pe, NORM_AT["n2"], T, sqb)
        phase_end(pe, "norm1")

        def pair1(i, s, fills):
            A, u = a_sem[1], AT["pr1"].u
            pe.wait_ge(A["oev"], i * 8 + 4)
            pe.wait_ge(lo_ready[0], i + (u[0] + LO0 + 1))
            for k in range(KC):
                ins = mm3(pe, slot(0, 0, SEQ), [w[0][:, k * P:(k + 1) * P] for w in (whi, wlo)],
                          [x[:, k, 0:SEQ] for x in xn], k == 0, k == KC - 1)
            ins.then_inc(used[0], 1)
            pe.wait_ge(lo_ready[1], i + (u[1] + LO0 + 1))
            for k in range(KC):
                for a, b in pieces(T):
                    ins = mm3(pe, slot(1, a, b), [w[1][:, k * P:(k + 1) * P] for w in (whi, wlo)],
                              [x[:, k, a:b] for x in xn], k == 0, k == KC - 1)
            ins.then_inc(used[1], 1)
            pe.wait_ge(A["qsq"], i + 1)
            for b in range(4):
                ins = pe.matmul(slot(2, 1000 + b * 2, 1002 + b * 2), sq1[:, b * P:(b + 1) * P], half2[:, :],
                                start=True, stop=True)
            ins.then_inc(A["rq"], 1)
            pe.wait_ge(A["ksq"], i + 1)
            pe.wait_ge(A["qx"], i + 1)
            for a, b in pieces(T):
                ins = pe.matmul(slot(0, a, b), ones64[:, :], sq1[:, a:b], start=True, stop=True)
            ins.then_inc(A["ks"], 1)
            pe.wait_ge(lo_ready[2], i + (u[2] + LO0 + 1))
            for tb in range(6):
                for k in range(KC):
                    ins = mm3(pe, slot(3, tb * P, (tb + 1) * P), [x[:, k, tb * P:(tb + 1) * P] for x in xn],
                              [w[2][:, k * P:(k + 1) * P] for w in (whi, wlo)], k == 0, k == KC - 1)
            ins.then_inc(used[2], 1)
            pe.wait_ge(A["klo"], i + 1)
            pe.wait_ge(A["qlo"], i + 1)
            pe.wait_ge(A["vlo"], i + 1)
            pe.wait_ge(A["rqd"], i + 1)
            att_pe(pe, 1, i)

        pe.wait_ge(s_zero, 1)
        pairs(pe, 1, pair1)
        phase_end(pe, "att1")
        phase_end(pe, "split1")
        linear("out1", 8, mix1_hl, SEQ, 14)
        phase_end(pe, "out1")

        E = e_sem
        norm_pe(pe, NORM_AT["n3"], SEQ, fn_sq)
        pe.wait_ge(E["in"], 16 * len(E_CONSTS))
        for k in range(KC):
            pe.wait_ge(nr[5], (NORM_AT["n3"]) * 8 + k + 1)
            if k >= 4:
                pe.wait_ge(E["xtlo"], k - 3)
            for b in range(4):
                ins = pe.transpose(bank(k % 4, b * P, P), xfm[k % 2][:, b * P:(b + 1) * P], ident[:, :])
            for b in range(4):
                ins = pe.matmul(bank(5, b * 8, 8), xfm[k % 2][:, b * P:(b + 1) * P], wr[:, k, :],
                                start=k == 0 and b == 0, stop=k == KC - 1, skip_group_check=True)
            ins.then_inc(E["xt"], 1)
        pe.wait_ge(E["sel"], 1)
        for b in range(4):
            for b2 in range(b + 1):
                ins = pe.matmul(bank(4, b * 8, 8), (tri if b2 == b else ones)[:, :], seltok[:, b2, :],
                                start=b2 == 0, stop=b2 == b)
        for b2 in range(4):
            ins = pe.matmul(bank(4, 32, 8), ones[:, :], seltok[:, b2, :], start=b2 == 0, stop=b2 == 3)
        ins.then_inc(E["pos"], 1)
        phase_end(pe, "router")

        def item(it, N):
            J = N // P
            pe.wait_ge(E["gm"], it + 1)
            for k in range(KC):
                pe.wait_ge(E["xlo"], it * 8 + (k + 1))
                for b in range(4):
                    for w in range(2):
                        ins = pe.matmul(bank(5 + k % 3, 0, N), xt[w][:, b, k * P:(k + 1) * P], gm[:, b, 0:N],
                                        start=b == 0 and w == 0, stop=b == 3 and w == 1)
                ins.then_inc(E["gmt"], 1)
            pe.wait_ge(E["xlo"], it * 8 + 11)
            for j in range(J):
                for b in range(4):
                    ins = pe.transpose(bank(4 + j, b * P, P), gm[:, b, j * P:(j + 1) * P].bitcast(F32), ident[:, :])
            ins.then_inc(E["sc"], 1)
            for j in range(J):
                for b in range(4):
                    ins = pe.matmul(bank(6, j, 1), gm[:, b, j * P:(j + 1) * P].bitcast(F32),
                                    cmbi[:, b, ds(it, 1)], start=b == 0, stop=b == 3)
            ins.then_inc(E["ws"], 1)
            pe.wait_ge(E["gt"], it + 1)
            pe.wait_ge(E["wsc"], it + 1)
            ffn_pe(pe, "exp", it * EX_CHUNKS, AT["exp"].u, N, "slots", True, True,
                   lambda: pe.wait_ge(E["scev"], it * 8 + 4))
            pe.wait_ge(E["ylo"], it * 2 + 2)
            for m in range(KC):
                pe.wait_ge(E["scev"], it * 8 + (m + 1))
                for j in range(J):
                    for w in range(2):
                        ins = pe.matmul(bank(m % 4, 0, 512), yhl[w][:, j, m * P:(m + 1) * P], gt[:, j, :],
                                        start=j == 0 and w == 0, stop=j == J - 1 and w == 1)
                ins.then_inc(E["sct"], 1)

        items(pe, item)
        phase_end(pe, "moe")

    @block.scalar
    def _(act):
        act.sem_inc(a_sem[0]["oev"], 4)
        act.sem_inc(a_sem[1]["oev"], 4)
        act.wait_ge(s_const, 16 * len(CONSTS))
        act.activation(scond[:, :, :], cond[:, :, :], ACT.Silu).then_inc(s_scond, 1)
        phase_end(act, "mods0")
        norm_act(act, 0, res_all, T, sqb, rstd, zb, xfb, cols_all(0), lambda k: xn[0][:, k, :])
        phase_end(act, "norm0")

        def linear_hi(nm, m):
            r, t = m % 3, m // 3
            hi_unit(act, r, raw[t][:, r, :], U, t, AT[nm].f[t] + 1, AT[nm].u[r] + t)

        for m in range(3):
            linear_hi("ain", m)
        for m in range(6):
            if m + 3 < 6:
                linear_hi("ain", m + 3)
            act.wait_ge(used[m % 3], USED0 + AT["ain"].u[m % 3] + m // 3 + 1)
            act.activation(plat[:, m, :], slot(m % 4, 0, T), ACT.Copy).then_inc(lin_evac, 1)
        phase_end(act, "ain")
        SQ, SUM, STD, X, HI, LO, KR = c_sem
        for kc in range(2):
            act.activation(l0_sq[:, kc, :], plat[:, kc, :], ACT.Square).then_inc(SQ, 1)
        act.activation(l0_x[:, 0, :], plat[:, 2, :], ACT.Square).then_inc(SQ, 1)
        act.activation(sqk0[64:128, :], plat[64:128, 3, :], ACT.Square)
        act.wait_ge(SUM, 1)
        act.activation(l0_rs[:, 0, :], slot(0, 0, T), ACT.Sqrt, bias=eps[:, 0:1], scale=1.0 / A_QR).then_inc(STD, 1)
        act.wait_ge(SUM, 2)
        act.activation(l0_rs[:, 1, :], slot(1, 0, T), ACT.Sqrt, bias=eps[:, 0:1], scale=1.0 / A_KVR).then_inc(STD, 1)
        for n, (dst, src) in enumerate(((cq[0][:, 0, :], l0_t[:, 0, :]), (cq[0][:, 1, :], l0_t[:, 1, :]),
                                        (ckv[0][:, :], l0_x[:, 1, :]))):
            act.wait_ge(X, n + 1)
            act.activation(dst, src, ACT.Copy).then_inc(HI, 1)
        phase_end(act, "lat")
        fa, fahi, falo, fev, fhi, flo = f_sem
        for ch in range(2):
            act.activation(ff_hl[0][:, ch, :], plat[:, 4 + ch, :], ACT.Copy).then_inc(fhi, 1)
        for m in range(3):
            linear_hi("four", m)
        for tb in range(6):
            act.wait_ge(fa, tb + 1)
            act.activation(four_a[0][:, tb, :], slot(tb % 4, 0, 512), ACT.Copy).then_inc(fahi, 1)
        for m in range(3, 6):
            linear_hi("four", m)
        act.wait_ge(used[2], USED0 + AT["four"].u[2] + 2)
        for ch in range(2):
            act.activation(mix0[:, 6 + ch, :], slot(ch, 0, T), ACT.Copy)
        phase_end(act, "four")

        def pair_hi(l, i, s, fills, r):
            n = UNITS[l][r]
            hi_unit(act, r, raw[s][:, r, 0:n], n, s, fills + 1, i + AT[("pr0", "pr1")[l]].u[r])

        def pair0(i, s, fills):
            A, u = a_sem[0], AT["pr0"].u
            for r in range(3):
                pair_hi(0, i, s, fills, r)
            act.wait_ge(used[0], i + (u[0] + USED0 + 1))
            for h in range(2):
                act.activation(sqq0[:, h, :], slot(h, 0, T), ACT.Square).then_inc(A["qsq"], 1)
            act.wait_ge(A["qx"], i * 2 + 1)
            act.activation(q0[0][:, 0, :], qx0[:, :], ACT.Copy).then_inc(A["qhi"], 1)
            act.wait_ge(A["qx"], i * 2 + 2)
            act.activation(q0[0][:, 1, :], qx0[:, :], ACT.Copy).then_inc(A["qhi"], 1)
            act.wait_ge(used[1], i + (u[1] + USED0 + 1))
            for h in range(2):
                if h:
                    act.wait_ge(A["ks"], i * 2 + 1)
                act.activation(sqk0[0:64, :], slot(2 + h, 0, T)[0:64, :], ACT.Square).then_inc(A["ksq"], 1)
                act.wait_ge(A["ks"], i * 2 + (h + 1))
                if h:
                    act.wait_ge(A["kx"], i * 2 + 1)
                act.activation(rk0[:, :], slot(h, 0, T), ACT.Sqrt, bias=eps[:, 0:1], scale=1.0 / A_QK
                               ).then_inc(A["kstd"], 1)
                act.wait_ge(A["kx"], i * 2 + (h + 1))
                act.activation(k0[0][:, h, :], kx0[:, :], ACT.Copy).then_inc(A["khi"], 1)
            act.wait_ge(A["rq"], i + 1)
            act.activation(rqs[:, 0:12], slot(2, 1000, 1012), ACT.Sqrt, bias=eps[:, 1:2]).then_inc(A["rqs"], 1)
            act.wait_ge(used[2], i + (u[2] + USED0 + 1))
            act.activation(v0[0][:, :, :], slot(3, 0, T), ACT.Copy).then_inc(A["vhi"], 1)
            att_act(act, 0, i)

        pairs(act, 0, pair0)
        phase_end(act, "att0")
        for k in range(KC):
            act.activation(mix0_hl[0][:, k, :], mix0[:, k, :], ACT.Copy).then_inc(mx_hi, 1)
        phase_end(act, "split0")
        for m in range(8):
            linear_hi("out0", m)
        phase_end(act, "out0")
        with act.Fori(0, 3) as t:
            act.wait_ge(used[1], t * 22 + (AT["mlp"].u[1] + USED0))
            norm_act(act, t + NORM_AT["n1"], res_block(t), BLK, fn_sq, fn_rs, fn_z, fn_x, cols_block(t),
                     lambda k: xg[0][:, k, :])
            ffn_act(act, "mlp", t * 22, t * 2, AT["mlp"], BLK)
            ffn_act(act, "mlp", t * 22 + 11, t * 2 + 1, AT["mlp"], BLK)
        phase_end(act, "mlp")
        phase_end(act, "mods1")
        norm_act(act, NORM_AT["n2"], res_all, T, sqb, rstd, zb, xfb, cols_all(1), lambda k: xn[0][:, k, :])
        phase_end(act, "norm1")

        def pair1(i, s, fills):
            A, u = a_sem[1], AT["pr1"].u
            for r in range(3):
                pair_hi(1, i, s, fills, r)
            act.wait_ge(used[0], i + (u[0] + USED0 + 1))
            act.activation(sq1[:, 0:SEQ], slot(0, 0, SEQ), ACT.Square).then_inc(A["qsq"], 1)
            act.wait_ge(A["qx"], i + 1)
            for h in range(2):
                rows = slice(h * 64, h * 64 + 64)
                ins = act.activation(q1[0][rows, h, :], qx1[rows, :], ACT.Copy)
            ins.then_inc(A["qhi"], 1)
            act.wait_ge(used[1], i + (u[1] + USED0 + 1))
            act.wait_ge(A["rq"], i + 1)
            act.activation(sq1[:, :], slot(1, 0, T), ACT.Square).then_inc(A["ksq"], 1)
            act.activation(rqs[:, 0:8], slot(2, 1000, 1008), ACT.Sqrt, bias=eps[:, 2:3]).then_inc(A["rqs"], 1)
            act.wait_ge(A["ks"], i + 1)
            act.activation(rk1[:, :], slot(0, 0, T), ACT.Sqrt, bias=eps[:, 0:1], scale=1.0 / DH
                           ).then_inc(A["kstd"], 1)
            act.wait_ge(A["kx"], i + 1)
            act.activation(k1[0][:, :], rk1[:, :], ACT.Copy).then_inc(A["khi"], 1)
            act.wait_ge(used[2], i + (u[2] + USED0 + 1))
            act.activation(v1[0][:, :, :], slot(3, 0, T), ACT.Copy).then_inc(A["vhi"], 1)
            att_act(act, 1, i)

        pairs(act, 1, pair1)
        phase_end(act, "att1")
        for k in range(KC):
            act.activation(mix1_hl[0][:, k, :], mix1[:, k, :], ACT.Copy).then_inc(mx_hi, 1)
        phase_end(act, "split1")
        for m in range(8):
            linear_hi("out1", m)
        phase_end(act, "out1")

        E = e_sem
        n3 = NORM_AT["n3"]
        norm_act_first(act, n3)
        for k in range(KC):
            act.wait_ge(nr[4], n3 * 8 + k + 1)
            if k >= 2:
                act.wait_ge(E["xt"], k - 1)
            a, b, scale, shift = cols_moe(k)[0]
            act.activation(xfm[k % 2][:, :], fn_z[k % 2][:, :], ACT.Identity, bias=shift, scale=scale
                           ).then_inc(nr[5], 1)
            if k >= 1:
                turned_hi(act, k - 1)
        turned_hi(act, KC - 1)
        act.wait_ge(E["exps"], 1)
        act.activation(wexp[:, :, :], wexp[:, :, :], ACT.Exp).then_inc(E["exps"], 1)
        phase_end(act, "router")

        def item(it, N):
            J = N // P
            for k in range(KC):
                act.wait_ge(E["gmt"], it * 8 + (k + 1))
                act.activation(xg[0][:, k, 0:N], bank(5 + k % 3, 0, N), ACT.Copy).then_inc(E["xhi"], 1)
            act.wait_ge(E["sc"], it + 1)
            for j in range(J):
                ins = act.activation(gt[:, j, :], bank(4 + j, 0, 512), ACT.Copy)
            ins.then_inc(E["gt"], 1)
            ffn_act(act, "exp", it * EX_CHUNKS, it, AT["exp"], N)
            act.wait_ge(used[2], it * EX_CHUNKS + (AT["exp"].u[2] + USED0 + EX_CHUNKS))
            for part in range(2):
                yb, j, a, b = y_part(J, part)
                act.activation(yx[part][:, a:b], yb, ACT.Copy, scale=wslot[:, j:j + 1]).then_inc(E["yx"], 1)
                act.wait_ge(E["yx"], it * 2 + (part + 1))
                act.activation(yhl[0][:, j, a:b], yx[part][:, a:b], ACT.Copy).then_inc(E["yhi"], 1)

        items(act, item)
        phase_end(act, "moe")

    @block.vector
    def _(dve):
        for r in range(3):
            dve.sem_inc(lo_ready[r], LO0)
        dve.sem_inc(m_evac, 1)
        for n in ("mlp", "exp"):
            dve.sem_inc(ff[n]["hm"], 2)
        dve.sem_inc(y_evac, 1)
        dve.sem_inc(e_sem["scev"], 4)
        dve.sem_inc(e_sem["xlo"], 3)
        dve.sem_inc(lin_evac, 4)
        chain = [0]

        def link(ins):
            chain[0] += 1
            ins.then_inc(s_chain, 1)
            dve.wait_ge(s_chain, chain[0])

        dve.wait_ge(s_const, 16 * len(CONSTS))

        def mods_dve(l):
            def out(j, n):
                dve.wait_ge(m_used, j * 3 + (N_MOD * l + 3 + n))
                dve.tensor_tensor(mods[:, l, ds(j * 9, 3 * n), :],
                                  bank(7, 0, 6 * n).rearrange("p (s c) -> p s c", c=2),
                                  bmod[:, l, ds(j * 9, 3 * n)].unsqueeze(2).broadcast_to([P, 3 * n, 2]),
                                  ALU.add).then_inc(m_evac, 1)
            with dve.Fori(0, 5) as j:
                out(j, 3)
            out(5, 1)
            dve.wait_ge(m_evac, 6 * l + 7)
            for n in range(2):
                sc = mods[:, l, (3 * n + 1) * KC:(3 * n + 2) * KC, :]
                link(dve.tensor_scalar(nsc[:, l, n, :, :], sc, 1.0, None, ALU.add))
                link(dve.tensor_tensor(nsc[:, l, n, :, :], nsc[:, l, n, :, :],
                                       ng[:, l, n, :].unsqueeze(2).broadcast_to([P, KC, 2]), ALU.mult))

        mods_dve(0)
        phase_end(dve, "mods0")
        norm_dve(dve, 0, res_all, T, rstd, zb, xfb, lambda k: xn[0][:, k, :], lambda k: xn[1][:, k, :])
        phase_end(dve, "norm0")

        def linear_lo(nm, m):
            r, t = m % 3, m // 3
            lo_unit(dve, r, raw[t][:, r, :], U, AT[nm].u[r] + t + 1)

        for m in range(6):
            linear_lo("ain", m)
        phase_end(dve, "ain")
        SQ, SUM, STD, X, HI, LO, KR = c_sem
        link(dve.scalar_tensor_tensor(out=l0_x[64:128, 2, :], in0=plat[64:128, 3, :], scalar=gcol[64:128, 5:6],
                                      in1=ktab[64:128, :], op0=ALU.mult, op1=ALU.mult))
        link(dve.scalar_tensor_tensor(out=krope[64:128, :], in0=plat[0:64, 3, :], scalar=gcol[0:64, 5:6],
                                      in1=ktab[0:64, :], op0=ALU.mult, op1=ALU.mult))
        link(dve.tensor_tensor(krope[64:128, :], krope[64:128, :], l0_x[64:128, 2, :], ALU.add))
        link(dve.tensor_scalar(csg[:, :], qtab[:, :], gcol[:, 3:4], None, ALU.mult))
        dve.wait_ge(STD, 1)
        link(dve.reciprocal(l0_rs[:, 0, :], l0_rs[:, 0, :]))
        dve.wait_ge(STD, 2)
        link(dve.reciprocal(l0_rs[:, 1, :], l0_rs[:, 1, :]))
        vals = ((plat[:, 0, :], 0, l0_rs[:, 0, :], l0_t[:, 0, :], cq[0][:, 0, :], cq[1][:, 0, :]),
                (plat[:, 1, :], 1, l0_rs[:, 0, :], l0_t[:, 1, :], cq[0][:, 1, :], cq[1][:, 1, :]),
                (plat[:, 2, :], 2, l0_rs[:, 1, :], l0_x[:, 1, :], ckv[0][:, :], ckv[1][:, :]))
        for src, g, rs, dst, hi, lo in vals:
            dve.scalar_tensor_tensor(out=dst, in0=src, scalar=gcol[:, g:g + 1], in1=rs, op0=ALU.mult,
                                     op1=ALU.mult).then_inc(X, 1)
        for n, (src, g, rs, dst, hi, lo) in enumerate(vals):
            dve.wait_ge(HI, n + 1)
            dve.tensor_tensor(lo, dst, hi.bitcast(F32), ALU.subtract).then_inc(LO, 1)
        phase_end(dve, "lat")
        fa, fahi, falo, fev, fhi, flo = f_sem
        for ch in range(2):
            dve.wait_ge(fhi, ch + 1)
            dve.tensor_tensor(ff_hl[1][:, ch, :], plat[:, 4 + ch, :], ff_hl[0][:, ch, :].bitcast(F32),
                              ALU.subtract).then_inc(flo, 1)
        for m in range(3):
            linear_lo("four", m)
        for tb in range(6):
            dve.wait_ge(fahi, tb + 1)
            dve.tensor_tensor(four_a[1][:, tb, :], slot(tb % 4, 0, 512), four_a[0][:, tb, :].bitcast(F32),
                              ALU.subtract).then_inc(falo, 1)
        for m in range(3, 6):
            linear_lo("four", m)
        phase_end(dve, "four")

        def pair_lo(l, i, s, r):
            n = UNITS[l][r]
            lo_unit(dve, r, raw[s][:, r, 0:n], n, i + (AT[("pr0", "pr1")[l]].u[r] + 1))

        def pair0(i, s, fills):
            A, u = a_sem[0], AT["pr0"].u
            for r in range(3):
                pair_lo(0, i, s, r)
            dve.wait_ge(A["o"], i * 12 + NPT[0])
            dve.wait_ge(used[0], i + (u[0] + USED0 + 1))
            for h in range(2):
                if h:
                    dve.wait_ge(A["qlo"], i * 2 + 1)
                dve.wait_ge(A["qsq"], i * 2 + (h + 1))
                dve.tensor_tensor(qx0[:, :], slot(h, 0, T), csg[:, :], ALU.mult).then_inc(A["qx"], 1)
                dve.wait_ge(A["qhi"], i * 2 + (h + 1))
                dve.tensor_tensor(q0[1][:, h, :], qx0[:, :], q0[0][:, h, :].bitcast(F32), ALU.subtract
                                  ).then_inc(A["qlo"], 1)
            for h in range(2):
                if h:
                    dve.wait_ge(A["klo"], i * 2 + 1)
                dve.wait_ge(A["kstd"], i * 2 + (h + 1))
                dve.reciprocal(rk0[:, :], rk0[:, :]).then_inc(A["rk"], 1)
                dve.wait_ge(A["rk"], i * 2 + (h + 1))
                dve.scalar_tensor_tensor(out=kx0[0:64, :], in0=slot(2 + h, 0, T)[0:64, :],
                                         scalar=gcol[0:64, 4:5], in1=rk0[0:64, :], op0=ALU.mult, op1=ALU.mult)
                dve.tensor_tensor(kx0[64:128, :], krope[64:128, :], rk0[64:128, :], ALU.mult
                                  ).then_inc(A["kx"], 1)
                dve.wait_ge(A["khi"], i * 2 + (h + 1))
                dve.tensor_tensor(k0[1][:, h, :], kx0[:, :], k0[0][:, h, :].bitcast(F32), ALU.subtract
                                  ).then_inc(A["klo"], 1)
            dve.wait_ge(A["rqs"], i + 1)
            dve.reciprocal(rq[:, 0:12], rqs[:, 0:12]).then_inc(A["rqd"], 1)
            dve.wait_ge(A["vhi"], i + 1)
            dve.tensor_tensor(v0[1][:, :, :], slot(3, 0, T), v0[0][:, :, :].bitcast(F32), ALU.subtract
                              ).then_inc(A["vlo"], 1)
            dve.wait_ge(A["rqd"], i + 1)
            att_dve(dve, 0, i)

        pairs(dve, 0, pair0)
        phase_end(dve, "att0")
        for k in range(KC):
            dve.wait_ge(mx_hi, k + 1)
            dve.tensor_tensor(mix0_hl[1][:, k, :], mix0[:, k, :], mix0_hl[0][:, k, :].bitcast(F32), ALU.subtract)
        phase_end(dve, "split0")

        def out_dve(nm, l, parts):
            for m in range(3):
                linear_lo(nm, m)
            for m in range(8):
                dve.wait_ge(used[m % 3], USED0 + AT[nm].u[m % 3] + m // 3 + 1)
                for n, (a, b, s) in enumerate(parts):
                    ins = dve.scalar_tensor_tensor(out=res[:, m, a:b], in0=slot(m % 4, a, b),
                                                   scalar=mods[:, l, 2 * KC + m, s:s + 1], in1=res[:, m, a:b],
                                                   op0=ALU.mult, op1=ALU.add)
                ins.then_inc(lin_evac, 1)
                if m + 3 < 8:
                    linear_lo(nm, m + 3)

        out_dve("out0", 0, [(0, SEQ, 0), (SEQ, T, 1)])
        for dst, src in ((nscr, nsc[:, 0, 1, :, :]), (nshr, mods[:, 0, 3 * KC:4 * KC, :]),
                         (ngtr, mods[:, 0, 5 * KC:6 * KC, :])):
            for t, s in enumerate((0, 0, 1)):
                dve.tensor_copy(dst[:, :, t], src[:, :, s])
        phase_end(dve, "out0")
        with dve.Fori(0, 3) as t:
            norm_dve(dve, t + NORM_AT["n1"], res_block(t), BLK, fn_rs, fn_z, fn_x,
                     lambda k: xg[0][:, k, :], lambda k: xg[1][:, k, :])
            ffn_dve(dve, "mlp", t * 22, AT["mlp"], BLK)
            ffn_dve(dve, "mlp", t * 22 + 11, AT["mlp"], BLK)
            dve.wait_ge(used[2], t * 22 + (AT["mlp"].u[2] + USED0 + 22))
            for m in range(KC):
                ins = dve.scalar_tensor_tensor(out=res[:, m, ds(t * BLK, BLK)], in0=bank(m // 2, (m % 2) * BLK, BLK),
                                               scalar=ngtr[:, m, ds(t, 1)], in1=res[:, m, ds(t * BLK, BLK)],
                                               op0=ALU.mult, op1=ALU.add)
            ins.then_inc(y_evac, 1)
        phase_end(dve, "mlp")
        mods_dve(1)
        phase_end(dve, "mods1")
        norm_dve(dve, NORM_AT["n2"], res_all, T, rstd, zb, xfb, lambda k: xn[0][:, k, :], lambda k: xn[1][:, k, :])
        phase_end(dve, "norm1")
        for t in q1:
            dve.tensor_copy(t[64:128, 0, :].rearrange("p (a b) -> p a b", b=64),
                            ones64[64:128, 0:64].unsqueeze(1).broadcast_to([64, 8, 64]))
            ins = dve.tensor_copy(t[0:64, 1, :].rearrange("p (a b) -> p a b", b=64),
                                  ones64[0:64, 64:128].unsqueeze(1).broadcast_to([64, 8, 64]))
        ins.then_inc(s_zero, 1)

        dve.wait_ge(s_zero, 1)

        def pair1(i, s, fills):
            A, u = a_sem[1], AT["pr1"].u
            for r in range(3):
                pair_lo(1, i, s, r)
            dve.wait_ge(A["o"], i * 8 + NPT[1])
            dve.wait_ge(used[0], i + (u[0] + USED0 + 1))
            dve.wait_ge(A["qsq"], i + 1)
            dve.tensor_scalar(qx1[:, :], slot(0, 0, SEQ), gcol[:, 6:7], None, ALU.mult).then_inc(A["qx"], 1)
            dve.wait_ge(A["qhi"], i + 1)
            for h in range(2):
                rows = slice(h * 64, h * 64 + 64)
                ins = dve.tensor_tensor(q1[1][rows, h, :], qx1[rows, :], q1[0][rows, h, :].bitcast(F32), ALU.subtract)
            ins.then_inc(A["qlo"], 1)
            dve.wait_ge(A["rqs"], i + 1)
            dve.reciprocal(rq[:, 0:8], rqs[:, 0:8]).then_inc(A["rqd"], 1)
            dve.wait_ge(A["kstd"], i + 1)
            dve.reciprocal(rk1[:, :], rk1[:, :]).then_inc(A["rk"], 1)
            dve.wait_ge(A["rk"], i + 1)
            dve.scalar_tensor_tensor(out=rk1[:, :], in0=slot(1, 0, T), scalar=gcol[:, 7:8], in1=rk1[:, :],
                                     op0=ALU.mult, op1=ALU.mult).then_inc(A["kx"], 1)
            dve.wait_ge(A["khi"], i + 1)
            dve.tensor_tensor(k1[1][:, :], rk1[:, :], k1[0][:, :].bitcast(F32), ALU.subtract).then_inc(A["klo"], 1)
            dve.wait_ge(A["vhi"], i + 1)
            dve.tensor_tensor(v1[1][:, :, :], slot(3, 0, T), v1[0][:, :, :].bitcast(F32), ALU.subtract
                              ).then_inc(A["vlo"], 1)
            dve.wait_ge(A["rqd"], i + 1)
            att_dve(dve, 1, i)

        pairs(dve, 1, pair1)
        phase_end(dve, "att1")
        for k in range(KC):
            dve.wait_ge(mx_hi, KC + k + 1)
            dve.tensor_tensor(mix1_hl[1][:, k, :], mix1[:, k, :], mix1_hl[0][:, k, :].bitcast(F32), ALU.subtract)
        phase_end(dve, "split1")
        out_dve("out1", 1, [(0, SEQ, 0)])
        phase_end(dve, "out1")

        E = e_sem
        n3 = NORM_AT["n3"]
        dve.wait_ge(nr[2], n3 + 1)
        link(dve.reciprocal(fn_rs[:, :], fn_rs[:, :]))

        def turned_lo(k):
            dve.wait_ge(E["xthi"], k + 1)
            dve.tensor_tensor(xt[1][:, :, k * P:(k + 1) * P], bank(k % 4, 0, 512).rearrange("p (b c) -> p b c", b=4),
                              xt[0][:, :, k * P:(k + 1) * P].bitcast(F32), ALU.subtract).then_inc(E["xtlo"], 1)

        for k in range(KC):
            if k >= 2:
                dve.wait_ge(nr[5], n3 * 8 + k - 1)
            dve.tensor_tensor(fn_z[k % 2][:, :], res_lat(k), fn_rs[:, :], ALU.mult).then_inc(nr[4], 1)
            if k >= 2:
                turned_lo(k - 2)
        turned_lo(KC - 2)
        turned_lo(KC - 1)

        dve.wait_ge(E["xt"], KC)
        dve.wait_ge(E["in"], 16 * len(E_CONSTS))
        link(dve.tensor_copy(lg[:, :, :], bank(5, 0, 32).rearrange("p (b e) -> p b e", b=4)))
        for b in range(4):
            mine = lg[:, b, :].unsqueeze(2).broadcast_to([P, 8, 8])
            other = lg[:, b, :].unsqueeze(1).broadcast_to([P, 8, 8])
            link(dve.tensor_tensor(r64[:, b, :, :], other, mine, ALU.is_gt))
            link(dve.tensor_tensor(r64b[:, b, :, :], other, mine, ALU.is_equal))
            link(dve.tensor_tensor(r64b[:, b, :, :], r64b[:, b, :, :], ltj[:, :, :], ALU.mult))
        link(dve.tensor_tensor(r64[:, :, :, :], r64[:, :, :, :], r64b[:, :, :, :], ALU.add))
        link(dve.reduce_sum(rank[:, :, :], r64[:, :, :, :], AX))
        dve.tensor_scalar(seltok[:, :, :], rank[:, :, :], 2.0, None, ALU.is_lt).then_inc(E["sel"], 1)
        link(dve.reduce_max(lmax[:, :], lg[:, :, :], AX))
        dve.tensor_tensor(wexp[:, :, :], lg[:, :, :], lmax[:, :].unsqueeze(2).broadcast_to([P, 4, 8]),
                          ALU.subtract).then_inc(E["exps"], 1)
        dve.wait_ge(E["exps"], 2)
        dve.wait_ge(E["sel"], 1)
        link(dve.tensor_tensor(wexp[:, :, :], wexp[:, :, :], seltok[:, :, :], ALU.mult))
        link(dve.reduce_sum(wsum[:, :], wexp[:, :, :], AX))
        link(dve.reciprocal(wsum[:, :], wsum[:, :]))
        link(dve.tensor_tensor(comb[:, :, :], wexp[:, :, :], wsum[:, :].unsqueeze(2).broadcast_to([P, 4, 8]), ALU.mult))
        dve.wait_ge(E["pos"], 1)
        link(dve.tensor_scalar(posn[:, :, :], bank(4, 0, 32).rearrange("p (b e) -> p b e", b=4), 1.0, None, ALU.add))
        link(dve.tensor_tensor(posn[:, :, :], posn[:, :, :], seltok[:, :, :], ALU.mult))
        link(dve.tensor_copy(cnts[:, :], bank(4, 32, 8)))
        link(dve.tensor_scalar(nit[:, :], cnts[:, :], 0.0, None, ALU.is_gt))
        link(dve.tensor_scalar(endi[:, :], cnts[:, :], float(BLK), None, ALU.is_gt))
        link(dve.tensor_tensor(nit[:, :], nit[:, :], endi[:, :], ALU.add))
        link(dve.tensor_tensor(r64[:, 0, :, :], nit[:, :].unsqueeze(1).broadcast_to([P, 8, 8]), ltj[:, :, :], ALU.mult))
        link(dve.reduce_sum(starti[:, :], r64[:, 0, :, :], AX))
        link(dve.tensor_tensor(endi[:, :], starti[:, :], nit[:, :], ALU.add))
        inum = itn[:, :].unsqueeze(2).broadcast_to([P, ITEMS, 8])
        link(dve.tensor_tensor(oneh[:, :, :], inum, starti[:, :].unsqueeze(1).broadcast_to([P, ITEMS, 8]), ALU.is_ge))
        link(dve.tensor_tensor(oneb[:, :, :], inum, endi[:, :].unsqueeze(1).broadcast_to([P, ITEMS, 8]), ALU.is_lt))
        link(dve.tensor_tensor(oneh[:, :, :], oneh[:, :, :], oneb[:, :, :], ALU.mult))

        def of_item(dst, vec):
            link(dve.tensor_tensor(oneb[:, :, :], oneh[:, :, :], vec[:, :].unsqueeze(1).broadcast_to([P, ITEMS, 8]),
                                   ALU.mult))
            link(dve.reduce_sum(dst, oneb[:, :, :], AX))

        link(dve.reduce_sum(tab[:, 0, :], oneh[:, :, :], AX))
        of_item(tab[:, 1, :], erow)
        of_item(tab[:, 3, :], starti)
        of_item(tab[:, 4, :], cnts)
        link(dve.tensor_tensor(tab[:, 5, :], itn[:, :], tab[:, 3, :], ALU.subtract))
        link(dve.tensor_scalar(tab[:, 5, :], tab[:, 5, :], float(BLK), None, ALU.mult))
        link(dve.tensor_tensor(tab[:, 4, :], tab[:, 4, :], tab[:, 5, :], ALU.subtract))
        link(dve.tensor_scalar(tab[:, 2, :], tab[:, 4, :], float(P), None, ALU.is_gt))
        link(dve.tensor_copy(tabi[:, :, :], tab[:, :, :]))
        for b in range(4):
            link(dve.tensor_tensor(oneb[:, :, :], oneh[:, :, :],
                                   posn[:, b, :].unsqueeze(1).broadcast_to([P, ITEMS, 8]), ALU.mult))
            link(dve.reduce_sum(posi[:, b, :], oneb[:, :, :], AX))
            link(dve.tensor_tensor(oneb[:, :, :], oneh[:, :, :],
                                   comb[:, b, :].unsqueeze(1).broadcast_to([P, ITEMS, 8]), ALU.mult))
            link(dve.reduce_sum(cmbi[:, b, :], oneb[:, :, :], AX))
            link(dve.tensor_tensor(posi[:, b, :], posi[:, b, :], tab[:, 5, :], ALU.subtract))
            link(dve.tensor_scalar(posi[:, b, :], posi[:, b, :], -1.0, None, ALU.add))
        dve.tensor_copy(cmbi[:, 0, 0:1], cmbi[:, 0, 0:1]).then_inc(E["tab"], 1)
        phase_end(dve, "router")

        def item(it, N):
            J = N // P
            dve.wait_ge(E["ws"], it + 1)
            for b in range(4):
                ins = dve.tensor_scalar(gm[:, b, 0:N], iot[:, 0:N], posi[:, b, ds(it, 1)], None, ALU.is_equal)
            ins.then_inc(E["gm"], 1)
            for k in range(KC):
                dve.wait_ge(E["xhi"], it * 8 + (k + 1))
                dve.tensor_tensor(xg[1][:, k, 0:N], bank(5 + k % 3, 0, N), xg[0][:, k, 0:N].bitcast(F32),
                                  ALU.subtract).then_inc(E["xlo"], 1)
            dve.wait_ge(E["ws"], it + 2)
            dve.tensor_copy(wslot[:, 0:J], bank(6, 0, J)).then_inc(E["wsc"], 1)
            ffn_dve(dve, "exp", it * EX_CHUNKS, AT["exp"], N)
            for part in range(2):
                yb, j, a, b = y_part(J, part)
                dve.wait_ge(E["yhi"], it * 2 + (part + 1))
                dve.tensor_tensor(yhl[1][:, j, a:b], yx[part][:, a:b], yhl[0][:, j, a:b].bitcast(F32), ALU.subtract
                                  ).then_inc(E["ylo"], 1)
            for m in range(KC):
                dve.wait_ge(E["sct"], it * 8 + (m + 1))
                dve.scalar_tensor_tensor(out=res[:, m, 0:SEQ], in0=bank(m % 4, 0, 512),
                                         scalar=mods[:, 1, 5 * KC + m, 0:1], in1=res[:, m, 0:SEQ],
                                         op0=ALU.mult, op1=ALU.add).then_inc(E["scev"], 1)

        items(dve, item)
        phase_end(dve, "moe")

    @block.gpsimd
    def _(pool):
        for name in ("mods0", "norm0", "ain", "lat", "four"):
            phase_end(pool, name)
        pairs(pool, 0, lambda i, s, fills: att_pool(pool, 0, i))
        for name in ("att0", "split0", "out0", "mlp", "mods1", "norm1"):
            phase_end(pool, name)
        pairs(pool, 1, lambda i, s, fills: att_pool(pool, 1, i))
        for name in ("att1", "split1", "out1", "router", "moe"):
            phase_end(pool, name)


def _unit(w, m):
    k = w.shape[0] // P
    return w[:, m * P:(m + 1) * P].reshape(k, P, P).transpose(1, 0, 2).reshape(P, k * P)


def _swap(n):
    return np.arange(n) ^ 1


def layout(x, c, ctx, c_ctx, w_mod, b_mod, norm_g, a_w_in, a_g_cq, a_g_ckv, a_w_uq, a_w_ukv, a_g_q, a_g_k,
           a_w_out, f_w_gate, f_w_up, f_w_down, c_w_in, c_g_q, c_g_k, c_rpb, c_w_out, m_w_router, m_w_gate,
           m_w_up, m_w_down):
    f = np.float32
    order = np.arange(SEQ).reshape(ROWS, GRID_W).T.reshape(-1)
    a = {}
    tok = np.concatenate([x[0][order], ctx[0]], axis=0)
    a["xT"] = tok.T.reshape(KC, P, T).transpose(1, 0, 2)
    a["cond"] = np.stack([c[0], c_ctx], axis=-1).reshape(KC, P, 2).transpose(1, 0, 2)
    a["bmod"] = b_mod.reshape(2, 48, P).transpose(2, 0, 1)
    a["ng"] = norm_g.reshape(2, 2, KC, P).transpose(3, 0, 1, 2)
    g = np.ones((P, 8), f)
    sw = _swap(A_ROPE)
    g[:, 0:2] = a_g_cq[0].reshape(2, P).T
    g[:, 2] = a_g_ckv[0]
    g[0:96, 3] = a_g_q[0]
    g[96:128, 3] = a_g_q[0][64:][sw]
    g[0:64, 4] = a_g_k[0][0:64]
    rope = a_g_k[0][64:]
    g[:, 5] = np.concatenate([rope[sw], rope[sw], rope, rope])
    g[:, 6] = np.tile(c_g_q[0], 2)
    g[:, 7] = np.tile(c_g_k[0], 2)
    a["gcol"] = g
    a["ident"] = np.eye(P, dtype=f)
    a["ones"] = np.ones((P, P), f)
    o96 = np.zeros((P, P), f)
    o96[0:96] = 1
    a["ones96"] = o96
    o64 = np.zeros((P, P), f)
    o64[0:64, 0:64] = 1
    o64[64:, 64:] = 1
    a["ones64"] = o64
    h2 = np.zeros((P, 2), f)
    h2[0:64, 0] = 1
    h2[64:, 1] = 1
    a["half2"] = h2
    a["eps"] = np.tile(np.array([EPS, A_QK * EPS, DH * EPS], f), (P, 1))
    inv = 10000.0 ** (-np.arange(8, dtype=np.float64) / 8)
    ang = np.concatenate([(order // GRID_W)[:, None] * inv, (order % GRID_W)[:, None] * inv], axis=1)
    cos = np.ones((A_ROPE, T))
    sin = np.zeros((A_ROPE, T))
    cos[:, 0:SEQ] = np.repeat(np.cos(ang).T, 2, axis=0)
    sin[:, 0:SEQ] = np.repeat(np.sin(ang).T, 2, axis=0) * np.tile([-1.0, 1.0], 16)[:, None]
    a["qtab"] = np.concatenate([np.ones((64, T)), cos, sin]).astype(f)
    a["ktab"] = np.concatenate([sin, sin, cos, cos]).astype(f)
    rows = []

    def triple(*units):
        t = np.zeros((P, 3, U), f)
        for n, u in enumerate(units):
            t[:, n, 0:u.shape[1]] = u
        rows.append(t.reshape(P, 3 * U))

    def triples(units):
        for n in range(0, len(units), 3):
            triple(*units[n:n + 3])

    triples([_unit(w_mod[0], m) for m in range(48)])
    w = a_w_in[0]
    kr = w[:, 384:416]
    w_in = np.concatenate([w[:, 0:384], kr[:, sw], kr[:, sw], kr, kr, w[:, 416:672]], axis=1)
    triples([_unit(w_in, m) for m in range(6)])
    uq = a_w_uq[0].reshape(A_QR, A_HEADS, A_QK)
    uq = np.concatenate([uq, uq[:, :, 64:][:, :, sw]], axis=2)
    ukv = a_w_ukv[0].reshape(A_KVR, A_HEADS, 128)
    for i in range(PAIRS0):
        q = np.concatenate([uq[kc * P:(kc + 1) * P, 2 * i + h] for h in range(2) for kc in range(2)], axis=1)
        ka, kb = ukv[:, 2 * i, 0:64], ukv[:, 2 * i + 1, 0:64]
        v = np.concatenate([ukv[:, 2 * i, 64:], ukv[:, 2 * i + 1, 64:]], axis=1)
        triple(q, np.concatenate([ka, kb, kb, ka], axis=1), v)
    triples([_unit(a_w_out[0], m) for m in range(8)])
    for cch in range(FF_CHUNKS):
        triple(_unit(f_w_gate[0], cch), _unit(f_w_up[0], cch), f_w_down[0][cch * P:(cch + 1) * P])
    triples([_unit(w_mod[1], m) for m in range(48)])
    for i in range(PAIRS1):
        triple(*[_unit(c_w_in[0][:, s * D:(s + 1) * D], i) for s in range(3)])
    triples([_unit(c_w_out[0], m) for m in range(8)])
    for e in range(EXPERTS):
        for cch in range(EX_CHUNKS):
            triple(_unit(m_w_gate[0, e], cch), _unit(m_w_up[0, e], cch), m_w_down[0, e][cch * P:(cch + 1) * P])
    a["stream"] = np.stack(rows)
    assert a["stream"].shape[0] == TR_END
    units = []
    ch = 2 * np.pi * np.outer(np.arange(64), np.arange(64)) / 64
    z = np.zeros((64, 64))
    units.append(np.concatenate([np.block([[fn(ch), z], [z, fn(ch)]]) for fn in (np.cos, np.sin)], axis=1))
    th = 2 * np.pi * ((order[:, None] * order[None, :]) % SEQ) / SEQ
    for fn, sign in ((np.cos, 1), (np.sin, -1)):
        m = sign * fn(th) / np.sqrt(SEQ * 64)
        for u in range(2):
            units.append(np.concatenate([m[(2 * u + kb) * P:(2 * u + kb + 1) * P] for kb in range(2)], axis=1))
    tc = np.arange(CTX)
    th = 2 * np.pi * ((tc[:, None] * tc[None, :]) % CTX) / CTX
    units.append(np.concatenate([s * fn(th)[kb * P:(kb + 1) * P] / np.sqrt(CTX * 64)
                                 for fn, s in ((np.cos, 1), (np.sin, -1)) for kb in range(2)], axis=1))
    fo = np.zeros((2, P, 3, U), f)
    for n, u in enumerate(units):
        fo[n // 3, :, n % 3, 0:u.shape[1]] = u
    a["fourier"] = fo.reshape(2, P, 3 * U)
    qi = np.arange(P)
    tiles = []
    for b, kbs in ((0, (0, 1)), (1, (0, 1, 2)), (3, (2, 3))):
        cq_, rq_ = b * 16 + qi // 8, qi % 8
        start = np.clip(cq_ - WIN_C // 2, 0, GRID_W - WIN_C)
        for kb in kbs:
            ck, rk = kb * 16 + qi // 8, qi % 8
            inside = (ck[None, :] >= start[:, None]) & (ck[None, :] < start[:, None] + WIN_C)
            dr = rk[None, :] - rq_[:, None] + WIN_R - 1
            dc = np.clip(ck[None, :] - cq_[:, None] + WIN_C - 1, 0, 2 * WIN_C - 2)
            t = c_rpb[0][:, dr, dc]
            tiles.append(np.where(inside[None], t, f(-BIG)))
    bias = np.concatenate(tiles, axis=2)
    a["bias"] = bias.reshape(PAIRS1, 2, P, BIAS_TILES * P).transpose(0, 2, 1, 3)
    a["wr"] = m_w_router[0].reshape(KC, P, 8).transpose(1, 0, 2)
    a["tri"] = np.triu(np.ones((P, P), f), 1)
    a["iot"] = np.tile(np.arange(BLK, dtype=f), (P, 1))
    a["ltj"] = np.tile(np.tril(np.ones((8, 8), f), -1), (P, 1, 1))
    a["itn"] = np.tile(np.arange(ITEMS, dtype=f), (P, 1))
    a["erow"] = np.tile(TR_EXP + EX_CHUNKS * np.arange(8, dtype=f), (P, 1))
    return {k: np.ascontiguousarray(v, dtype=f) for k, v in a.items()}, order


def kernel(**inputs):
    import concourse.bacc as bacc
    from concourse.bass_utils import run_bass_kernel_spmd as run

    arrays, order = layout(**{k: np.asarray(v) for k, v in inputs.items()})
    nc = bacc.Bacc("TRN2", target_bir_lowering=False, num_devices=1)
    io = {n: nc.dram_tensor(n, v.shape, F32, kind="ExternalInput").ap() for n, v in arrays.items()}
    io["out"] = nc.dram_tensor("out", (P, KC, SEQ), F32, kind="ExternalOutput").ap()
    build(nc, io)
    r = run(nc, [arrays], core_ids=[0])
    y = r.results[0]["out"].transpose(1, 0, 2).reshape(D, SEQ)
    out = np.empty((1, SEQ, D), y.dtype)
    out[0, order] = y.T
    return out
```

```python
from contextlib import ExitStack

import numpy as np
import concourse.bass as bass
from concourse import mybir

F32 = mybir.dt.float32
F32R = mybir.dt.float32r
I32 = mybir.dt.int32
ALU = mybir.AluOpType
ACT = mybir.ActivationFunctionType
AX = mybir.AxisListType.X
ds = bass.ds

P = 128
D = 1024
KC = D // P
SEQ, CTX = 512, 256
T = SEQ + CTX
GRID_W, ROWS = 64, 8
EPS = 1e-6
A_HEADS, A_NOPE, A_ROPE, A_QK = 12, 64, 32, 96
A_QR, A_KVR = 256, 128
PAIRS0, PAIRS1 = A_HEADS // 2, 8
DH = 64
WIN_R, WIN_C = 8, 16
FF_CHUNKS = 22
EXPERTS, EX_CHUNKS = 8, 11
U = 1024
BIG = 1e30
BLK = 256
ITEMS = (2 * SEQ + EXPERTS * (BLK - 1)) // BLK
COLS = ITEMS + 1
BIAS_TILES = 7
LOCAL = [([0, 1], 0), ([0, 1, 2], 2), ([1, 2, 3], 2), ([2, 3], 5)]

TR_MOD0, N_MOD = 0, 16
TR_AIN = TR_MOD0 + N_MOD
TR_PAIR0 = TR_AIN + 2
TR_OUT0 = TR_PAIR0 + PAIRS0
TR_MLP = TR_OUT0 + 3
TR_MOD1 = TR_MLP + FF_CHUNKS
TR_PAIR1 = TR_MOD1 + N_MOD
TR_OUT1 = TR_PAIR1 + PAIRS1
TR_EXP = TR_OUT1 + 3
TR_END = TR_EXP + EXPERTS * EX_CHUNKS


LO0, USED0 = 4, 1
NPT = [2, 2]


class At:

    def __init__(self, units, fills):
        self.u, self.f = units, fills


def plan():
    at, u, f = {}, [0, 0, 0], [0, 0, 0]
    for name, nu, nf in (("md0", (N_MOD,) * 3, (4, 4, 4)), ("ain", (2, 2, 2), (1, 1, 0)), ("four", (2, 2, 2), (1, 1, 0)),
                         ("pr0", (PAIRS0,) * 3, (PAIRS0 // 2, PAIRS0 // 2, 0)),
                         ("out0", (3, 3, 2), (1, 1, 1)),
                         ("mlp", (3 * FF_CHUNKS,) * 3, (24, 24, 18)),
                         ("md1", (N_MOD,) * 3, (4, 4, 4)),
                         ("pr1", (PAIRS1,) * 3, (PAIRS1 // 2, PAIRS1 // 2, 0)),
                         ("out1", (3, 3, 2), (1, 1, 1)), ("exp", (0, 0, 0), (0, 0, 0))):
        at[name] = At(list(u), list(f))
        u = [x + y for x, y in zip(u, nu)]
        f = [x + y for x, y in zip(f, nf)]
    return at


AT = plan()
NORM_AT = {"n0": 0, "n1": 1, "n2": 4, "n3": 5}


def build(nc, io, stop_after=None):
    ctx = ExitStack()
    with ctx:
        _build(nc, io, ctx, stop_after)


def _build(nc, io, ctx, stop_after):
    def sem(name):
        return ctx.enter_context(nc.semaphore(name))

    at = [(nc.sbuf_base + 63) // 64 * 64]

    def place(name, shape, dt, offset=None):
        size = int(np.prod(shape[1:])) * 4
        off = at[0] if offset is None else offset
        t = nc.alloc_sbuf_tensor_at(name, shape, dt, offset=off)
        if offset is None:
            at[0] += (size + 31) // 32 * 32
        return t

    class Area:
        def __init__(self, start):
            self.at = start

        def __call__(self, name, shape, dt=F32):
            t = place(name, shape, dt, self.at)
            self.at += (int(np.prod(shape[1:])) * 4 + 31) // 32 * 32
            return t

        def pair(self, name, shape):
            return self(name + "_hi", shape, F32R), self(name + "_lo", shape, F32R)

    ones = place("ones", [P, P], F32)
    ident = place("ident", [P, P], F32)
    ones96 = place("ones96", [P, P], F32)
    ones64 = place("ones64", [P, P], F32)
    onesr = place("onesr", [P, P], F32)
    half2 = place("half2", [P, 2], F32)
    eps = place("eps", [P, 3], F32)
    cond = place("cond", [P, KC, 2], F32)
    scond = place("scond", [P, KC, 2], F32)
    scond_hl = place("scond_hl", [P, KC, P], F32R)
    hl_sum = place("hl_sum", [P, 2], F32)
    bmod = place("bmod", [P, 2, 48], F32)
    mods = place("mods", [P, 2, 48, 2], F32)
    ng = place("ng", [P, 2, 2, KC], F32)
    nsc = place("nsc", [P, 2, 2, KC, 2], F32)
    gcol = place("gcol", [P, 8], F32)
    res = place("res", [P, KC, T], F32)
    raw = [place(f"raw{s}", [P, 3, U], F32) for s in range(3)]
    whi = [place(f"w_hi{r}", [P, U], F32R) for r in range(3)]
    wlo = [place(f"w_lo{r}", [P, U], F32R) for r in range(3)]
    x_start = at[0]
    att_start = x_start + 2 * KC * T * 4

    PS = ctx.enter_context(nc.psum_tensor("ps", [P, 8, 512], F32))

    def slot(s, a=0, b=1024):
        return PS[:, 2 * s:2 * s + 2, :].rearrange("p a b -> p (a b)")[:, a:b]

    def bank(b, a, n):
        return PS[:, b, a:a + n]

    ax = Area(x_start)
    xn = ax.pair("xn", [P, KC, T])
    an = Area(att_start)
    sqb = [an(f"sqb{i}", [P, T]) for i in range(2)]
    rstd = an("rstd", [P, T])
    zb = [an(f"zb{i}", [P, T]) for i in range(2)]
    xfb = [an(f"xfb{i}", [P, T]) for i in range(2)]

    am = Area(x_start)
    raw_m = am("raw3", [P, 3, U])
    mrow = [am(f"mrow{i}", [P, 512]) for i in range(3)]

    ap_ = Area(att_start)
    plat = ap_("plat", [P, 6, T])
    ff_hl = ap_.pair("four_in", [P, 2, T])
    four_a = ap_.pair("four_a", [P, 6, 512])
    a0 = Area(x_start)
    cq = a0.pair("cq", [P, 2, T])
    ckv = a0.pair("ckv", [P, T])
    krope = a0("krope", [P, T])
    csg = a0("csg", [P, T])
    mix0 = a0("mix0", [P, KC, T])
    a0t = Area(att_start + 6 * T * 4)
    l0_sq = a0t("l0_sq", [P, 2, T])
    l0_rs = a0t("l0_rs", [P, 2, T])
    qtab = a0t("qtab", [P, T])
    ktab = a0t("ktab", [P, T])
    l0_t = a0t("l0_t", [P, 2, T])
    l0_x = a0t("l0_x", [P, 3, T])

    b0 = Area(att_start)
    q0 = b0.pair("q0", [P, 2, T])
    k0 = b0.pair("k0", [P, 2, T])
    v0 = b0.pair("v0", [P, 6, P])
    p0 = [b0(f"p0_{i}", [P, T]) for i in range(2)]
    pt0_start = b0.at
    pt0 = [b0.pair(f"pt0_{i}", [P, T]) for i in range(2)]
    b0.at = pt0_start
    qx0 = [b0(f"qx0_{h}", [P, T]) for h in range(2)]
    rk0 = b0("rk0", [P, T])
    kx0_0 = b0("kx0_0", [P, T])
    b0.at = pt0_start + 4 * T * 4
    sqq0 = b0("sqq0", [P, 2, T])
    sqk0 = b0("sqk0", [P, T])
    sqr = b0("sqr", [P, T])
    kx0 = [kx0_0, b0("kx0_1", [P, T])]
    b1 = Area(att_start)
    mix1 = b1("mix1", [P, KC, SEQ])
    q1 = b1.pair("q1", [P, 2, SEQ])
    k1 = b1.pair("k1", [P, T])
    v1 = b1.pair("v1", [P, 6, P])
    p1 = [b1(f"p1_{i}", [P, 5 * P]) for i in range(2)]
    biasb = b1("biasb", [P, 2, BIAS_TILES * P])
    pt1_start = b1.at
    pt1 = [b1.pair(f"pt1_{i}", [P, 5 * P]) for i in range(2)]
    b1.at = pt1_start
    qx1 = b1("qx1", [P, SEQ])
    rk1 = b1("rk1", [P, T])
    b1.at = pt1_start + 4 * 5 * P * 4
    sq1 = b1("sq1", [P, T])
    sqq1 = b1("sqq1", [P, SEQ])
    asm = Area(max(b0.at, b1.at))
    rq = asm("rq", [P, 12])
    rqs = asm("rqs", [P, 12])
    nmax = asm("nmax", [P, 8])
    nneg = asm("nneg", [P, 8])
    rsum = asm("rsum", [P, 8])
    rinv = asm("rinv", [P, 8])
    o0 = Area(att_start)
    mix0_hl = o0.pair("mix0s", [P, KC, T])
    o1 = Area(x_start)
    mix1_hl = o1.pair("mix1s", [P, KC, SEQ])
    f_ = Area(x_start)
    xg = f_.pair("xg", [P, KC, BLK])
    hx = [f_(f"hx{i}", [P, BLK]) for i in range(3)]
    sg = [f_(f"sg{i}", [P, BLK]) for i in range(3)]
    hb = [f_.pair(f"hb{i}", [P, BLK]) for i in range(3)]
    fn_sq = [f_(f"fn_sq{i}", [P, SEQ]) for i in range(2)]
    fn_rs = f_("fn_rs", [P, SEQ])
    fn_z = [f_(f"fn_z{i}", [P, SEQ]) for i in range(2)]
    fn_x = [f_(f"fn_x{i}", [P, BLK]) for i in range(2)]
    nscr = f_("nscr", [P, KC, 3])
    nshr = f_("nshr", [P, KC, 3])
    ngtr = f_("ngtr", [P, KC, 3])
    xt = f_.pair("xt", [P, 4, D])
    xfm = [f_(f"xfm{i}", [P, SEQ]) for i in range(2)]
    wr = f_("wr", [P, KC, 8])
    tri = f_("tri", [P, P])
    iot = f_("iot", [P, BLK])
    ltj = f_("ltj", [P, 8, 8])
    itn = f_("itn", [P, COLS])
    lg = f_("lg", [P, 4, 8])
    r64 = f_("r64", [P, 4, 8, 8])
    r64b = f_("r64b", [P, 4, 8, 8])
    rank = f_("rank", [P, 4, 8])
    seltok = f_("seltok", [P, 4, 8])
    lmax = f_("lmax", [P, 4])
    wexp = f_("wexp", [P, 4, 8])
    comb = f_("comb", [P, 4, 8])
    wsum = f_("wsum", [P, 4])
    posn = f_("posn", [P, 4, 8])
    cnts = f_("cnts", [P, 8])
    nit = f_("nit", [P, 8])
    endi = f_("endi", [P, 8])
    starti = f_("starti", [P, 8])
    erow = f_("erow", [P, 8])
    oneh = f_("oneh", [P, COLS, 8])
    oneb = f_("oneb", [P, COLS, 8])
    tab = f_("tab", [P, 6, COLS])
    tabi = f_("tabi", [P, 6, COLS], I32)
    posi = f_("posi", [P, 4, COLS])
    cmbi = f_("cmbi", [P, 4, COLS])
    gm = f_("gm", [P, 4, BLK], F32R)
    gt = f_("gt", [P, 2, SEQ], F32R)
    wslot = f_("wslot", [P, 2])
    yx = [f_(f"yx{i}", [P, D]) for i in range(2)]
    yhl = f_.pair("yhl", [P, 2, D])
    assert max(f_.at, asm.at, o0.at, ap_.at, a0t.at) <= nc.sbuf_usable_end, (
        f_.at, asm.at, o0.at, ap_.at, a0t.at, nc.sbuf_usable_end)

    s_const = sem("s_const")
    s_fetch = sem("s_fetch")
    s_scond = sem("s_scond")
    s_phase = sem("s_phase")
    s_chain = sem("s_chain")
    m_full3 = sem("m_raw_full3")
    m_blk = sem("m_blk")
    m_row = sem("m_row")
    m_tr = sem("m_tr")
    raw_full = [sem(f"raw_full{i}") for i in range(3)]
    hi_ready = [sem(f"hi_ready{i}") for i in range(3)]
    lo_ready = [sem(f"lo_ready{i}") for i in range(3)]
    used = [sem(f"used{i}") for i in range(3)]
    nr = [sem(f"norm_{w}") for w in ("sq", "sum", "std", "rstd", "z", "x", "hi", "lo")]
    lin_evac = sem("lin_evac")
    mx_hi, mx_lo = sem("mix_hi"), sem("mix_lo")
    c_sem = [sem(f"c_{n}") for n in ("sq", "sum", "std", "x", "hi", "lo", "kr")]
    f_sem = [sem(f"f_{n}") for n in ("a", "ahi", "alo", "evac", "fhi", "flo")]
    at_names = ("qsq", "qx", "qhi", "qlo", "ksq", "ks", "kstd", "rk", "kx", "khi", "klo",
                "vhi", "vlo", "rq", "rqs", "rqd", "qm", "kr", "kd", "vc", "vt",
                "s", "max", "neg", "exp", "inv", "p", "t", "hi", "lo", "o", "oev")
    a_sem = [{n: sem(f"a{l}_{n}") for n in at_names} for l in range(2)]
    a_sem[1]["sadd"], a_sem[1]["bias"] = sem("a1_sadd"), sem("a1_bias")
    s_zero = sem("s_zero")
    ff = {n: {w: sem(f"{n}_{w}") for w in ("hm", "sg", "hh", "h")} for n in ("mlp", "exp")}
    y_evac = sem("y_evac")
    e_sem = {n: sem(f"e_{n}") for n in
             ("in", "xt", "xthi", "xtlo", "sel", "exps", "pos", "tab", "gm", "gmt", "gt", "xhi", "xlo",
              "sc", "ws", "wsc", "yx", "yhi", "ylo", "sct", "scev")}
    s_out = sem("s_out")

    block = ctx.enter_context(nc.Block())

    def mm3(pe, out, w, x, first, last, skip=False):
        for n, (a, b) in enumerate(((0, 0), (0, 1), (1, 0))):
            ins = pe.matmul(out, w[a], x[b], start=first and n == 0, stop=last and n == 2,
                            skip_group_check=skip)
        return ins

    def pieces(n):
        return [(0, n)] if n <= 512 else [(0, 512), (512, n)]

    PHASES = {n: k for k, n in enumerate((
        "mods0", "norm0", "ain", "lat", "four", "att0", "split0", "out0", "mlp", "mods1", "norm1",
        "att1", "split1", "out1", "router", "moe"))}

    def phase_end(eng, name):
        eng.drain().then_inc(s_phase, 1)
        eng.wait_ge(s_phase, 4 * (PHASES[name] + 1))

    def three(row):
        return row.rearrange("p (r u) -> p r u", r=3)

    def all_of(t):
        return t[tuple(slice(None) for _ in t.shape)]

    CONSTS = (("ident", ident), ("ones", ones), ("cond", cond), ("bmod", bmod), ("ng", ng), ("gcol", gcol),
              ("ones96", ones96), ("ones64", ones64), ("onesr", onesr), ("half2", half2), ("hl_sum", hl_sum), ("eps", eps), ("qtab", qtab),
              ("ktab", ktab), ("xT", res))
    E_CONSTS = (("wr", wr), ("tri", tri), ("iot", iot), ("ltj", ltj), ("itn", itn), ("erow", erow))

    @block.sync
    def _(sp):
        for name, tile in CONSTS:
            sp.dma_start(all_of(tile), io[name]).then_inc(s_const, 16)
        W = io["stream"]

        def slots_split(units):
            for r in range(3):
                sp.wait_ge(lo_ready[r], LO0 + units[r])

        def load(row, s, done):
            sp.dma_start(raw[s][:, :, :], three(row)).then_inc(done[s], 16)

        def load_dyn(row, s, done):
            sp.dma_start((raw + [raw_m])[s][:, :, :], W[ds(row, 1)].rearrange("a p (r u) -> p (a r) u", r=3)
                         ).then_inc(done[s], 16)

        def load_mods(l):
            row0 = (TR_MOD0, TR_MOD1)[l]
            u = AT[("md0", "md1")[l]].u
            with sp.Fori(0, N_MOD // 4) as j:
                for s in range(4):
                    sp.wait_ge(lo_ready[2], j * 4 + (LO0 + u[2] + s - 3))
                    sp.sem_inc(s_fetch, 1)
                    load_dyn(j * 4 + (row0 + s), s, raw_full + [m_full3])

        def load_list(name, rows, slots):
            base = AT[name].u
            for n, row in enumerate(rows):
                if n >= slots:
                    for r in range(3):
                        sp.wait_ge(lo_ready[r], LO0 + base[r] + n - slots + 1)
                load(row, n % slots, raw_full)

        load_mods(0)
        slots_split(AT["ain"].u)
        load_list("ain", [W[TR_AIN + n] for n in range(2)], 2)
        slots_split(AT["four"].u)
        load_list("four", [io["fourier"][n] for n in range(2)], 2)
        slots_split(AT["pr0"].u)
        load_list("pr0", [W[TR_PAIR0 + n] for n in range(PAIRS0)], 2)
        slots_split(AT["out0"].u)
        load_list("out0", [W[TR_OUT0 + n] for n in range(3)], 3)
        slots_split(AT["mlp"].u)

        def load_chunks(g0, row0, base):
            for c in range(EX_CHUNKS):
                sp.wait_ge(lo_ready[2], g0 + (base[2] + c + LO0 - (1 if c < 2 else 2)))
                sp.sem_inc(s_fetch, 1)
                load_dyn(row0 + c, c % 3, raw_full)

        with sp.Fori(0, 3) as t:
            with sp.Fori(0, 2) as half:
                load_chunks(t * 22 + half * 11, half * 11 + TR_MLP, AT["mlp"].u)
        slots_split(AT["md1"].u)
        sp.wait_ge(s_phase, 4 * (PHASES["mlp"] + 1))
        load_mods(1)
        slots_split(AT["pr1"].u)
        base = AT["pr1"].u
        for n in range(PAIRS1):
            if n >= 2:
                for r in range(3):
                    sp.wait_ge(lo_ready[r], LO0 + base[r] + n - 1)
            load(W[TR_PAIR1 + n], n % 2, raw_full)
            if n == 0:
                sp.wait_ge(s_phase, 4 * (PHASES["norm1"] + 1))
            else:
                sp.wait_ge(a_sem[1]["sadd"], 16 * n)
            sp.dma_start(biasb[:, :, :], io["bias"][n]).then_inc(a_sem[1]["bias"], 16)
        slots_split(AT["out1"].u)
        load_list("out1", [W[TR_OUT1 + n] for n in range(3)], 3)
        sp.wait_ge(s_phase, 4 * (PHASES["out1"] + 1))
        for name, tile in E_CONSTS:
            sp.dma_start(all_of(tile), io[name]).then_inc(e_sem["in"], 16)
        sp.wait_ge(e_sem["tab"], 1)
        slots_split(AT["exp"].u)
        with sp.Fori(0, ITEMS) as it:
            live = sp.value_load(tabi[0:1, 0, ds(it, 1)], min_val=0, max_val=1)
            row = sp.value_load(tabi[0:1, 1, ds(it, 1)], min_val=0, max_val=TR_END - EX_CHUNKS)
            with sp.If(live > 0):
                load_chunks(it * EX_CHUNKS, row, AT["exp"].u)
        sp.wait_ge(s_phase, 4 * (PHASES["moe"] + 1))
        sp.dma_start(io["out"], res[:, :, 0:SEQ]).then_inc(s_out, 16)
        sp.wait_ge(s_out, 16)

    def hi_unit(act, r, src, cols, s, n_full, n_used):
        act.wait_ge((raw_full + [m_full3])[s], n_full * 16)
        act.wait_ge(used[r], n_used + USED0)
        act.activation(whi[r][:, 0:cols], src, ACT.Copy).then_inc(hi_ready[r], 1)

    def lo_unit(dve, r, src, cols, n):
        dve.wait_ge(hi_ready[r], n)
        dve.tensor_tensor(wlo[r][:, 0:cols], src, whi[r][:, 0:cols].bitcast(F32), ALU.subtract
                          ).then_inc(lo_ready[r], 1)

    def norm_pe(pe, nb, n, sq):
        SQ, SUM = nr[:2]
        for k in range(KC):
            pe.wait_ge(SQ, nb * 8 + (k + 1))
            for a, b in pieces(n):
                ins = pe.matmul(slot(3, a, b), ones[:, :], sq[k % 2][:, a:b], start=k == 0, stop=k == KC - 1)
            ins.then_inc(SUM, 1)

    def norm_act(act, nb, src, n, sq, rs, z, xf, cols, dst_hi):
        SQ, SUM, STD, RSTD, Z, X, HI, LO = nr
        for k in range(KC):
            if k >= 2:
                act.wait_ge(SUM, nb * 8 + (k - 1))
            act.activation(sq[k % 2][:, 0:n], src(k), ACT.Square).then_inc(SQ, 1)
        act.wait_ge(SUM, nb * 8 + 8)
        act.activation(rs[:, 0:n], slot(3, 0, n), ACT.Sqrt, bias=eps[:, 0:1], scale=1.0 / D).then_inc(STD, 1)
        for k in range(KC):
            act.wait_ge(Z, nb * 8 + (k + 1))
            if dst_hi is None:
                if k >= 2:
                    act.wait_ge(e_sem["xt"], k - 1)
            elif k >= 2:
                act.wait_ge(LO, nb * 8 + (k - 1))
            parts = cols(k)
            for a, b, scale, shift in parts:
                ins = act.activation(xf[k % 2][:, a:b], z[k % 2][:, a:b], ACT.Identity, bias=shift, scale=scale)
            ins.then_inc(X, 1)
            if dst_hi is not None:
                act.wait_ge(X, nb * 8 + (k + 1))
                act.activation(dst_hi(k), xf[k % 2][:, 0:n], ACT.Copy).then_inc(HI, 1)

    def norm_dve(dve, nb, src, n, rs, z, xf, dst_hi, dst_lo):
        SQ, SUM, STD, RSTD, Z, X, HI, LO = nr
        dve.wait_ge(STD, nb + 1)
        dve.reciprocal(rs[:, 0:n], rs[:, 0:n]).then_inc(RSTD, 1)
        dve.wait_ge(RSTD, nb + 1)
        for k in range(KC + 1):
            if k < KC:
                if k >= 2:
                    dve.wait_ge(X, nb * 8 + (k - 1))
                dve.tensor_tensor(z[k % 2][:, 0:n], src(k), rs[:, 0:n], ALU.mult).then_inc(Z, 1)
            if k >= 1 and dst_lo is not None:
                dve.wait_ge(HI, nb * 8 + k)
                dve.tensor_tensor(dst_lo(k - 1), xf[(k - 1) % 2][:, 0:n], dst_hi(k - 1).bitcast(F32),
                                  ALU.subtract).then_inc(LO, 1)

    def res_all(k):
        return res[:, k, :]

    def res_lat(k):
        return res[:, k, 0:SEQ]

    def res_block(t):
        return lambda k: res[:, k, ds(t * BLK, BLK)]

    def cols_all(l):
        return lambda k: [(0, SEQ, nsc[:, l, 0, k, 0:1], mods[:, l, k, 0:1]),
                          (SEQ, T, nsc[:, l, 0, k, 1:2], mods[:, l, k, 1:2])]

    def cols_block(t):
        return lambda k: [(0, BLK, nscr[:, k, ds(t, 1)], nshr[:, k, ds(t, 1)])]

    def cols_moe(k):
        return [(0, SEQ, nsc[:, 1, 1, k, 0:1], mods[:, 1, 3 * KC + k, 0:1])]

    def ffn_pe(pe, nm, g0, base, N, ymode, y_start, y_stop, y_wait):
        F = ff[nm]

        def down(c):
            pe.wait_ge(lo_ready[2], g0 + (base[2] + c + LO0 + 1))
            pe.wait_ge(F["h"], g0 + (c + 1))
            if c == 0:
                y_wait()
            first, last = y_start and c == 0, y_stop and c == EX_CHUNKS - 1
            if ymode == "channels":
                h = [t[:, 0:N] for t in hb[c % 3]]
                for m in range(KC):
                    o = bank(m // 2, (m % 2) * BLK, N)
                    for n, (a, b) in enumerate(((0, 0), (0, 1), (1, 0))):
                        ins = pe.matmul(o, (whi, wlo)[a][2][:, m * P:(m + 1) * P], h[b],
                                        start=first and n == 0 and m % 2 == 0, stop=last and n == 2,
                                        skip_group_check=True)
            else:
                for j in range(N // P):
                    for q in range(2):
                        ins = mm3(pe, bank(2 * j + q, 0, 512), [t[:, j * P:(j + 1) * P] for t in hb[c % 3]],
                                  [t[2][:, q * 512:(q + 1) * 512] for t in (whi, wlo)], first, last)
            ins.then_inc(used[2], 1)

        for c in range(EX_CHUNKS):
            pe.wait_ge(F["hm"], g0 + (c + 1))
            for r in range(2):
                pe.wait_ge(lo_ready[r], g0 + (base[r] + c + LO0 + 1))
                n = BLK if c == 0 else N
                for k in range(KC):
                    ins = mm3(pe, bank(4 + c % 3, r * BLK, n),
                              [t[r][:, k * P:(k + 1) * P] for t in (whi, wlo)],
                              [t[:, k, 0:n] for t in xg], k == 0, k == KC - 1)
                ins.then_inc(used[r], 1)
            if c:
                down(c - 1)
        down(EX_CHUNKS - 1)

    def ffn_act(act, nm, g0, item, at_, N, then=lambda: None):
        F = ff[nm]

        def hi(r, c):
            hi_unit(act, r, raw[c % 3][:, r, :], U, c % 3,
                    item * [4, 4, 3][c % 3] + (at_.f[c % 3] + c // 3 + 1), g0 + (at_.u[r] + c))

        hi(0, 0)
        hi(1, 0)
        then()
        for c in range(EX_CHUNKS):
            if c < EX_CHUNKS - 1:
                hi(0, c + 1)
            act.wait_ge(used[1], g0 + (at_.u[1] + c + 1 + USED0))
            act.activation(sg[c % 3][:, 0:N], bank(4 + c % 3, 0, N), ACT.Silu).then_inc(F["sg"], 1)
            if c < EX_CHUNKS - 1:
                hi(1, c + 1)
            act.wait_ge(F["hm"], g0 + (c + 3))
            act.activation(hb[c % 3][0][:, 0:N], hx[c % 3][:, 0:N], ACT.Copy).then_inc(F["hh"], 1)
            hi(2, c)

    def ffn_dve(dve, nm, g0, at_, N, then=lambda: None):
        F = ff[nm]

        def lo(r, c):
            lo_unit(dve, r, raw[c % 3][:, r, :], U, g0 + (at_.u[r] + c + 1))

        lo(0, 0)
        lo(1, 0)
        then()
        for c in range(EX_CHUNKS):
            if c < EX_CHUNKS - 1:
                lo(0, c + 1)
            dve.wait_ge(F["sg"], g0 + (c + 1))
            dve.tensor_tensor(hx[c % 3][:, 0:N], sg[c % 3][:, 0:N], bank(4 + c % 3, BLK, N), ALU.mult
                              ).then_inc(F["hm"], 1)
            if c < EX_CHUNKS - 1:
                lo(1, c + 1)
            dve.wait_ge(F["hh"], g0 + (c + 1))
            dve.tensor_tensor(hb[c % 3][1][:, 0:N], hx[c % 3][:, 0:N], hb[c % 3][0][:, 0:N].bitcast(F32),
                              ALU.subtract).then_inc(F["h"], 1)
            lo(2, c)

    UNITS = [[512, 128, 128], [U, U, U]]
    ROLE_ORDER = (1, 0, 2)

    def pair_hi(act, l, i, s, fills, r):
        n = UNITS[l][r]
        hi_unit(act, r, raw[s][:, r, 0:n], n, s, fills + 1, i + AT[("pr0", "pr1")[l]].u[r])

    def pair_lo(dve, l, i, s, fills, r):
        n = UNITS[l][r]
        lo_unit(dve, r, raw[s][:, r, 0:n], n, i + (AT[("pr0", "pr1")[l]].u[r] + 1))

    def steps_of(l):
        out = []
        for h in range(2):
            if l == 0:
                out += [(h, b, list(range(6)), 512, None) for b in range(4)]
                out += [(h, b, [4, 5], 0, None) for b in (4, 5)]
            else:
                out += [(h, b, LOCAL[b][0] + [4, 5], len(LOCAL[b][0]) * P, LOCAL[b][1]) for b in range(4)]
        return out

    def operands(l):
        return (q0, k0, v0, p0, pt0, mix0) if l == 0 else (q1, k1, v1, p1, pt1, mix1)

    def att_pe(pe, l, i, before):
        A = a_sem[l]
        q, k, v, p, pt, mix = operands(l)
        steps = steps_of(l)
        J = len(steps)

        def scores(j):
            h, b, tiles, nl, _ = steps[j]
            pe.wait_ge(A["oev"], i * J + (j + 1))
            s = j % 4
            qs = [t[:, h, b * P:(b + 1) * P] for t in q]
            if l == 0:
                runs = [(0, 0, 512), (512, 512, T)] if b < 4 else [(512, 512, T)]
                kk = [[t[:, h, x:y] for t in k] for _, x, y in runs]
            else:
                runs = [(0, tiles[0] * P, tiles[0] * P + nl), (512, 512, T)]
                kk = [[t[:, x:y] for t in k] for _, x, y in runs]
            for (o, x, y), ks in zip(runs, kk):
                ins = mm3(pe, slot(s, o, o + y - x), qs, ks, True, True)
            ins.then_inc(A["s"], 1)

        def turn(j):
            tiles = steps[j][2]
            pe.wait_ge(A["p"], i * J + (j + 1))
            for n in range(len(tiles)):
                ins = pe.transpose(slot(j % 4, n * P, (n + 1) * P), p[j % 2][:, n * P:(n + 1) * P], ident[:, :])
            ins.then_inc(A["t"], 1)

        def values(j):
            tiles = steps[j][2]
            pe.wait_ge(A["lo"], i * J + (j + 1))
            for n, kt in enumerate(tiles):
                ins = mm3(pe, slot(j % 4, 768, 896), [t[:, kt, :] for t in v],
                          [t[:, n * P:(n + 1) * P] for t in pt[j % len(pt)]], n == 0, n == len(tiles) - 1)
            ins.then_inc(A["o"], 1)

        for j in range(J + 3):
            if j < J:
                before(j)
                scores(j)
            if j >= 3:
                values(j - 3)
            if 1 <= j <= J:
                turn(j - 1)

    def att_act(act, l, i, nxt):
        A = a_sem[l]
        q, k, v, p, pt, mix = operands(l)
        steps = steps_of(l)
        J = len(steps)
        npt = NPT[l]

        def out(j):
            h, b = steps[j][:2]
            act.wait_ge(A["o"], i * J + (j + 1 + npt))
            act.activation(mix[h * 64:(h + 1) * 64, ds(i, 1), b * P:(b + 1) * P],
                           slot(j % 4, 768, 896)[h * 64:(h + 1) * 64, :], ACT.Copy).then_inc(A["oev"], 1)

        for j in range(J + 3):
            if j >= 3:
                out(j - 3)
            if j < J:
                h, b, tiles, nl, _ = steps[j]
                n = len(tiles) * P
                c = j % 8
                act.wait_ge(A["neg"], i * J + (j + 1))
                act.wait_ge(A["t"], i * J + (j + 1))
                if l == 0:
                    a = 0 if b < 4 else 512
                    act.activation(p[j % 2][:, 0:n], slot(j % 4, a, a + n), ACT.Exp, bias=nneg[:, c:c + 1],
                                   scale=rq[:, h * 6 + b:h * 6 + b + 1], accum_out=rsum[:, c:c + 1]
                                   ).then_inc(A["exp"], 1)
                else:
                    act.activation(p[j % 2][:, 0:n], p[j % 2][:, 0:n], ACT.Exp, bias=nneg[:, c:c + 1],
                                   accum_out=rsum[:, c:c + 1]).then_inc(A["exp"], 1)
            if 1 <= j <= J:
                n = len(steps[j - 1][2]) * P
                act.wait_ge(A["t"], i * J + (j + 2))
                act.wait_ge(A["o"], i * J + j)
                act.activation(pt[(j - 1) % npt][0][:, 0:n], slot((j - 1) % 4, 0, n), ACT.Copy
                               ).then_inc(A["hi"], 1)
            if J - 2 <= j <= J and nxt:
                pair_hi(act, l, *nxt, ROLE_ORDER[j - J + 2])

    def att_dve(dve, l, i, nxt):
        A = a_sem[l]
        q, k, v, p, pt, mix = operands(l)
        steps = steps_of(l)
        J = len(steps)
        npt = NPT[l]

        def turned(j):
            n = len(steps[j][2]) * P
            dve.wait_ge(A["hi"], i * J + (j + 1))
            dve.tensor_tensor(pt[j % npt][1][:, 0:n], slot(j % 4, 0, n), pt[j % npt][0][:, 0:n].bitcast(F32),
                              ALU.subtract).then_inc(A["lo"], 1)

        for j in range(J + 2):
            if j < J:
                h, b, tiles, nl, bt = steps[j]
                n = len(tiles) * P
                c = j % 8
                dve.wait_ge(A["s"], i * J + (j + 1))
                if l == 0:
                    a = 0 if b < 4 else 512
                    dve.reduce_max(nmax[:, c:c + 1], slot(j % 4, a, a + n), AX).then_inc(A["max"], 1)
                    dve.wait_ge(A["max"], i * J + (j + 1))
                    dve.tensor_scalar(nneg[:, c:c + 1], nmax[:, c:c + 1], rq[:, h * 6 + b:h * 6 + b + 1], -1.0,
                                      ALU.mult, ALU.mult).then_inc(A["neg"], 1)
                else:
                    if j == 0:
                        dve.wait_ge(A["bias"], i * 16 + 16)
                    dve.wait_ge(A["t"], i * J + (j + 1))
                    r = rq[:, b * 2 + h:b * 2 + h + 1]
                    dve.scalar_tensor_tensor(out=p[j % 2][:, 0:nl], in0=slot(j % 4, 0, nl), scalar=r,
                                             in1=biasb[:, h, bt * P:bt * P + nl], op0=ALU.mult, op1=ALU.add
                                             ).then_inc(A["sadd"], 1)
                    dve.tensor_scalar(p[j % 2][:, nl:n], slot(j % 4, 512, T), r, None, ALU.mult
                                      ).then_inc(A["sadd"], 1)
                    dve.wait_ge(A["sadd"], i * (2 * J) + (2 * j + 2))
                    dve.reduce_max(nmax[:, c:c + 1], p[j % 2][:, 0:n], AX).then_inc(A["max"], 1)
                    dve.wait_ge(A["max"], i * J + (j + 1))
                    dve.tensor_scalar(nneg[:, c:c + 1], nmax[:, c:c + 1], -1.0, None, ALU.mult
                                      ).then_inc(A["neg"], 1)
            if j >= 2:
                turned(j - 2)
            if j < J:
                dve.wait_ge(A["exp"], i * J + (j + 1))
                dve.reciprocal(rinv[:, c:c + 1], rsum[:, c:c + 1]).then_inc(A["inv"], 1)
            if J - 2 <= j <= J and nxt:
                pair_lo(dve, l, *nxt, ROLE_ORDER[j - J + 2])

    def att_pool(pool, l, i):
        A = a_sem[l]
        p = operands(l)[3]
        steps = steps_of(l)
        J = len(steps)
        for j in range(J):
            n = len(steps[j][2]) * P
            pool.wait_ge(A["inv"], i * J + (j + 1))
            pool.tensor_tensor(p[j % 2][:, 0:n], p[j % 2][:, 0:n],
                               rinv[:, j % 8:j % 8 + 1].broadcast_to([P, n]), ALU.mult).then_inc(A["p"], 1)

    def pairs(eng, l, body):
        name, n = ("pr0", PAIRS0) if l == 0 else ("pr1", PAIRS1)
        f = AT[name].f
        with eng.Fori(0, n // 2 - 1) as ii:
            body(ii * 2, (ii * 2 + 1, 1, ii + f[1]))
            body(ii * 2 + 1, (ii * 2 + 2, 0, ii + (f[0] + 1)))
        body(n - 2, (n - 1, 1, n // 2 - 1 + f[1]))
        body(n - 1, None)

    def items(eng, body):
        eng.wait_ge(e_sem["tab"], 1)
        with eng.Fori(0, ITEMS) as it:
            live = eng.value_load(tabi[0:1, 0, ds(it, 1)], min_val=0, max_val=1)
            wide = eng.value_load(tabi[0:1, 2, ds(it, 1)], min_val=0, max_val=1)
            with eng.If(live > 0):
                with eng.If(wide > 0):
                    body(it, BLK)
                with eng.Else():
                    body(it, P)
                eng.nop()
            eng.nop()

    def norm_act_first(act, nb):
        for k in range(KC):
            if k >= 2:
                act.wait_ge(nr[1], nb * 8 + (k - 1))
            act.activation(fn_sq[k % 2][:, :], res_lat(k), ACT.Square).then_inc(nr[0], 1)
        act.wait_ge(nr[1], nb * 8 + 8)
        act.activation(fn_rs[:, :], slot(3, 0, SEQ), ACT.Sqrt, bias=eps[:, 0:1], scale=1.0 / D).then_inc(nr[2], 1)

    def turned_hi(act, k):
        act.wait_ge(e_sem["xt"], k + 1)
        act.activation(xt[0][:, :, k * P:(k + 1) * P], bank(k % 4, 0, 512).rearrange("p (b c) -> p b c", b=4),
                       ACT.Copy).then_inc(e_sem["xthi"], 1)

    def y_part(J, part):
        if J == 2:
            return slot(part), part, 0, D
        return bank(part, 0, 512), 0, part * 512, part * 512 + 512

    @block.tensor
    def _(pe):
        for r in range(3):
            pe.sem_inc(used[r], USED0)
        for l in range(2):
            pe.sem_inc(a_sem[l]["t"], 2)
            pe.sem_inc(a_sem[l]["o"], NPT[l])

        def mods_pe(l):
            u = AT[("md0", "md1")[l]].u

            def turn_block(j, b):
                pe.wait_ge(m_row, j * 3 + (12 * l + b + 1 + 3))
                for n in range(4):
                    ins = pe.matmul(PS[:, 7, ds(j * 24 + (b * 4 + n) * 2, 2)], mrow[b][:, n * P:(n + 1) * P],
                                    hl_sum[:, :], start=True, stop=True)
                ins.then_inc(m_tr, 1)

            with pe.Fori(0, N_MOD // 4) as j:
                for b in range(3):
                    pe.wait_ge(m_row, j * 3 + (12 * l + b + 1))
                    for q in range(4):
                        t, r = (b * 4 + q) // 3, (b * 4 + q) % 3
                        pe.wait_ge(lo_ready[r], j * 4 + (LO0 + u[r] + t + 1))
                        for h in range(2):
                            for w in (whi, wlo):
                                ins = pe.matmul(bank(b, 0, 512), scond_hl[:, 2 * q + h, :],
                                                w[r][:, h * 512:(h + 1) * 512], start=q == 0 and h == 0 and w is whi,
                                                stop=q == 3 and h == 1 and w is wlo)
                        ins.then_inc(used[r], 1)
                    pe.drain().then_inc(m_blk, 1)
                    if b:
                        turn_block(j, b - 1)
                turn_block(j, 2)

        def linear(nm, subs, x, n, before):
            for m in range(subs):
                r, t = m % 3, m // 3
                pe.wait_ge(lin_evac, before + m + 1)
                pe.wait_ge(lo_ready[r], LO0 + AT[nm].u[r] + t + 1)
                for k in range(KC):
                    for a, b in pieces(n):
                        ins = mm3(pe, slot(m % 4, a, b), [w[r][:, k * P:(k + 1) * P] for w in (whi, wlo)],
                                  [h[:, k, a:b] for h in x], k == 0, k == KC - 1)
                ins.then_inc(used[r], 1)

        pe.wait_ge(s_const, 16 * len(CONSTS))
        pe.wait_ge(s_scond, 4)
        mods_pe(0)
        phase_end(pe, "mods0")
        norm_pe(pe, 0, T, sqb)
        phase_end(pe, "norm0")
        linear("ain", 6, xn, T, 0)
        phase_end(pe, "ain")
        SQ, SUM = c_sem[0], c_sem[1]
        pe.wait_ge(SQ, 2)
        for kc in range(2):
            for a, b in pieces(T):
                ins = pe.matmul(slot(0, a, b), ones[:, :], l0_sq[:, kc, a:b], start=kc == 0, stop=kc == 1)
        ins.then_inc(SUM, 1)
        pe.wait_ge(SQ, 3)
        for a, b in pieces(T):
            ins = pe.matmul(slot(1, a, b), ones[:, :], l0_x[:, 0, a:b], start=True, stop=True)
        ins.then_inc(SUM, 1)
        phase_end(pe, "lat")
        fa, fahi, falo, fev, fhi, flo = f_sem
        u4 = AT["four"].u
        pe.wait_ge(flo, 2)
        pe.wait_ge(lo_ready[0], LO0 + u4[0] + 1)
        for tb in range(6):
            if tb >= 4:
                pe.wait_ge(falo, tb - 3)
            for ch in range(2):
                ins = mm3(pe, slot(tb % 4, ch * 256, ch * 256 + 256), [t[:, ch, tb * P:(tb + 1) * P] for t in ff_hl],
                          [w[0][:, 0:256] for w in (whi, wlo)], True, True)
            ins.then_inc(fa, 1)
        pe.drain().then_inc(used[0], 1)
        pe.wait_ge(falo, 6)
        for u in range(4):
            r, t = (u + 1) % 3, (u + 1) // 3
            pe.wait_ge(lo_ready[r], LO0 + u4[r] + t + 1)
            for ch in range(2):
                for kb in range(2):
                    o = ch * 256 + (u // 2) * 128
                    ins = mm3(pe, slot(ch, 0, 512), [x[:, (u % 2) * 2 + kb, o:o + 128] for x in four_a],
                              [w[r][:, kb * 512:(kb + 1) * 512] for w in (whi, wlo)],
                              u == 0 and kb == 0, u == 3 and kb == 1)
            ins.then_inc(used[r], 1)
        pe.wait_ge(lo_ready[2], LO0 + u4[2] + 2)
        for ch in range(2):
            for u in range(2):
                for kb in range(2):
                    o = ch * 256 + u * 128
                    ins = mm3(pe, slot(ch, 512, 768), [x[:, 4 + kb, o:o + 128] for x in four_a],
                              [w[2][:, (u * 2 + kb) * 256:(u * 2 + kb + 1) * 256] for w in (whi, wlo)],
                              u == 0 and kb == 0, u == 1 and kb == 1)
        ins.then_inc(used[2], 1)
        phase_end(pe, "four")

        def pair0(i, nxt):
            A, u = a_sem[0], AT["pr0"].u
            pe.wait_ge(A["oev"], i * 12 + 4)
            pe.wait_ge(lo_ready[1], i + (u[1] + LO0 + 1))
            for a, b in pieces(T):
                ins = mm3(pe, slot(2, a, b), [w[1][:, 0:P] for w in (whi, wlo)], [x[:, a:b] for x in ckv],
                          True, True)
            ins.then_inc(used[1], 1)

            def queries(h):
                for a, b in pieces(T):
                    for kc in range(2):
                        o = (h * 2 + kc) * P
                        ins = mm3(pe, slot(h, a, b), [w[0][:, o:o + P] for w in (whi, wlo)],
                                  [x[:, kc, a:b] for x in cq], kc == 0, kc == 1)
                return ins

            pe.wait_ge(lo_ready[0], i + (u[0] + LO0 + 1))
            queries(0).then_inc(A["qm"], 1)
            pe.wait_ge(A["ksq"], i + 1)
            for a, b in pieces(T):
                pe.matmul(slot(3, a, b), ones64[:, :], sqk0[:, a:b], start=True, stop=False)
                ins = pe.matmul(slot(3, a, b), onesr[:, :], sqr[:, a:b], start=False, stop=True)
            ins.then_inc(A["ks"], 1)
            queries(1).then_inc(used[0], 1)
            pe.wait_ge(lo_ready[2], i + (u[2] + LO0 + 1))
            pe.wait_ge(A["kstd"], i + 1)
            for tb in range(6):
                ins = mm3(pe, slot(3, tb * P, (tb + 1) * P), [x[:, tb * P:(tb + 1) * P] for x in ckv],
                          [w[2][:, 0:P] for w in (whi, wlo)], True, True)
            for h in range(2):
                pe.wait_ge(A["qsq"], i * 2 + (h + 1))
                for b in range(6):
                    ins = pe.matmul(slot(3, 1000 + h * 6 + b, 1001 + h * 6 + b), sqq0[:, h, b * P:(b + 1) * P],
                                    ones96[:, 0:1], start=True, stop=True)
            ins.then_inc(used[2], 1)

            def before(j):
                if j == 0:
                    pe.wait_ge(A["klo"], i * 2 + 1)
                    pe.wait_ge(A["qlo"], i * 2 + 1)
                if j == 1:
                    pe.wait_ge(A["qx"], i * 2 + 2)
                if j == 2:
                    pe.wait_ge(A["kx"], i * 2 + 2)
                if j == 3:
                    pe.wait_ge(A["rqs"], i + 1)
                    pe.wait_ge(A["vlo"], i + 1)
                if j == 6:
                    pe.wait_ge(A["klo"], i * 2 + 2)
                    pe.wait_ge(A["qlo"], i * 2 + 2)

            att_pe(pe, 0, i, before)

        pairs(pe, 0, pair0)
        phase_end(pe, "att0")
        phase_end(pe, "split0")
        linear("out0", 8, mix0_hl, T, 6)
        phase_end(pe, "out0")

        with pe.Fori(0, 3) as t:
            norm_pe(pe, t + NORM_AT["n1"], BLK, fn_sq)
            pe.wait_ge(nr[7], t * 8 + (NORM_AT["n1"] + 1) * 8)
            ffn_pe(pe, "mlp", t * 22, AT["mlp"].u, BLK, "channels", True, False,
                   lambda: pe.wait_ge(y_evac, t + 1))
            ffn_pe(pe, "mlp", t * 22 + 11, AT["mlp"].u, BLK, "channels", False, True, lambda: None)
        phase_end(pe, "mlp")
        mods_pe(1)
        phase_end(pe, "mods1")
        norm_pe(pe, NORM_AT["n2"], T, sqb)
        phase_end(pe, "norm1")

        def pair1(i, nxt):
            A, u = a_sem[1], AT["pr1"].u

            def project(r, slot_, n, ks):
                for k in ks:
                    for a, b in pieces(n):
                        ins = mm3(pe, slot(slot_, a, b), [w[r][:, k * P:(k + 1) * P] for w in (whi, wlo)],
                                  [x[:, k, a:b] for x in xn], k == 0, k == KC - 1)
                return ins

            pe.wait_ge(A["oev"], i * 8 + 4)
            pe.wait_ge(lo_ready[1], i + (u[1] + LO0 + 1))
            project(1, 1, T, range(KC)).then_inc(used[1], 1)
            pe.wait_ge(lo_ready[0], i + (u[0] + LO0 + 1))
            project(0, 2, SEQ, range(2))
            pe.wait_ge(A["ksq"], i + 1)
            for a, b in pieces(T):
                ins = pe.matmul(slot(0, a, b), ones64[:, :], sq1[:, a:b], start=True, stop=True)
            ins.then_inc(A["ks"], 1)
            project(0, 2, SEQ, range(2, KC)).then_inc(used[0], 1)
            pe.wait_ge(lo_ready[2], i + (u[2] + LO0 + 1))
            project(2, 3, T, range(KC)).then_inc(used[2], 1)
            pe.wait_ge(A["qsq"], i + 1)
            for b in range(4):
                ins = pe.matmul(slot(2, 1000 + b * 2, 1002 + b * 2), sqq1[:, b * P:(b + 1) * P], half2[:, :],
                                start=True, stop=True)
            ins.then_inc(A["rq"], 1)

            def before(j):
                if j == 0:
                    pe.wait_ge(A["klo"], i + 1)
                    pe.wait_ge(A["qlo"], i + 1)
                if j == 1:
                    pe.wait_ge(A["vc"], i + 1)
                    for tb in range(6):
                        ins = pe.transpose(slot(3, tb * P, (tb + 1) * P), sq1[:, tb * P:(tb + 1) * P], ident[:, :])
                    ins.then_inc(A["vt"], 1)
                if j == 2:
                    pe.wait_ge(A["rqs"], i + 1)
                if j == 3:
                    pe.wait_ge(A["vlo"], i + 1)

            att_pe(pe, 1, i, before)

        pe.wait_ge(s_zero, 1)
        pairs(pe, 1, pair1)
        phase_end(pe, "att1")
        phase_end(pe, "split1")
        linear("out1", 8, mix1_hl, SEQ, 14)
        phase_end(pe, "out1")

        E = e_sem
        norm_pe(pe, NORM_AT["n3"], SEQ, fn_sq)
        pe.wait_ge(E["in"], 16 * len(E_CONSTS))
        for k in range(KC):
            pe.wait_ge(nr[5], (NORM_AT["n3"]) * 8 + k + 1)
            if k >= 4:
                pe.wait_ge(E["xtlo"], k - 3)
            for b in range(4):
                ins = pe.transpose(bank(k % 4, b * P, P), xfm[k % 2][:, b * P:(b + 1) * P], ident[:, :])
            for b in range(4):
                ins = pe.matmul(bank(5, b * 8, 8), xfm[k % 2][:, b * P:(b + 1) * P], wr[:, k, :],
                                start=k == 0 and b == 0, stop=k == KC - 1, skip_group_check=True)
            ins.then_inc(E["xt"], 1)
        pe.wait_ge(E["sel"], 1)
        for b in range(4):
            for b2 in range(b + 1):
                ins = pe.matmul(bank(4, b * 8, 8), (tri if b2 == b else ones)[:, :], seltok[:, b2, :],
                                start=b2 == 0, stop=b2 == b)
        for b2 in range(4):
            ins = pe.matmul(bank(4, 32, 8), ones[:, :], seltok[:, b2, :], start=b2 == 0, stop=b2 == 3)
        ins.then_inc(E["pos"], 1)
        phase_end(pe, "router")

        def gather(g):
            pe.wait_ge(E["gm"], g + 1)
            for k in range(KC):
                pe.wait_ge(E["xlo"], g * 8 + (k + 1))
                for b in range(4):
                    for w in range(2):
                        ins = pe.matmul(bank(5 + k % 3, 0, BLK), xt[w][:, b, k * P:(k + 1) * P], gm[:, b, :],
                                        start=b == 0 and w == 0, stop=b == 3 and w == 1)
                ins.then_inc(E["gmt"], 1)

        def item(it, N):
            J = N // P
            pe.wait_ge(E["xlo"], it * 8 + 11)
            for j in range(J):
                for b in range(4):
                    ins = pe.matmul(bank(5, j, 1), gm[:, b, j * P:(j + 1) * P].bitcast(F32),
                                    cmbi[:, b, ds(it, 1)], start=b == 0, stop=b == 3)
            ins.then_inc(E["ws"], 1)
            for j in range(J):
                for b in range(4):
                    ins = pe.transpose(bank(7 - j, b * P, P), gm[:, b, j * P:(j + 1) * P].bitcast(F32), ident[:, :])
            ins.then_inc(E["sc"], 1)
            pe.wait_ge(E["gt"], it + 1)
            pe.wait_ge(E["wsc"], it + 1)
            ffn_pe(pe, "exp", it * EX_CHUNKS, AT["exp"].u, N, "slots", True, True,
                   lambda: pe.wait_ge(E["scev"], it * 8 + 4))
            gather(it + 1)
            pe.wait_ge(E["ylo"], it * 2 + 2)
            for m in range(KC):
                pe.wait_ge(E["scev"], it * 8 + (m + 1))
                for j in range(J):
                    for w in range(2):
                        ins = pe.matmul(bank(m % 4, 0, 512), yhl[w][:, j, m * P:(m + 1) * P], gt[:, j, :],
                                        start=j == 0 and w == 0, stop=j == J - 1 and w == 1)
                ins.then_inc(E["sct"], 1)

        gather(0)
        items(pe, item)
        phase_end(pe, "moe")

    @block.scalar
    def _(act):
        act.sem_inc(a_sem[0]["oev"], 4)
        act.sem_inc(a_sem[1]["oev"], 4)
        act.wait_ge(s_const, 16 * len(CONSTS))
        act.activation(scond[:, :, :], cond[:, :, :], ACT.Silu).then_inc(s_scond, 1)
        act.wait_ge(s_scond, 2)
        act.activation(scond_hl[:, :, 0:2], scond[:, :, :], ACT.Copy).then_inc(s_scond, 1)

        def mods_act(l):
            name = ("md0", "md1")[l]
            u, f = AT[name].u, AT[name].f + [4 * l]
            with act.Fori(0, N_MOD // 4) as j:
                for b in range(3):
                    for q in range(4):
                        t, r = (b * 4 + q) // 3, (b * 4 + q) % 3
                        hi_unit(act, r, (raw + [raw_m])[t][:, r, :], U, t, j + (f[t] + 1), j * 4 + (u[r] + t))
                    act.wait_ge(m_blk, j * 3 + (12 * l + b + 1))
                    if 12 * l + b >= 3:
                        act.wait_ge(m_tr, j * 3 + (12 * l + b - 2))
                    act.activation(mrow[b][:, :], bank(b, 0, 512), ACT.Copy).then_inc(m_row, 1)

        mods_act(0)
        phase_end(act, "mods0")
        norm_act(act, 0, res_all, T, sqb, rstd, zb, xfb, cols_all(0), lambda k: xn[0][:, k, :])
        phase_end(act, "norm0")

        def linear_hi(nm, m):
            r, t = m % 3, m // 3
            hi_unit(act, r, raw[t][:, r, :], U, t, AT[nm].f[t] + 1, AT[nm].u[r] + t)

        for m in range(3):
            linear_hi("ain", m)
        for m in range(6):
            if m + 3 < 6:
                linear_hi("ain", m + 3)
            act.wait_ge(used[m % 3], USED0 + AT["ain"].u[m % 3] + m // 3 + 1)
            act.activation(plat[:, m, :], slot(m % 4, 0, T), ACT.Copy).then_inc(lin_evac, 1)
        phase_end(act, "ain")
        SQ, SUM, STD, X, HI, LO, KR = c_sem
        for kc in range(2):
            act.activation(l0_sq[:, kc, :], plat[:, kc, :], ACT.Square).then_inc(SQ, 1)
        act.activation(l0_x[:, 0, :], plat[:, 2, :], ACT.Square).then_inc(SQ, 1)
        act.activation(sqr[:, :], plat[:, 3, :], ACT.Square)
        act.wait_ge(SUM, 1)
        act.activation(l0_rs[:, 0, :], slot(0, 0, T), ACT.Sqrt, bias=eps[:, 0:1], scale=1.0 / A_QR).then_inc(STD, 1)
        act.wait_ge(SUM, 2)
        act.activation(l0_rs[:, 1, :], slot(1, 0, T), ACT.Sqrt, bias=eps[:, 0:1], scale=1.0 / A_KVR).then_inc(STD, 1)
        for n, (dst, src) in enumerate(((cq[0][:, 0, :], l0_t[:, 0, :]), (cq[0][:, 1, :], l0_t[:, 1, :]),
                                        (ckv[0][:, :], l0_x[:, 1, :]))):
            act.wait_ge(X, n + 1)
            act.activation(dst, src, ACT.Copy).then_inc(HI, 1)
        phase_end(act, "lat")
        fa, fahi, falo, fev, fhi, flo = f_sem
        for ch in range(2):
            act.activation(ff_hl[0][:, ch, :], plat[:, 4 + ch, :], ACT.Copy).then_inc(fhi, 1)
        for m in range(3):
            linear_hi("four", m)
        for tb in range(6):
            act.wait_ge(fa, tb + 1)
            act.activation(four_a[0][:, tb, :], slot(tb % 4, 0, 512), ACT.Copy).then_inc(fahi, 1)
        for m in range(3, 6):
            linear_hi("four", m)
        act.wait_ge(used[2], USED0 + AT["four"].u[2] + 2)
        for ch in range(2):
            act.activation(mix0[:, 6 + ch, :], slot(ch, 0, T), ACT.Copy)
        phase_end(act, "four")

        def pair0(i, nxt):
            A, u = a_sem[0], AT["pr0"].u
            act.wait_ge(used[1], i + (u[1] + USED0 + 1))
            act.activation(sqk0[:, :], slot(2, 0, T), ACT.Square).then_inc(A["ksq"], 1)
            act.wait_ge(A["qm"], i + 1)
            act.activation(sqq0[:, 0, :], slot(0, 0, T), ACT.Square).then_inc(A["qsq"], 1)
            act.wait_ge(A["qx"], i * 2 + 1)
            act.activation(q0[0][:, 0, :], qx0[0][:, :], ACT.Copy).then_inc(A["qhi"], 1)
            act.wait_ge(A["ks"], i + 1)
            act.activation(rk0[:, :], slot(3, 0, T), ACT.Sqrt, bias=eps[:, 0:1], scale=1.0 / A_QK
                           ).then_inc(A["kstd"], 1)
            act.wait_ge(used[0], i + (u[0] + USED0 + 1))
            act.activation(sqq0[:, 1, :], slot(1, 0, T), ACT.Square).then_inc(A["qsq"], 1)
            act.wait_ge(used[2], i + (u[2] + USED0 + 1))
            act.activation(rqs[:, 0:12], slot(3, 1000, 1012), ACT.Sqrt, bias=eps[:, 1:2]).then_inc(A["rqs"], 1)
            act.activation(v0[0][:, :, :], slot(3, 0, T), ACT.Copy).then_inc(A["vhi"], 1)
            for h in range(2):
                act.wait_ge(A["kx"], i * 2 + (h + 1))
                if h == 0:
                    act.wait_ge(A["kd"], i + 1)
                act.activation(k0[0][:, h, :], kx0[h][:, :], ACT.Copy).then_inc(A["khi"], 1)
            act.wait_ge(A["qx"], i * 2 + 2)
            act.activation(q0[0][:, 1, :], qx0[1][:, :], ACT.Copy).then_inc(A["qhi"], 1)
            att_act(act, 0, i, nxt)

        for r in ROLE_ORDER:
            pair_hi(act, 0, 0, 0, AT["pr0"].f[0], r)
        pairs(act, 0, pair0)
        phase_end(act, "att0")
        for k in range(KC):
            act.activation(mix0_hl[0][:, k, :], mix0[:, k, :], ACT.Copy).then_inc(mx_hi, 1)
        phase_end(act, "split0")
        for m in range(8):
            linear_hi("out0", m)
        phase_end(act, "out0")
        with act.Fori(0, 3) as t:
            act.wait_ge(used[1], t * 22 + (AT["mlp"].u[1] + USED0))
            norm_act(act, t + NORM_AT["n1"], res_block(t), BLK, fn_sq, fn_rs, fn_z, fn_x, cols_block(t),
                     lambda k: xg[0][:, k, :])
            ffn_act(act, "mlp", t * 22, t * 2, AT["mlp"], BLK)
            ffn_act(act, "mlp", t * 22 + 11, t * 2 + 1, AT["mlp"], BLK)
        phase_end(act, "mlp")
        mods_act(1)
        phase_end(act, "mods1")
        norm_act(act, NORM_AT["n2"], res_all, T, sqb, rstd, zb, xfb, cols_all(1), lambda k: xn[0][:, k, :])
        phase_end(act, "norm1")

        def pair1(i, nxt):
            A, u = a_sem[1], AT["pr1"].u
            act.wait_ge(used[1], i + (u[1] + USED0 + 1))
            act.activation(sq1[:, :], slot(1, 0, T), ACT.Square).then_inc(A["ksq"], 1)
            act.wait_ge(A["ks"], i + 1)
            act.activation(rk1[:, :], slot(0, 0, T), ACT.Sqrt, bias=eps[:, 0:1], scale=1.0 / DH
                           ).then_inc(A["kstd"], 1)
            act.wait_ge(used[0], i + (u[0] + USED0 + 1))
            act.activation(sqq1[:, :], slot(2, 0, SEQ), ACT.Square).then_inc(A["qsq"], 1)
            act.wait_ge(A["kx"], i + 1)
            act.activation(k1[0][:, :], rk1[:, :], ACT.Copy).then_inc(A["khi"], 1)
            act.wait_ge(A["qx"], i + 1)
            for h in range(2):
                rows = slice(h * 64, h * 64 + 64)
                ins = act.activation(q1[0][rows, h, :], qx1[rows, :], ACT.Copy)
            ins.then_inc(A["qhi"], 1)
            act.wait_ge(used[2], i + (u[2] + USED0 + 1))
            act.activation(sq1[:, :], slot(3, 0, T), ACT.Copy).then_inc(A["vc"], 1)
            act.wait_ge(A["rq"], i + 1)
            act.activation(rqs[:, 0:8], slot(2, 1000, 1008), ACT.Sqrt, bias=eps[:, 2:3]).then_inc(A["rqs"], 1)
            act.wait_ge(A["vt"], i + 1)
            act.activation(v1[0][:, :, :], slot(3, 0, T), ACT.Copy).then_inc(A["vhi"], 1)
            att_act(act, 1, i, nxt)

        for r in ROLE_ORDER:
            pair_hi(act, 1, 0, 0, AT["pr1"].f[0], r)
        pairs(act, 1, pair1)
        phase_end(act, "att1")
        for k in range(KC):
            act.activation(mix1_hl[0][:, k, :], mix1[:, k, :], ACT.Copy).then_inc(mx_hi, 1)
        phase_end(act, "split1")
        for m in range(8):
            linear_hi("out1", m)
        phase_end(act, "out1")

        E = e_sem
        n3 = NORM_AT["n3"]
        norm_act_first(act, n3)
        for k in range(KC):
            act.wait_ge(nr[4], n3 * 8 + k + 1)
            if k >= 2:
                act.wait_ge(E["xt"], k - 1)
            a, b, scale, shift = cols_moe(k)[0]
            act.activation(xfm[k % 2][:, :], fn_z[k % 2][:, :], ACT.Identity, bias=shift, scale=scale
                           ).then_inc(nr[5], 1)
            if k >= 1:
                turned_hi(act, k - 1)
        turned_hi(act, KC - 1)
        act.wait_ge(E["exps"], 1)
        act.activation(wexp[:, :, :], wexp[:, :, :], ACT.Exp).then_inc(E["exps"], 1)
        phase_end(act, "router")

        def gathered_hi(g, ks):
            for k in ks:
                act.wait_ge(E["gmt"], g * 8 + (k + 1))
                act.activation(xg[0][:, k, :], bank(5 + k % 3, 0, BLK), ACT.Copy).then_inc(E["xhi"], 1)

        def item(it, N):
            J = N // P

            def turned_selection():
                act.wait_ge(E["sc"], it + 1)
                for j in range(J):
                    ins = act.activation(gt[:, j, :], bank(7 - j, 0, 512), ACT.Copy)
                ins.then_inc(E["gt"], 1)

            ffn_act(act, "exp", it * EX_CHUNKS, it, AT["exp"], N, turned_selection)
            act.wait_ge(used[2], it * EX_CHUNKS + (AT["exp"].u[2] + USED0 + EX_CHUNKS))
            for part in range(2):
                yb, j, a, b = y_part(J, part)
                act.activation(yx[part][:, a:b], yb, ACT.Copy, scale=wslot[:, j:j + 1]).then_inc(E["yx"], 1)
                act.wait_ge(E["yx"], it * 2 + (part + 1))
                act.activation(yhl[0][:, j, a:b], yx[part][:, a:b], ACT.Copy).then_inc(E["yhi"], 1)
                gathered_hi(it + 1, range(2) if part == 0 else range(2, KC))

        gathered_hi(0, range(KC))
        items(act, item)
        phase_end(act, "moe")

    @block.vector
    def _(dve):
        for r in range(3):
            dve.sem_inc(lo_ready[r], LO0)
        dve.sem_inc(m_row, 3)
        for n in ("mlp", "exp"):
            dve.sem_inc(ff[n]["hm"], 2)
        dve.sem_inc(y_evac, 1)
        dve.sem_inc(e_sem["scev"], 4)
        dve.sem_inc(e_sem["xlo"], 3)
        dve.sem_inc(lin_evac, 4)
        chain = [0]

        def link(ins):
            chain[0] += 1
            ins.then_inc(s_chain, 1)
            dve.wait_ge(s_chain, chain[0])

        dve.wait_ge(s_const, 16 * len(CONSTS))

        dve.tensor_scalar(scond_hl[:, :, :], ones[:, :].unsqueeze(1).broadcast_to([P, KC, P]), 0.0, None, ALU.mult
                          ).then_inc(s_scond, 1)
        dve.wait_ge(s_scond, 3)
        dve.tensor_tensor(scond_hl[:, :, 2:4], scond[:, :, :], scond_hl[:, :, 0:2].bitcast(F32), ALU.subtract
                          ).then_inc(s_scond, 1)

        def mods_dve(l):
            u = AT[("md0", "md1")[l]].u
            with dve.Fori(0, N_MOD // 4) as j:
                for n in range(12):
                    t, r = n // 3, n % 3
                    lo_unit(dve, r, (raw + [raw_m])[t][:, r, :], U, j * 4 + (u[r] + t + 1))
            dve.wait_ge(m_tr, 12 * l + 12)
            link(dve.tensor_tensor(mods[:, l, :, :], bank(7, 0, 96).rearrange("p (s c) -> p s c", c=2),
                                   bmod[:, l, :].unsqueeze(2).broadcast_to([P, 48, 2]), ALU.add))
            for n in range(2):
                sc = mods[:, l, (3 * n + 1) * KC:(3 * n + 2) * KC, :]
                link(dve.tensor_scalar(nsc[:, l, n, :, :], sc, 1.0, None, ALU.add))
                link(dve.tensor_tensor(nsc[:, l, n, :, :], nsc[:, l, n, :, :],
                                       ng[:, l, n, :].unsqueeze(2).broadcast_to([P, KC, 2]), ALU.mult))

        mods_dve(0)
        phase_end(dve, "mods0")
        norm_dve(dve, 0, res_all, T, rstd, zb, xfb, lambda k: xn[0][:, k, :], lambda k: xn[1][:, k, :])
        phase_end(dve, "norm0")

        def linear_lo(nm, m):
            r, t = m % 3, m // 3
            lo_unit(dve, r, raw[t][:, r, :], U, AT[nm].u[r] + t + 1)

        for m in range(6):
            linear_lo("ain", m)
        phase_end(dve, "ain")
        SQ, SUM, STD, X, HI, LO, KR = c_sem
        link(dve.scalar_tensor_tensor(out=l0_x[64:128, 2, :], in0=plat[64:128, 3, :], scalar=gcol[64:128, 5:6],
                                      in1=ktab[64:128, :], op0=ALU.mult, op1=ALU.mult))
        link(dve.scalar_tensor_tensor(out=krope[64:128, :], in0=plat[0:64, 3, :], scalar=gcol[0:64, 5:6],
                                      in1=ktab[0:64, :], op0=ALU.mult, op1=ALU.mult))
        link(dve.tensor_tensor(krope[64:128, :], krope[64:128, :], l0_x[64:128, 2, :], ALU.add))
        link(dve.tensor_copy(krope[0:64, :], krope[64:128, :]))
        link(dve.tensor_scalar(csg[:, :], qtab[:, :], gcol[:, 3:4], None, ALU.mult))
        dve.wait_ge(STD, 1)
        link(dve.reciprocal(l0_rs[:, 0, :], l0_rs[:, 0, :]))
        dve.wait_ge(STD, 2)
        link(dve.reciprocal(l0_rs[:, 1, :], l0_rs[:, 1, :]))
        vals = ((plat[:, 0, :], 0, l0_rs[:, 0, :], l0_t[:, 0, :], cq[0][:, 0, :], cq[1][:, 0, :]),
                (plat[:, 1, :], 1, l0_rs[:, 0, :], l0_t[:, 1, :], cq[0][:, 1, :], cq[1][:, 1, :]),
                (plat[:, 2, :], 2, l0_rs[:, 1, :], l0_x[:, 1, :], ckv[0][:, :], ckv[1][:, :]))
        for src, g, rs, dst, hi, lo in vals:
            dve.scalar_tensor_tensor(out=dst, in0=src, scalar=gcol[:, g:g + 1], in1=rs, op0=ALU.mult,
                                     op1=ALU.mult).then_inc(X, 1)
        for n, (src, g, rs, dst, hi, lo) in enumerate(vals):
            dve.wait_ge(HI, n + 1)
            dve.tensor_tensor(lo, dst, hi.bitcast(F32), ALU.subtract).then_inc(LO, 1)
        phase_end(dve, "lat")
        fa, fahi, falo, fev, fhi, flo = f_sem
        for ch in range(2):
            dve.wait_ge(fhi, ch + 1)
            dve.tensor_tensor(ff_hl[1][:, ch, :], plat[:, 4 + ch, :], ff_hl[0][:, ch, :].bitcast(F32),
                              ALU.subtract).then_inc(flo, 1)
        for m in range(3):
            linear_lo("four", m)
        for tb in range(6):
            dve.wait_ge(fahi, tb + 1)
            dve.tensor_tensor(four_a[1][:, tb, :], slot(tb % 4, 0, 512), four_a[0][:, tb, :].bitcast(F32),
                              ALU.subtract).then_inc(falo, 1)
        for m in range(3, 6):
            linear_lo("four", m)
        phase_end(dve, "four")

        def pair0(i, nxt):
            A, u = a_sem[0], AT["pr0"].u

            def queries(h):
                dve.wait_ge(A["qsq"], i * 2 + (h + 1))
                dve.tensor_tensor(qx0[h][:, :], slot(h, 0, T), csg[:, :], ALU.mult).then_inc(A["qx"], 1)

            dve.wait_ge(A["o"], i * 12 + NPT[0])
            queries(0)
            dve.wait_ge(A["kstd"], i + 1)
            dve.reciprocal(rk0[:, :], rk0[:, :]).then_inc(A["rk"], 1)
            dve.wait_ge(A["rk"], i + 1)
            for h in range(2):
                rows = slice(h * 64, h * 64 + 64)
                if h:
                    dve.wait_ge(A["kr"], i + 1)
                dve.scalar_tensor_tensor(out=kx0[h][0:64, :], in0=slot(2, 0, T)[rows, :], scalar=gcol[rows, 4:5],
                                         in1=rk0[rows, :], op0=ALU.mult, op1=ALU.mult).then_inc(A["kx"], 1)
                if h == 0:
                    dve.tensor_tensor(kx0[0][64:128, :], krope[0:64, :], rk0[0:64, :], ALU.mult).then_inc(A["kd"], 1)
            queries(1)
            for h in range(2):
                dve.wait_ge(A["khi"], i * 2 + (h + 1))
                dve.tensor_tensor(k0[1][:, h, :], kx0[h][:, :], k0[0][:, h, :].bitcast(F32), ALU.subtract
                                  ).then_inc(A["klo"], 1)
            dve.wait_ge(A["rqs"], i + 1)
            dve.reciprocal(rq[:, 0:12], rqs[:, 0:12]).then_inc(A["rqd"], 1)
            dve.wait_ge(A["vhi"], i + 1)
            dve.tensor_tensor(v0[1][:, :, :], slot(3, 0, T), v0[0][:, :, :].bitcast(F32), ALU.subtract
                              ).then_inc(A["vlo"], 1)
            dve.wait_ge(A["rqd"], i + 1)
            att_dve(dve, 0, i, nxt)

        for r in ROLE_ORDER:
            pair_lo(dve, 0, 0, 0, 0, r)
        pairs(dve, 0, pair0)
        phase_end(dve, "att0")
        for k in range(KC):
            dve.wait_ge(mx_hi, k + 1)
            dve.tensor_tensor(mix0_hl[1][:, k, :], mix0[:, k, :], mix0_hl[0][:, k, :].bitcast(F32), ALU.subtract)
        phase_end(dve, "split0")

        def out_dve(nm, l, parts):
            for m in range(3):
                linear_lo(nm, m)
            for m in range(8):
                dve.wait_ge(used[m % 3], USED0 + AT[nm].u[m % 3] + m // 3 + 1)
                for n, (a, b, s) in enumerate(parts):
                    ins = dve.scalar_tensor_tensor(out=res[:, m, a:b], in0=slot(m % 4, a, b),
                                                   scalar=mods[:, l, 2 * KC + m, s:s + 1], in1=res[:, m, a:b],
                                                   op0=ALU.mult, op1=ALU.add)
                ins.then_inc(lin_evac, 1)
                if m + 3 < 8:
                    linear_lo(nm, m + 3)

        out_dve("out0", 0, [(0, SEQ, 0), (SEQ, T, 1)])
        for dst, src in ((nscr, nsc[:, 0, 1, :, :]), (nshr, mods[:, 0, 3 * KC:4 * KC, :]),
                         (ngtr, mods[:, 0, 5 * KC:6 * KC, :])):
            for t, s in enumerate((0, 0, 1)):
                dve.tensor_copy(dst[:, :, t], src[:, :, s])
        phase_end(dve, "out0")
        with dve.Fori(0, 3) as t:
            norm_dve(dve, t + NORM_AT["n1"], res_block(t), BLK, fn_rs, fn_z, fn_x,
                     lambda k: xg[0][:, k, :], lambda k: xg[1][:, k, :])
            ffn_dve(dve, "mlp", t * 22, AT["mlp"], BLK)
            ffn_dve(dve, "mlp", t * 22 + 11, AT["mlp"], BLK)
            dve.wait_ge(used[2], t * 22 + (AT["mlp"].u[2] + USED0 + 22))
            for m in range(KC):
                ins = dve.scalar_tensor_tensor(out=res[:, m, ds(t * BLK, BLK)], in0=bank(m // 2, (m % 2) * BLK, BLK),
                                               scalar=ngtr[:, m, ds(t, 1)], in1=res[:, m, ds(t * BLK, BLK)],
                                               op0=ALU.mult, op1=ALU.add)
            ins.then_inc(y_evac, 1)
        phase_end(dve, "mlp")
        mods_dve(1)
        phase_end(dve, "mods1")
        norm_dve(dve, NORM_AT["n2"], res_all, T, rstd, zb, xfb, lambda k: xn[0][:, k, :], lambda k: xn[1][:, k, :])
        phase_end(dve, "norm1")
        for t in q1:
            dve.tensor_copy(t[64:128, 0, :].rearrange("p (a b) -> p a b", b=64),
                            ones64[64:128, 0:64].unsqueeze(1).broadcast_to([64, 8, 64]))
            ins = dve.tensor_copy(t[0:64, 1, :].rearrange("p (a b) -> p a b", b=64),
                                  ones64[0:64, 64:128].unsqueeze(1).broadcast_to([64, 8, 64]))
        ins.then_inc(s_zero, 1)

        dve.wait_ge(s_zero, 1)

        def pair1(i, nxt):
            A, u = a_sem[1], AT["pr1"].u
            dve.wait_ge(A["o"], i * 8 + NPT[1])
            dve.wait_ge(A["kstd"], i + 1)
            dve.reciprocal(rk1[:, :], rk1[:, :]).then_inc(A["rk"], 1)
            dve.wait_ge(A["rk"], i + 1)
            dve.scalar_tensor_tensor(out=rk1[:, :], in0=slot(1, 0, T), scalar=gcol[:, 7:8], in1=rk1[:, :],
                                     op0=ALU.mult, op1=ALU.mult).then_inc(A["kx"], 1)
            dve.wait_ge(A["qsq"], i + 1)
            dve.tensor_scalar(qx1[:, :], slot(2, 0, SEQ), gcol[:, 6:7], None, ALU.mult).then_inc(A["qx"], 1)
            dve.wait_ge(A["khi"], i + 1)
            dve.tensor_tensor(k1[1][:, :], rk1[:, :], k1[0][:, :].bitcast(F32), ALU.subtract).then_inc(A["klo"], 1)
            dve.wait_ge(A["qhi"], i + 1)
            for h in range(2):
                rows = slice(h * 64, h * 64 + 64)
                ins = dve.tensor_tensor(q1[1][rows, h, :], qx1[rows, :], q1[0][rows, h, :].bitcast(F32), ALU.subtract)
            ins.then_inc(A["qlo"], 1)
            dve.wait_ge(A["rqs"], i + 1)
            dve.reciprocal(rq[:, 0:8], rqs[:, 0:8]).then_inc(A["rqd"], 1)
            dve.wait_ge(A["vhi"], i + 1)
            dve.tensor_tensor(v1[1][:, :, :], slot(3, 0, T), v1[0][:, :, :].bitcast(F32), ALU.subtract
                              ).then_inc(A["vlo"], 1)
            dve.wait_ge(A["rqd"], i + 1)
            att_dve(dve, 1, i, nxt)

        for r in ROLE_ORDER:
            pair_lo(dve, 1, 0, 0, 0, r)
        pairs(dve, 1, pair1)
        phase_end(dve, "att1")
        for k in range(KC):
            dve.wait_ge(mx_hi, KC + k + 1)
            dve.tensor_tensor(mix1_hl[1][:, k, :], mix1[:, k, :], mix1_hl[0][:, k, :].bitcast(F32), ALU.subtract)
        phase_end(dve, "split1")
        out_dve("out1", 1, [(0, SEQ, 0)])
        phase_end(dve, "out1")

        E = e_sem
        n3 = NORM_AT["n3"]
        dve.wait_ge(nr[2], n3 + 1)
        link(dve.reciprocal(fn_rs[:, :], fn_rs[:, :]))

        def turned_lo(k):
            dve.wait_ge(E["xthi"], k + 1)
            dve.tensor_tensor(xt[1][:, :, k * P:(k + 1) * P], bank(k % 4, 0, 512).rearrange("p (b c) -> p b c", b=4),
                              xt[0][:, :, k * P:(k + 1) * P].bitcast(F32), ALU.subtract).then_inc(E["xtlo"], 1)

        for k in range(KC):
            if k >= 2:
                dve.wait_ge(nr[5], n3 * 8 + k - 1)
            dve.tensor_tensor(fn_z[k % 2][:, :], res_lat(k), fn_rs[:, :], ALU.mult).then_inc(nr[4], 1)
            if k >= 2:
                turned_lo(k - 2)
        turned_lo(KC - 2)
        turned_lo(KC - 1)

        dve.wait_ge(E["xt"], KC)
        dve.wait_ge(E["in"], 16 * len(E_CONSTS))
        link(dve.tensor_copy(lg[:, :, :], bank(5, 0, 32).rearrange("p (b e) -> p b e", b=4)))
        for b in range(4):
            mine = lg[:, b, :].unsqueeze(2).broadcast_to([P, 8, 8])
            other = lg[:, b, :].unsqueeze(1).broadcast_to([P, 8, 8])
            link(dve.tensor_tensor(r64[:, b, :, :], other, mine, ALU.is_gt))
            link(dve.tensor_tensor(r64b[:, b, :, :], other, mine, ALU.is_equal))
            link(dve.tensor_tensor(r64b[:, b, :, :], r64b[:, b, :, :], ltj[:, :, :], ALU.mult))
        link(dve.tensor_tensor(r64[:, :, :, :], r64[:, :, :, :], r64b[:, :, :, :], ALU.add))
        link(dve.reduce_sum(rank[:, :, :], r64[:, :, :, :], AX))
        dve.tensor_scalar(seltok[:, :, :], rank[:, :, :], 2.0, None, ALU.is_lt).then_inc(E["sel"], 1)
        link(dve.reduce_max(lmax[:, :], lg[:, :, :], AX))
        dve.tensor_tensor(wexp[:, :, :], lg[:, :, :], lmax[:, :].unsqueeze(2).broadcast_to([P, 4, 8]),
                          ALU.subtract).then_inc(E["exps"], 1)
        dve.wait_ge(E["exps"], 2)
        dve.wait_ge(E["sel"], 1)
        link(dve.tensor_tensor(wexp[:, :, :], wexp[:, :, :], seltok[:, :, :], ALU.mult))
        link(dve.reduce_sum(wsum[:, :], wexp[:, :, :], AX))
        link(dve.reciprocal(wsum[:, :], wsum[:, :]))
        link(dve.tensor_tensor(comb[:, :, :], wexp[:, :, :], wsum[:, :].unsqueeze(2).broadcast_to([P, 4, 8]), ALU.mult))
        dve.wait_ge(E["pos"], 1)
        link(dve.tensor_scalar(posn[:, :, :], bank(4, 0, 32).rearrange("p (b e) -> p b e", b=4), 1.0, None, ALU.add))
        link(dve.tensor_tensor(posn[:, :, :], posn[:, :, :], seltok[:, :, :], ALU.mult))
        link(dve.tensor_copy(cnts[:, :], bank(4, 32, 8)))
        link(dve.tensor_scalar(nit[:, :], cnts[:, :], 0.0, None, ALU.is_gt))
        link(dve.tensor_scalar(endi[:, :], cnts[:, :], float(BLK), None, ALU.is_gt))
        link(dve.tensor_tensor(nit[:, :], nit[:, :], endi[:, :], ALU.add))
        link(dve.tensor_tensor(r64[:, 0, :, :], nit[:, :].unsqueeze(1).broadcast_to([P, 8, 8]), ltj[:, :, :], ALU.mult))
        link(dve.reduce_sum(starti[:, :], r64[:, 0, :, :], AX))
        link(dve.tensor_tensor(endi[:, :], starti[:, :], nit[:, :], ALU.add))
        inum = itn[:, :].unsqueeze(2).broadcast_to([P, COLS, 8])
        link(dve.tensor_tensor(oneh[:, :, :], inum, starti[:, :].unsqueeze(1).broadcast_to([P, COLS, 8]), ALU.is_ge))
        link(dve.tensor_tensor(oneb[:, :, :], inum, endi[:, :].unsqueeze(1).broadcast_to([P, COLS, 8]), ALU.is_lt))
        link(dve.tensor_tensor(oneh[:, :, :], oneh[:, :, :], oneb[:, :, :], ALU.mult))

        def of_item(dst, vec):
            link(dve.tensor_tensor(oneb[:, :, :], oneh[:, :, :], vec[:, :].unsqueeze(1).broadcast_to([P, COLS, 8]),
                                   ALU.mult))
            link(dve.reduce_sum(dst, oneb[:, :, :], AX))

        link(dve.reduce_sum(tab[:, 0, :], oneh[:, :, :], AX))
        of_item(tab[:, 1, :], erow)
        of_item(tab[:, 3, :], starti)
        of_item(tab[:, 4, :], cnts)
        link(dve.tensor_tensor(tab[:, 5, :], itn[:, :], tab[:, 3, :], ALU.subtract))
        link(dve.tensor_scalar(tab[:, 5, :], tab[:, 5, :], float(BLK), None, ALU.mult))
        link(dve.tensor_tensor(tab[:, 4, :], tab[:, 4, :], tab[:, 5, :], ALU.subtract))
        link(dve.tensor_scalar(tab[:, 2, :], tab[:, 4, :], float(P), None, ALU.is_gt))
        link(dve.tensor_copy(tabi[:, :, :], tab[:, :, :]))
        for b in range(4):
            link(dve.tensor_tensor(oneb[:, :, :], oneh[:, :, :],
                                   posn[:, b, :].unsqueeze(1).broadcast_to([P, COLS, 8]), ALU.mult))
            link(dve.reduce_sum(posi[:, b, :], oneb[:, :, :], AX))
            link(dve.tensor_tensor(oneb[:, :, :], oneh[:, :, :],
                                   comb[:, b, :].unsqueeze(1).broadcast_to([P, COLS, 8]), ALU.mult))
            link(dve.reduce_sum(cmbi[:, b, :], oneb[:, :, :], AX))
            link(dve.tensor_tensor(posi[:, b, :], posi[:, b, :], tab[:, 5, :], ALU.subtract))
            link(dve.tensor_scalar(posi[:, b, :], posi[:, b, :], -1.0, None, ALU.add))
        dve.tensor_copy(cmbi[:, 0, 0:1], cmbi[:, 0, 0:1]).then_inc(E["tab"], 1)
        phase_end(dve, "router")

        def selection(g):
            for b in range(4):
                ins = dve.tensor_scalar(gm[:, b, :], iot[:, :], posi[:, b, ds(g, 1)], None, ALU.is_equal)
            ins.then_inc(E["gm"], 1)

        def gathered_lo(g, ks):
            for k in ks:
                dve.wait_ge(E["xhi"], g * 8 + (k + 1))
                dve.tensor_tensor(xg[1][:, k, :], bank(5 + k % 3, 0, BLK), xg[0][:, k, :].bitcast(F32),
                                  ALU.subtract).then_inc(E["xlo"], 1)

        def item(it, N):
            J = N // P

            def next_selection():
                dve.wait_ge(E["ws"], it + 1)
                dve.tensor_copy(wslot[:, 0:J], bank(5, 0, J)).then_inc(E["wsc"], 1)
                dve.wait_ge(E["sc"], it + 1)
                selection(it + 1)

            ffn_dve(dve, "exp", it * EX_CHUNKS, AT["exp"], N, next_selection)
            for part in range(2):
                yb, j, a, b = y_part(J, part)
                dve.wait_ge(E["yhi"], it * 2 + (part + 1))
                dve.tensor_tensor(yhl[1][:, j, a:b], yx[part][:, a:b], yhl[0][:, j, a:b].bitcast(F32), ALU.subtract
                                  ).then_inc(E["ylo"], 1)
                gathered_lo(it + 1, range(2) if part == 0 else range(2, KC))
            for m in range(KC):
                dve.wait_ge(E["sct"], it * 8 + (m + 1))
                dve.scalar_tensor_tensor(out=res[:, m, 0:SEQ], in0=bank(m % 4, 0, 512),
                                         scalar=mods[:, 1, 5 * KC + m, 0:1], in1=res[:, m, 0:SEQ],
                                         op0=ALU.mult, op1=ALU.add).then_inc(E["scev"], 1)

        selection(0)
        gathered_lo(0, range(KC))
        items(dve, item)
        phase_end(dve, "moe")

    @block.gpsimd
    def _(pool):
        for name in ("mods0", "norm0", "ain", "lat", "four"):
            phase_end(pool, name)

        def pair0(i, nxt):
            A = a_sem[0]

            def queries_lo(h):
                pool.wait_ge(A["qhi"], i * 2 + (h + 1))
                pool.tensor_tensor(q0[1][:, h, :], qx0[h][:, :], q0[0][:, h, :].bitcast(F32), ALU.subtract
                                   ).then_inc(A["qlo"], 1)

            queries_lo(0)
            pool.wait_ge(A["rk"], i + 1)
            pool.tensor_tensor(kx0[1][:, :], krope[:, :], rk0[:, :], ALU.mult).then_inc(A["kr"], 1)
            queries_lo(1)
            att_pool(pool, 0, i)

        pairs(pool, 0, pair0)
        for name in ("att0", "split0", "out0", "mlp", "mods1", "norm1"):
            phase_end(pool, name)
        pairs(pool, 1, lambda i, nxt: att_pool(pool, 1, i))
        for name in ("att1", "split1", "out1", "router", "moe"):
            phase_end(pool, name)


def _unit(w, m):
    k = w.shape[0] // P
    return w[:, m * P:(m + 1) * P].reshape(k, P, P).transpose(1, 0, 2).reshape(P, k * P)


def _swap(n):
    return np.arange(n) ^ 1


def layout(x, c, ctx, c_ctx, w_mod, b_mod, norm_g, a_w_in, a_g_cq, a_g_ckv, a_w_uq, a_w_ukv, a_g_q, a_g_k,
           a_w_out, f_w_gate, f_w_up, f_w_down, c_w_in, c_g_q, c_g_k, c_rpb, c_w_out, m_w_router, m_w_gate,
           m_w_up, m_w_down):
    f = np.float32
    order = np.arange(SEQ).reshape(ROWS, GRID_W).T.reshape(-1)
    a = {}
    tok = np.concatenate([x[0][order], ctx[0]], axis=0)
    a["xT"] = tok.T.reshape(KC, P, T).transpose(1, 0, 2)
    a["cond"] = np.stack([c[0], c_ctx], axis=-1).reshape(KC, P, 2).transpose(1, 0, 2)
    a["bmod"] = b_mod.reshape(2, 48, P).transpose(2, 0, 1)
    a["ng"] = norm_g.reshape(2, 2, KC, P).transpose(3, 0, 1, 2)
    g = np.ones((P, 8), f)
    sw = _swap(A_ROPE)
    g[:, 0:2] = a_g_cq[0].reshape(2, P).T
    g[:, 2] = a_g_ckv[0]
    g[0:96, 3] = a_g_q[0]
    g[96:128, 3] = a_g_q[0][64:][sw]
    g[:, 4] = np.tile(a_g_k[0][0:64], 2)
    rope = a_g_k[0][64:]
    g[:, 5] = np.concatenate([rope[sw], rope[sw], rope, rope])
    g[:, 6] = np.tile(c_g_q[0], 2)
    g[:, 7] = np.tile(c_g_k[0], 2)
    a["gcol"] = g
    a["ident"] = np.eye(P, dtype=f)
    a["ones"] = np.ones((P, P), f)
    o96 = np.zeros((P, P), f)
    o96[0:96] = 1
    a["ones96"] = o96
    o64 = np.zeros((P, P), f)
    o64[0:64, 0:64] = 1
    o64[64:, 64:] = 1
    a["ones64"] = o64
    onr = np.zeros((P, P), f)
    onr[64:96] = 1
    a["onesr"] = onr
    h2 = np.zeros((P, 2), f)
    h2[0:64, 0] = 1
    h2[64:, 1] = 1
    a["half2"] = h2
    hl = np.zeros((P, 2), f)
    hl[[0, 2], 0] = 1
    hl[[1, 3], 1] = 1
    a["hl_sum"] = hl
    a["eps"] = np.tile(np.array([EPS, A_QK * EPS, DH * EPS], f), (P, 1))
    inv = 10000.0 ** (-np.arange(8, dtype=np.float64) / 8)
    ang = np.concatenate([(order // GRID_W)[:, None] * inv, (order % GRID_W)[:, None] * inv], axis=1)
    cos = np.ones((A_ROPE, T))
    sin = np.zeros((A_ROPE, T))
    cos[:, 0:SEQ] = np.repeat(np.cos(ang).T, 2, axis=0)
    sin[:, 0:SEQ] = np.repeat(np.sin(ang).T, 2, axis=0) * np.tile([-1.0, 1.0], 16)[:, None]
    a["qtab"] = np.concatenate([np.ones((64, T)), cos, sin]).astype(f)
    a["ktab"] = np.concatenate([sin, sin, cos, cos]).astype(f)
    rows = []

    def triple(*units):
        t = np.zeros((P, 3, U), f)
        for n, u in enumerate(units):
            t[:, n, 0:u.shape[1]] = u
        rows.append(t.reshape(P, 3 * U))

    def triples(units):
        for n in range(0, len(units), 3):
            triple(*units[n:n + 3])

    def mod_units(w):
        return [np.concatenate([w[(2 * q + h) * P:(2 * q + h + 1) * P, b * 512:(b + 1) * 512] for h in range(2)],
                               axis=1) for b in range(12) for q in range(4)]

    triples(mod_units(w_mod[0]))
    w = a_w_in[0]
    kr = w[:, 384:416]
    w_in = np.concatenate([w[:, 0:384], kr[:, sw], kr[:, sw], kr, kr, w[:, 416:672]], axis=1)
    triples([_unit(w_in, m) for m in range(6)])
    uq = a_w_uq[0].reshape(A_QR, A_HEADS, A_QK)
    uq = np.concatenate([uq, uq[:, :, 64:][:, :, sw]], axis=2)
    ukv = a_w_ukv[0].reshape(A_KVR, A_HEADS, 128)
    for i in range(PAIRS0):
        q = np.concatenate([uq[kc * P:(kc + 1) * P, 2 * i + h] for h in range(2) for kc in range(2)], axis=1)
        ka, kb = ukv[:, 2 * i, 0:64], ukv[:, 2 * i + 1, 0:64]
        v = np.concatenate([ukv[:, 2 * i, 64:], ukv[:, 2 * i + 1, 64:]], axis=1)
        triple(q, np.concatenate([ka, kb], axis=1), v)
    triples([_unit(a_w_out[0], m) for m in range(8)])
    for cch in range(FF_CHUNKS):
        triple(_unit(f_w_gate[0], cch), _unit(f_w_up[0], cch), f_w_down[0][cch * P:(cch + 1) * P])
    triples(mod_units(w_mod[1]))
    for i in range(PAIRS1):
        triple(*[_unit(c_w_in[0][:, s * D:(s + 1) * D], i) for s in range(3)])
    triples([_unit(c_w_out[0], m) for m in range(8)])
    for e in range(EXPERTS):
        for cch in range(EX_CHUNKS):
            triple(_unit(m_w_gate[0, e], cch), _unit(m_w_up[0, e], cch), m_w_down[0, e][cch * P:(cch + 1) * P])
    a["stream"] = np.stack(rows)
    assert a["stream"].shape[0] == TR_END
    units = []
    ch = 2 * np.pi * np.outer(np.arange(64), np.arange(64)) / 64
    z = np.zeros((64, 64))
    units.append(np.concatenate([np.block([[fn(ch), z], [z, fn(ch)]]) for fn in (np.cos, np.sin)], axis=1))
    th = 2 * np.pi * ((order[:, None] * order[None, :]) % SEQ) / SEQ
    for fn, sign in ((np.cos, 1), (np.sin, -1)):
        m = sign * fn(th) / np.sqrt(SEQ * 64)
        for u in range(2):
            units.append(np.concatenate([m[(2 * u + kb) * P:(2 * u + kb + 1) * P] for kb in range(2)], axis=1))
    tc = np.arange(CTX)
    th = 2 * np.pi * ((tc[:, None] * tc[None, :]) % CTX) / CTX
    units.append(np.concatenate([s * fn(th)[kb * P:(kb + 1) * P] / np.sqrt(CTX * 64)
                                 for fn, s in ((np.cos, 1), (np.sin, -1)) for kb in range(2)], axis=1))
    fo = np.zeros((2, P, 3, U), f)
    for n, u in enumerate(units):
        fo[n // 3, :, n % 3, 0:u.shape[1]] = u
    a["fourier"] = fo.reshape(2, P, 3 * U)
    qi = np.arange(P)
    tiles = []
    for b, kbs in ((0, (0, 1)), (1, (0, 1, 2)), (3, (2, 3))):
        cq_, rq_ = b * 16 + qi // 8, qi % 8
        start = np.clip(cq_ - WIN_C // 2, 0, GRID_W - WIN_C)
        for kb in kbs:
            ck, rk = kb * 16 + qi // 8, qi % 8
            inside = (ck[None, :] >= start[:, None]) & (ck[None, :] < start[:, None] + WIN_C)
            dr = rk[None, :] - rq_[:, None] + WIN_R - 1
            dc = np.clip(ck[None, :] - cq_[:, None] + WIN_C - 1, 0, 2 * WIN_C - 2)
            t = c_rpb[0][:, dr, dc]
            tiles.append(np.where(inside[None], t, f(-BIG)))
    bias = np.concatenate(tiles, axis=2)
    a["bias"] = bias.reshape(PAIRS1, 2, P, BIAS_TILES * P).transpose(0, 2, 1, 3)
    a["wr"] = m_w_router[0].reshape(KC, P, 8).transpose(1, 0, 2)
    a["tri"] = np.triu(np.ones((P, P), f), 1)
    a["iot"] = np.tile(np.arange(BLK, dtype=f), (P, 1))
    a["ltj"] = np.tile(np.tril(np.ones((8, 8), f), -1), (P, 1, 1))
    a["itn"] = np.tile(np.arange(COLS, dtype=f), (P, 1))
    a["erow"] = np.tile(TR_EXP + EX_CHUNKS * np.arange(8, dtype=f), (P, 1))
    return {k: np.ascontiguousarray(v, dtype=f) for k, v in a.items()}, order


def kernel(**inputs):
    import concourse.bacc as bacc
    from concourse.bass_utils import run_bass_kernel_spmd as run

    arrays, order = layout(**{k: np.asarray(v) for k, v in inputs.items()})
    nc = bacc.Bacc("TRN2", target_bir_lowering=False, num_devices=1)
    io = {n: nc.dram_tensor(n, v.shape, F32, kind="ExternalInput").ap() for n, v in arrays.items()}
    io["out"] = nc.dram_tensor("out", (P, KC, SEQ), F32, kind="ExternalOutput").ap()
    build(nc, io)
    r = run(nc, [arrays], core_ids=[0])
    y = r.results[0]["out"].transpose(1, 0, 2).reshape(D, SEQ)
    out = np.empty((1, SEQ, D), y.dtype)
    out[0, order] = y.T
    return out
```

```python
from contextlib import ExitStack

import numpy as np
import concourse.bass as bass
from concourse import mybir

F32 = mybir.dt.float32
F32R = mybir.dt.float32r
I32 = mybir.dt.int32
ALU = mybir.AluOpType
ACT = mybir.ActivationFunctionType
AX = mybir.AxisListType.X
ds = bass.ds

P = 128
D = 1024
KC = D // P
SEQ, CTX = 512, 256
T = SEQ + CTX
GRID_W, ROWS = 64, 8
EPS = 1e-6
A_HEADS, A_NOPE, A_ROPE, A_QK = 12, 64, 32, 96
A_QR, A_KVR = 256, 128
PAIRS0, PAIRS1 = A_HEADS // 2, 8
DH = 64
WIN_R, WIN_C = 8, 16
FF_CHUNKS = 22
EXPERTS, EX_CHUNKS = 8, 11
U = 1024
BIG = 1e30
BLK = 256
ITEMS = (2 * SEQ + EXPERTS * (BLK - 1)) // BLK
COLS = ITEMS + 1
BIAS_TILES = 7
LOCAL = [([0, 1], 0), ([0, 1, 2], 2), ([1, 2, 3], 2), ([2, 3], 5)]

TR_MOD0, N_MOD = 0, 16
TR_AIN = TR_MOD0 + N_MOD
TR_PAIR0 = TR_AIN + 2
TR_OUT0 = TR_PAIR0 + PAIRS0
TR_MLP = TR_OUT0 + 3
TR_MOD1 = TR_MLP + FF_CHUNKS
TR_PAIR1 = TR_MOD1 + N_MOD
TR_OUT1 = TR_PAIR1 + PAIRS1
TR_EXP = TR_OUT1 + 3
TR_END = TR_EXP + EXPERTS * EX_CHUNKS


LO0, USED0 = 4, 1
NPT = [2, 2]


class At:

    def __init__(self, units, fills):
        self.u, self.f = units, fills


def plan():
    at, u, f = {}, [0, 0, 0], [0, 0, 0, 0]
    for name, nu, nf in (("md0", (N_MOD,) * 3, (4, 4, 4, 4)), ("ain", (2, 2, 2), (1, 1, 0, 0)),
                         ("four", (2, 2, 2), (1, 1, 0, 0)),
                         ("pr0", (PAIRS0,) * 3, (PAIRS0 // 2, PAIRS0 // 2, 0, 0)),
                         ("out0", (3, 3, 2), (1, 1, 1, 0)),
                         ("mlp", (3 * FF_CHUNKS,) * 3, (18, 18, 18, 12)),
                         ("md1", (N_MOD,) * 3, (4, 4, 4, 4)),
                         ("pr1", (PAIRS1,) * 3, (PAIRS1 // 2, PAIRS1 // 2, 0, 0)),
                         ("out1", (3, 3, 2), (1, 1, 1, 0)), ("exp", (0, 0, 0), (0, 0, 0, 0))):
        at[name] = At(list(u), list(f))
        u = [x + y for x, y in zip(u, nu)]
        f = [x + y for x, y in zip(f, nf)]
    return at


AT = plan()
NORM_AT = {"n0": 0, "n1": 1, "n2": 4, "n3": 5}


def build(nc, io):
    with ExitStack() as ctx:
        _build(nc, io, ctx)


def _build(nc, io, ctx):
    def sem(name):
        return ctx.enter_context(nc.semaphore(name))

    at = [(nc.sbuf_base + 63) // 64 * 64]

    def place(name, shape, dt, offset=None):
        size = int(np.prod(shape[1:])) * 4
        off = at[0] if offset is None else offset
        t = nc.alloc_sbuf_tensor_at(name, shape, dt, offset=off)
        if offset is None:
            at[0] += (size + 31) // 32 * 32
        return t

    class Area:
        def __init__(self, start):
            self.at = start

        def __call__(self, name, shape, dt=F32):
            t = place(name, shape, dt, self.at)
            self.at += (int(np.prod(shape[1:])) * 4 + 31) // 32 * 32
            return t

        def pair(self, name, shape):
            return self(name + "_hi", shape, F32R), self(name + "_lo", shape, F32R)

    ones = place("ones", [P, P], F32)
    ident = place("ident", [P, P], F32)
    ones96 = place("ones96", [P, P], F32)
    ones64 = place("ones64", [P, P], F32)
    onesr = place("onesr", [P, P], F32)
    half2 = place("half2", [P, 2], F32)
    eps = place("eps", [P, 3], F32)
    cond = place("cond", [P, KC, 2], F32)
    scond = place("scond", [P, KC, 2], F32)
    scond_hl = place("scond_hl", [P, KC, P], F32R)
    hl_sum = place("hl_sum", [P, 2], F32)
    bmod = place("bmod", [P, 2, 48], F32)
    mods = place("mods", [P, 2, 48, 2], F32)
    ng = place("ng", [P, 2, 2, KC], F32)
    nsc = place("nsc", [P, 2, 2, KC, 2], F32)
    gcol = place("gcol", [P, 8], F32)
    res = place("res", [P, KC, T], F32)
    raw = [place(f"raw{s}", [P, 3, U], F32) for s in range(3)]
    whi = [place(f"w_hi{r}", [P, U], F32R) for r in range(3)]
    wlo = [place(f"w_lo{r}", [P, U], F32R) for r in range(3)]
    x_start = at[0]
    att_start = x_start + 2 * KC * T * 4

    PS = ctx.enter_context(nc.psum_tensor("ps", [P, 8, 512], F32))

    def slot(s, a=0, b=1024):
        return PS[:, 2 * s:2 * s + 2, :].rearrange("p a b -> p (a b)")[:, a:b]

    def bank(b, a, n):
        return PS[:, b, a:a + n]

    ax = Area(x_start)
    xn = ax.pair("xn", [P, KC, T])
    an = Area(att_start)
    sqb = [an(f"sqb{i}", [P, T]) for i in range(2)]
    rstd = an("rstd", [P, T])
    zb = [an(f"zb{i}", [P, T]) for i in range(2)]
    xfb = [an(f"xfb{i}", [P, T]) for i in range(2)]

    am = Area(x_start)
    raw_m = am("raw3", [P, 3, U])
    mrow = [am(f"mrow{i}", [P, 512]) for i in range(3)]

    ap_ = Area(att_start)
    plat = ap_("plat", [P, 6, T])
    ff_hl = ap_.pair("four_in", [P, 2, T])
    four_a = ap_.pair("four_a", [P, 6, 512])
    a0 = Area(x_start)
    cq = a0.pair("cq", [P, 2, T])
    ckv = a0.pair("ckv", [P, T])
    krope = a0("krope", [P, T])
    csg = a0("csg", [P, T])
    mix0 = a0("mix0", [P, KC, T])
    a0t = Area(att_start + 6 * T * 4)
    l0_sq = a0t("l0_sq", [P, 2, T])
    l0_rs = a0t("l0_rs", [P, 2, T])
    qtab = a0t("qtab", [P, T])
    ktab = a0t("ktab", [P, T])
    l0_t = a0t("l0_t", [P, 2, T])
    l0_x = a0t("l0_x", [P, 3, T])

    b0 = Area(att_start)
    q0 = b0.pair("q0", [P, 2, T])
    k0 = b0.pair("k0", [P, 2, T])
    v0 = b0.pair("v0", [P, 6, P])
    p0 = [b0(f"p0_{i}", [P, T]) for i in range(2)]
    pt0_start = b0.at
    pt0 = [b0.pair(f"pt0_{i}", [P, T]) for i in range(2)]
    b0.at = pt0_start
    qx0 = [b0(f"qx0_{h}", [P, T]) for h in range(2)]
    rk0 = b0("rk0", [P, T])
    kx0_0 = b0("kx0_0", [P, T])
    b0.at = pt0_start + 4 * T * 4
    sqq0 = b0("sqq0", [P, 2, T])
    sqk0 = b0("sqk0", [P, T])
    sqr = b0("sqr", [P, T])
    kx0 = [kx0_0, b0("kx0_1", [P, T])]
    b1 = Area(att_start)
    mix1 = b1("mix1", [P, KC, SEQ])
    q1 = b1.pair("q1", [P, 2, SEQ])
    k1 = b1.pair("k1", [P, T])
    v1 = b1.pair("v1", [P, 6, P])
    p1 = [b1(f"p1_{i}", [P, 5 * P]) for i in range(2)]
    biasb = b1("biasb", [P, 2, BIAS_TILES * P])
    pt1_start = b1.at
    pt1 = [b1.pair(f"pt1_{i}", [P, 5 * P]) for i in range(2)]
    b1.at = pt1_start
    qx1 = b1("qx1", [P, SEQ])
    rk1 = b1("rk1", [P, T])
    b1.at = pt1_start + 4 * 5 * P * 4
    sq1 = b1("sq1", [P, T])
    sqq1 = b1("sqq1", [P, SEQ])
    asm = Area(max(b0.at, b1.at))
    rq = asm("rq", [P, 12])
    rqs = asm("rqs", [P, 12])
    nmax = asm("nmax", [P, 8])
    nneg = asm("nneg", [P, 8])
    rsum = asm("rsum", [P, 8])
    rinv = asm("rinv", [P, 8])
    o0 = Area(att_start)
    mix0_hl = o0.pair("mix0s", [P, KC, T])
    o1 = Area(x_start)
    mix1_hl = o1.pair("mix1s", [P, KC, SEQ])
    f_ = Area(x_start)
    xg = f_.pair("xg", [P, KC, BLK])
    hx = [f_(f"hx{i}", [P, BLK]) for i in range(3)]
    sg = [f_(f"sg{i}", [P, BLK]) for i in range(3)]
    hb = [f_.pair(f"hb{i}", [P, BLK]) for i in range(3)]
    fn_sq = [f_(f"fn_sq{i}", [P, SEQ]) for i in range(2)]
    fn_rs = f_("fn_rs", [P, SEQ])
    fn_z = [f_(f"fn_z{i}", [P, SEQ]) for i in range(2)]
    fn_x = [f_(f"fn_x{i}", [P, BLK]) for i in range(2)]
    nscr = f_("nscr", [P, KC, 3])
    nshr = f_("nshr", [P, KC, 3])
    ngtr = f_("ngtr", [P, KC, 3])
    xs = place("xs", [P, KC, BLK], F32, f_.at)
    raw_f = place("raw_f", [P, 3, U], F32, f_.at + KC * BLK * 4)
    xt = f_.pair("xt", [P, 4, D])
    xfm = [f_(f"xfm{i}", [P, SEQ]) for i in range(2)]
    wr = f_("wr", [P, KC, 8])
    tri = f_("tri", [P, P])
    iot = f_("iot", [P, BLK])
    ltj = f_("ltj", [P, 8, 8])
    itn = f_("itn", [P, COLS])
    lg = f_("lg", [P, 4, 8])
    r64 = f_("r64", [P, 4, 8, 8])
    r64b = f_("r64b", [P, 4, 8, 8])
    rank = f_("rank", [P, 4, 8])
    seltok = f_("seltok", [P, 4, 8])
    lmax = f_("lmax", [P, 4])
    wexp = f_("wexp", [P, 4, 8])
    comb = f_("comb", [P, 4, 8])
    wsum = f_("wsum", [P, 4])
    posn = f_("posn", [P, 4, 8])
    cnts = f_("cnts", [P, 8])
    nit = f_("nit", [P, 8])
    endi = f_("endi", [P, 8])
    starti = f_("starti", [P, 8])
    erow = f_("erow", [P, 8])
    oneh = f_("oneh", [P, COLS, 8])
    oneb = f_("oneb", [P, COLS, 8])
    tab = f_("tab", [P, 6, COLS])
    tabi = f_("tabi", [P, 6, COLS], I32)
    posi = f_("posi", [P, 4, COLS])
    cmbi = f_("cmbi", [P, 4, COLS])
    gm = f_("gm", [P, 4, BLK], F32R)
    gt = f_("gt", [P, 2, SEQ], F32R)
    wslot = f_("wslot", [P, 2])
    yx = [f_(f"yx{i}", [P, D]) for i in range(2)]
    yhl = f_.pair("yhl", [P, 2, D])
    assert max(f_.at, asm.at, o0.at, ap_.at, a0t.at) <= nc.sbuf_usable_end, (
        f_.at, asm.at, o0.at, ap_.at, a0t.at, nc.sbuf_usable_end)

    s_const = sem("s_const")
    s_fetch = sem("s_fetch")
    s_scond = sem("s_scond")
    s_phase = sem("s_phase")
    s_chain = sem("s_chain")
    m_blk = sem("m_blk")
    m_row = sem("m_row")
    m_tr = sem("m_tr")
    raw_full = [sem(f"raw_full{i}") for i in range(4)]
    hi_ready = [sem(f"hi_ready{i}") for i in range(3)]
    lo_ready = [sem(f"lo_ready{i}") for i in range(3)]
    used = [sem(f"used{i}") for i in range(3)]
    nr = [sem(f"norm_{w}") for w in ("sq", "sum", "std", "rstd", "z", "x", "hi", "lo")]
    lin_evac = sem("lin_evac")
    mx_hi = sem("mix_hi")
    c_sem = [sem(f"c_{n}") for n in ("sq", "sum", "std", "x", "hi", "lo", "kr")]
    f_sem = [sem(f"f_{n}") for n in ("a", "ahi", "alo", "evac", "fhi", "flo")]
    at_names = ("qsq", "qx", "qhi", "qlo", "ksq", "ks", "kstd", "rk", "kx", "khi", "klo",
                "vhi", "vlo", "rq", "rqs", "rqd", "qm", "kr", "kd", "vc", "vt",
                "s", "max", "neg", "exp", "inv", "p", "t", "hi", "lo", "o", "oev")
    a_sem = [{n: sem(f"a{l}_{n}") for n in at_names} for l in range(2)]
    a_sem[1]["sadd"], a_sem[1]["bias"] = sem("a1_sadd"), sem("a1_bias")
    s_zero = sem("s_zero")
    ff = {n: {w: sem(f"{n}_{w}") for w in ("hm", "sg", "hh", "h")} for n in ("mlp", "exp")}
    y_evac = sem("y_evac")
    e_sem = {n: sem(f"e_{n}") for n in
             ("in", "xt", "xthi", "xtlo", "sel", "exps", "pos", "tab", "gm", "gmt", "gt", "xhi", "xlo",
              "sc", "ws", "wsc", "yx", "yhi", "ylo", "sct", "scev")}
    s_out = sem("s_out")

    block = ctx.enter_context(nc.Block())

    def mm3(pe, out, w, x, first, last, skip=False):
        for n, (a, b) in enumerate(((0, 0), (0, 1), (1, 0))):
            ins = pe.matmul(out, w[a], x[b], start=first and n == 0, stop=last and n == 2,
                            skip_group_check=skip)
        return ins

    def pieces(n):
        return [(0, n)] if n <= 512 else [(0, 512), (512, n)]

    PHASES = {n: k for k, n in enumerate((
        "mods0", "norm0", "ain", "lat", "four", "att0", "split0", "out0", "mlp", "mods1", "norm1",
        "att1", "split1", "out1", "router", "moe"))}

    def phase_end(eng, name):
        eng.drain().then_inc(s_phase, 1)
        eng.wait_ge(s_phase, 4 * (PHASES[name] + 1))

    def three(row):
        return row.rearrange("p (r u) -> p r u", r=3)

    def all_of(t):
        return t[tuple(slice(None) for _ in t.shape)]

    CONSTS = (("ident", ident), ("ones", ones), ("cond", cond), ("bmod", bmod), ("ng", ng), ("gcol", gcol),
              ("ones96", ones96), ("ones64", ones64), ("onesr", onesr), ("half2", half2),
              ("hl_sum", hl_sum), ("eps", eps), ("qtab", qtab),
              ("ktab", ktab), ("xT", res))
    E_CONSTS = (("wr", wr), ("tri", tri), ("iot", iot), ("ltj", ltj), ("itn", itn), ("erow", erow))

    @block.sync
    def _(sp):
        for name, tile in CONSTS:
            sp.dma_start(all_of(tile), io[name]).then_inc(s_const, 16)
        W = io["stream"]

        def slots_split(units):
            for r in range(3):
                sp.wait_ge(lo_ready[r], LO0 + units[r])

        def load(row, s, done):
            sp.dma_start(raw[s][:, :, :], three(row)).then_inc(done[s], 16)

        def load_dyn(row, s, slots):
            sp.dma_start(slots[s][:, :, :], W[ds(row, 1)].rearrange("a p (r u) -> p (a r) u", r=3)
                         ).then_inc(raw_full[s], 16)

        def load_mods(l):
            row0 = (TR_MOD0, TR_MOD1)[l]
            u = AT[("md0", "md1")[l]].u
            with sp.Fori(0, N_MOD // 4) as j:
                for s in range(4):
                    sp.wait_ge(lo_ready[2], j * 4 + (LO0 + u[2] + s - 3))
                    sp.sem_inc(s_fetch, 1)
                    load_dyn(j * 4 + (row0 + s), s, raw + [raw_m])

        def load_list(name, rows, slots):
            base = AT[name].u
            for n, row in enumerate(rows):
                if n >= slots:
                    for r in range(3):
                        sp.wait_ge(lo_ready[r], LO0 + base[r] + n - slots + 1)
                load(row, n % slots, raw_full)

        load_mods(0)
        slots_split(AT["ain"].u)
        load_list("ain", [W[TR_AIN + n] for n in range(2)], 2)
        slots_split(AT["four"].u)
        load_list("four", [io["fourier"][n] for n in range(2)], 2)
        slots_split(AT["pr0"].u)
        load_list("pr0", [W[TR_PAIR0 + n] for n in range(PAIRS0)], 2)
        slots_split(AT["out0"].u)
        load_list("out0", [W[TR_OUT0 + n] for n in range(3)], 3)
        slots_split(AT["mlp"].u)

        def load_chunks(g0, row0, base, slots):
            n = len(slots)
            for c in range(EX_CHUNKS):
                last = c - n if c >= n else max(x for x in range(EX_CHUNKS) if x % n == c) - EX_CHUNKS
                sp.wait_ge(lo_ready[2], g0 + (base[2] + LO0 + last + 1))
                sp.sem_inc(s_fetch, 1)
                load_dyn(row0 + c, c % n, slots)

        sp.wait_ge(s_phase, 4 * (PHASES["out0"] + 1))
        with sp.Fori(0, 3) as t:
            with sp.Fori(0, 2) as half:
                load_chunks(t * 22 + half * 11, half * 11 + TR_MLP, AT["mlp"].u, raw + [raw_f])
        slots_split(AT["md1"].u)
        sp.wait_ge(s_phase, 4 * (PHASES["mlp"] + 1))
        load_mods(1)
        slots_split(AT["pr1"].u)
        base = AT["pr1"].u
        for n in range(PAIRS1):
            if n >= 2:
                for r in range(3):
                    sp.wait_ge(lo_ready[r], LO0 + base[r] + n - 1)
            load(W[TR_PAIR1 + n], n % 2, raw_full)
            if n == 0:
                sp.wait_ge(s_phase, 4 * (PHASES["norm1"] + 1))
            else:
                sp.wait_ge(a_sem[1]["sadd"], 16 * n)
            sp.dma_start(biasb[:, :, :], io["bias"][n]).then_inc(a_sem[1]["bias"], 16)
        slots_split(AT["out1"].u)
        load_list("out1", [W[TR_OUT1 + n] for n in range(3)], 3)
        sp.wait_ge(s_phase, 4 * (PHASES["out1"] + 1))
        for name, tile in E_CONSTS:
            sp.dma_start(all_of(tile), io[name]).then_inc(e_sem["in"], 16)
        sp.wait_ge(e_sem["tab"], 1)
        slots_split(AT["exp"].u)
        with sp.Fori(0, ITEMS) as it:
            live = sp.value_load(tabi[0:1, 0, ds(it, 1)], min_val=0, max_val=1)
            row = sp.value_load(tabi[0:1, 1, ds(it, 1)], min_val=0, max_val=TR_END - EX_CHUNKS)
            with sp.If(live > 0):
                load_chunks(it * EX_CHUNKS, row, AT["exp"].u, raw)
        sp.wait_ge(s_phase, 4 * (PHASES["moe"] + 1))
        sp.dma_start(io["out"], res[:, :, 0:SEQ]).then_inc(s_out, 16)
        sp.wait_ge(s_out, 16)

    def hi_unit(act, r, src, cols, s, n_full, n_used):
        act.wait_ge(raw_full[s], n_full * 16)
        act.wait_ge(used[r], n_used + USED0)
        act.activation(whi[r][:, 0:cols], src, ACT.Copy).then_inc(hi_ready[r], 1)

    def lo_unit(dve, r, src, cols, n):
        dve.wait_ge(hi_ready[r], n)
        dve.tensor_tensor(wlo[r][:, 0:cols], src, whi[r][:, 0:cols].bitcast(F32), ALU.subtract
                          ).then_inc(lo_ready[r], 1)

    def norm_pe(pe, nb, n, sq):
        SQ, SUM = nr[:2]
        for k in range(KC):
            pe.wait_ge(SQ, nb * 8 + (k + 1))
            for a, b in pieces(n):
                ins = pe.matmul(slot(3, a, b), ones[:, :], sq[k % 2][:, a:b], start=k == 0, stop=k == KC - 1)
            ins.then_inc(SUM, 1)

    def norm_act(act, nb, src, n, sq, rs, z, xf, cols, dst_hi, weights=lambda: None):
        SQ, SUM, STD, RSTD, Z, X, HI, LO = nr
        for k in range(KC):
            if k >= 2:
                act.wait_ge(SUM, nb * 8 + (k - 1))
            act.activation(sq[k % 2][:, 0:n], src(k), ACT.Square).then_inc(SQ, 1)
        weights()
        act.wait_ge(SUM, nb * 8 + 8)
        act.activation(rs[:, 0:n], slot(3, 0, n), ACT.Sqrt, bias=eps[:, 0:1], scale=1.0 / D).then_inc(STD, 1)
        for k in range(KC):
            act.wait_ge(Z, nb * 8 + (k + 1))
            if dst_hi is None:
                if k >= 2:
                    act.wait_ge(e_sem["xt"], k - 1)
            elif k >= 2:
                act.wait_ge(LO, nb * 8 + (k - 1))
            parts = cols(k)
            for a, b, scale, shift in parts:
                ins = act.activation(xf[k % 2][:, a:b], z[k % 2][:, a:b], ACT.Identity, bias=shift, scale=scale)
            ins.then_inc(X, 1)
            if dst_hi is not None:
                act.wait_ge(X, nb * 8 + (k + 1))
                act.activation(dst_hi(k), xf[k % 2][:, 0:n], ACT.Copy).then_inc(HI, 1)

    def norm_dve(dve, nb, src, n, rs, z, xf, dst_hi, dst_lo, weights=lambda: None):
        SQ, SUM, STD, RSTD, Z, X, HI, LO = nr
        weights()
        dve.wait_ge(STD, nb + 1)
        dve.reciprocal(rs[:, 0:n], rs[:, 0:n]).then_inc(RSTD, 1)
        dve.wait_ge(RSTD, nb + 1)
        for k in range(KC + 1):
            if k < KC:
                if k >= 2:
                    dve.wait_ge(X, nb * 8 + (k - 1))
                dve.tensor_tensor(z[k % 2][:, 0:n], src(k), rs[:, 0:n], ALU.mult).then_inc(Z, 1)
            if k >= 1 and dst_lo is not None:
                dve.wait_ge(HI, nb * 8 + k)
                dve.tensor_tensor(dst_lo(k - 1), xf[(k - 1) % 2][:, 0:n], dst_hi(k - 1).bitcast(F32),
                                  ALU.subtract).then_inc(LO, 1)

    def res_all(k):
        return res[:, k, :]

    def res_lat(k):
        return res[:, k, 0:SEQ]

    def res_block(t):
        return lambda k: res[:, k, ds(t * BLK, BLK)]

    def cols_all(l):
        return lambda k: [(0, SEQ, nsc[:, l, 0, k, 0:1], mods[:, l, k, 0:1]),
                          (SEQ, T, nsc[:, l, 0, k, 1:2], mods[:, l, k, 1:2])]

    def cols_block(t):
        return lambda k: [(0, BLK, nscr[:, k, ds(t, 1)], nshr[:, k, ds(t, 1)])]

    def cols_moe(k):
        return [(0, SEQ, nsc[:, 1, 1, k, 0:1], mods[:, 1, 3 * KC + k, 0:1])]

    def ffn_pe(pe, nm, g0, base, N, ymode, y_start, y_stop, y_wait, x_wait=lambda k: None, between=lambda c: None,
               more=False, joined=False):
        F = ff[nm]

        def down(c):
            pe.wait_ge(lo_ready[2], g0 + (base[2] + c + LO0 + 1))
            pe.wait_ge(F["h"], g0 + (c + 1))
            if c == 0:
                y_wait()
            first, last = y_start and c == 0, y_stop and c == EX_CHUNKS - 1
            hc = hb[c % 3 if c >= 0 else (EX_CHUNKS - 1) % 3]
            if ymode == "channels":
                h = [t[:, 0:N] for t in hc]
                for m in range(KC):
                    o = bank(m // 2, (m % 2) * BLK, N)
                    for n, (a, b) in enumerate(((0, 0), (0, 1), (1, 0))):
                        ins = pe.matmul(o, (whi, wlo)[a][2][:, m * P:(m + 1) * P], h[b],
                                        start=first and n == 0 and m % 2 == 0, stop=last and n == 2,
                                        skip_group_check=True)
            else:
                for j in range(N // P):
                    for q in range(2):
                        ins = mm3(pe, bank(2 * j + q, 0, 512), [t[:, j * P:(j + 1) * P] for t in hc],
                                  [t[2][:, q * 512:(q + 1) * 512] for t in (whi, wlo)], first, last)
            ins.then_inc(used[2], 1)

        for c in range(EX_CHUNKS):
            pe.wait_ge(F["hm"], g0 + (c + 1))
            for r in range(2):
                pe.wait_ge(lo_ready[r], g0 + (base[r] + c + LO0 + 1))
                n = BLK if c == 0 else N
                for k in range(KC):
                    if c == 0 and r == 0:
                        x_wait(k)
                    ins = mm3(pe, bank(4 + c % 3, r * BLK, n),
                              [t[r][:, k * P:(k + 1) * P] for t in (whi, wlo)],
                              [t[:, k, 0:n] for t in xg], k == 0, k == KC - 1)
                ins.then_inc(used[r], 1)
            if c or joined:
                down(c - 1)
            between(c)
        if not more:
            down(EX_CHUNKS - 1)

    def ffn_act(act, nm, g0, item, at_, N, between=lambda c: None, slots=raw, first=True,
                ahead=False):
        F = ff[nm]
        n = len(slots)
        per_item = [len(range(s, EX_CHUNKS, n)) for s in range(n)]

        def hi(r, c, later=0):
            hi_unit(act, r, slots[c % n][:, r, :], U, c % n,
                    item * per_item[c % n] + (at_.f[c % n] + later * per_item[c % n] + c // n + 1),
                    g0 + (at_.u[r] + later * EX_CHUNKS + c))

        if first:
            hi(0, 0)
            hi(1, 0)
        for c in range(EX_CHUNKS):
            if c < EX_CHUNKS - 1:
                hi(0, c + 1)
            elif ahead:
                hi(0, 0, 1)
            act.wait_ge(used[1], g0 + (at_.u[1] + c + 1 + USED0))
            act.activation(sg[c % 3][:, 0:N], bank(4 + c % 3, 0, N), ACT.Silu).then_inc(F["sg"], 1)
            if c < EX_CHUNKS - 1:
                hi(1, c + 1)
            elif ahead:
                hi(1, 0, 1)
            act.wait_ge(F["hm"], g0 + (c + 3))
            act.activation(hb[c % 3][0][:, 0:N], hx[c % 3][:, 0:N], ACT.Copy).then_inc(F["hh"], 1)
            hi(2, c)
            between(c)

    def ffn_dve(dve, nm, g0, at_, N, mid=lambda c: None, between=lambda c: None, slots=raw, first=True,
                ahead=False):
        F = ff[nm]

        def lo(r, c, later=0):
            lo_unit(dve, r, slots[c % len(slots)][:, r, :], U, g0 + (at_.u[r] + later * EX_CHUNKS + c + 1))

        if first:
            lo(0, 0)
            lo(1, 0)
        for c in range(EX_CHUNKS):
            if c < EX_CHUNKS - 1:
                lo(0, c + 1)
            elif ahead:
                lo(0, 0, 1)
            dve.wait_ge(F["sg"], g0 + (c + 1))
            dve.tensor_tensor(hx[c % 3][:, 0:N], sg[c % 3][:, 0:N], bank(4 + c % 3, BLK, N), ALU.mult
                              ).then_inc(F["hm"], 1)
            mid(c)
            if c < EX_CHUNKS - 1:
                lo(1, c + 1)
            elif ahead:
                lo(1, 0, 1)
            dve.wait_ge(F["hh"], g0 + (c + 1))
            dve.tensor_tensor(hb[c % 3][1][:, 0:N], hx[c % 3][:, 0:N], hb[c % 3][0][:, 0:N].bitcast(F32),
                              ALU.subtract).then_inc(F["h"], 1)
            lo(2, c)
            between(c)

    def next_norm_pe(pe, nb, g):
        g -= 1
        if 0 <= g < KC:
            pe.wait_ge(nr[0], nb * 8 + (g + 1))
            pe.matmul(bank(7, 0, BLK), ones[:, :], fn_sq[g % 2][:, 0:BLK], start=g == 0, stop=g == KC - 1
                      ).then_inc(nr[1], 1)

    def next_norm_act(act, nb, t, g):
        k = g - 11
        if g < KC:
            if g >= 2:
                act.wait_ge(nr[1], nb * 8 + (g - 1))
            act.activation(fn_sq[g % 2][:, 0:BLK], res_block(t)(g), ACT.Square).then_inc(nr[0], 1)
        elif g == 9:
            act.wait_ge(nr[1], nb * 8 + 8)
            act.activation(fn_rs[:, 0:BLK], bank(7, 0, BLK), ACT.Sqrt, bias=eps[:, 0:1], scale=1.0 / D
                           ).then_inc(nr[2], 1)
        elif 0 <= k < KC:
            act.wait_ge(nr[4], nb * 8 + (k + 1))
            a, b, scale, shift = cols_block(t)(k)[0]
            act.activation(xs[:, k, :], fn_z[k % 2][:, 0:BLK], ACT.Identity, bias=shift, scale=scale
                           ).then_inc(nr[5], 1)

    def next_norm_dve(dve, nb, t, g):
        k = g - 11
        if g == 10:
            dve.wait_ge(nr[2], nb + 1)
            dve.reciprocal(fn_rs[:, 0:BLK], fn_rs[:, 0:BLK]).then_inc(nr[3], 1)
        elif 0 <= k < KC:
            if k == 0:
                dve.wait_ge(nr[3], nb + 1)
            if k >= 2:
                dve.wait_ge(nr[5], nb * 8 + (k - 1))
            dve.tensor_tensor(fn_z[k % 2][:, 0:BLK], res_block(t)(k), fn_rs[:, 0:BLK], ALU.mult).then_inc(nr[4], 1)

    UNITS = [[512, 128, 128], [U, U, U]]
    ROLE_ORDER = (1, 0, 2)

    def pair_hi(act, l, i, s, fills, r):
        n = UNITS[l][r]
        hi_unit(act, r, raw[s][:, r, 0:n], n, s, fills + 1, i + AT[("pr0", "pr1")[l]].u[r])

    def pair_lo(dve, l, i, s, fills, r):
        n = UNITS[l][r]
        lo_unit(dve, r, raw[s][:, r, 0:n], n, i + (AT[("pr0", "pr1")[l]].u[r] + 1))

    def steps_of(l):
        out = []
        for h in range(2):
            if l == 0:
                out += [(h, b, list(range(6)), 512, None) for b in range(4)]
                out += [(h, b, [4, 5], 0, None) for b in (4, 5)]
            else:
                out += [(h, b, LOCAL[b][0] + [4, 5], len(LOCAL[b][0]) * P, LOCAL[b][1]) for b in range(4)]
        return out

    def operands(l):
        return (q0, k0, v0, p0, pt0, mix0) if l == 0 else (q1, k1, v1, p1, pt1, mix1)

    def att_pe(pe, l, i, before, nxt, head):
        A = a_sem[l]
        q, k, v, p, pt, mix = operands(l)
        steps = steps_of(l)
        J = len(steps)

        def scores(j):
            h, b, tiles, nl, _ = steps[j]
            pe.wait_ge(A["oev"], i * J + (j + 1))
            s = j % 4
            qs = [t[:, h, b * P:(b + 1) * P] for t in q]
            if l == 0:
                runs = [(0, 0, 512), (512, 512, T)] if b < 4 else [(512, 512, T)]
                kk = [[t[:, h, x:y] for t in k] for _, x, y in runs]
            else:
                runs = [(0, tiles[0] * P, tiles[0] * P + nl), (512, 512, T)]
                kk = [[t[:, x:y] for t in k] for _, x, y in runs]
            for (o, x, y), ks in zip(runs, kk):
                ins = mm3(pe, slot(s, o, o + y - x), qs, ks, True, True)
            ins.then_inc(A["s"], 1)

        def turn(j):
            tiles = steps[j][2]
            pe.wait_ge(A["p"], i * J + (j + 1))
            for n in range(len(tiles)):
                ins = pe.transpose(slot(j % 4, n * P, (n + 1) * P), p[j % 2][:, n * P:(n + 1) * P], ident[:, :])
            ins.then_inc(A["t"], 1)

        def values(j):
            tiles = steps[j][2]
            pe.wait_ge(A["lo"], i * J + (j + 1))
            for n, kt in enumerate(tiles):
                ins = mm3(pe, slot(j % 4, 768, 896), [t[:, kt, :] for t in v],
                          [t[:, n * P:(n + 1) * P] for t in pt[j % len(pt)]], n == 0, n == len(tiles) - 1)
            ins.then_inc(A["o"], 1)

        for j in range(J + 3):
            if j < J:
                before(j)
                scores(j)
            if j == J + 1 and nxt:
                head(nxt[0])
            if j >= 3:
                values(j - 3)
            if 1 <= j <= J:
                turn(j - 1)

    def att_act(act, l, i, nxt, head):
        A = a_sem[l]
        q, k, v, p, pt, mix = operands(l)
        steps = steps_of(l)
        J = len(steps)
        npt = NPT[l]

        def out(j):
            h, b = steps[j][:2]
            act.wait_ge(A["o"], i * J + (j + 1 + npt))
            act.activation(mix[h * 64:(h + 1) * 64, ds(i, 1), b * P:(b + 1) * P],
                           slot(j % 4, 768, 896)[h * 64:(h + 1) * 64, :], ACT.Copy).then_inc(A["oev"], 1)

        for j in range(J + 3):
            if j == J + 2 and nxt:
                head(nxt[0])
            if j >= 3:
                out(j - 3)
            if j < J:
                h, b, tiles, nl, _ = steps[j]
                n = len(tiles) * P
                c = j % 8
                act.wait_ge(A["neg"], i * J + (j + 1))
                act.wait_ge(A["t"], i * J + (j + 1))
                if l == 0:
                    a = 0 if b < 4 else 512
                    act.activation(p[j % 2][:, 0:n], slot(j % 4, a, a + n), ACT.Exp, bias=nneg[:, c:c + 1],
                                   scale=rq[:, h * 6 + b:h * 6 + b + 1], accum_out=rsum[:, c:c + 1]
                                   ).then_inc(A["exp"], 1)
                else:
                    act.activation(p[j % 2][:, 0:n], p[j % 2][:, 0:n], ACT.Exp, bias=nneg[:, c:c + 1],
                                   accum_out=rsum[:, c:c + 1]).then_inc(A["exp"], 1)
            if 1 <= j <= J:
                n = len(steps[j - 1][2]) * P
                act.wait_ge(A["t"], i * J + (j + 2))
                act.wait_ge(A["o"], i * J + j)
                act.activation(pt[(j - 1) % npt][0][:, 0:n], slot((j - 1) % 4, 0, n), ACT.Copy
                               ).then_inc(A["hi"], 1)
            if l == 0 and 3 <= j <= 3 + 2 and nxt:
                pair_hi(act, l, *nxt, ROLE_ORDER[j - 3])
            if l == 1 and j in (1, 3, 5) and nxt:
                pair_hi(act, l, *nxt, ROLE_ORDER[j // 2])

    def att_dve(dve, l, i, nxt):
        A = a_sem[l]
        q, k, v, p, pt, mix = operands(l)
        steps = steps_of(l)
        J = len(steps)
        npt = NPT[l]

        def turned(j):
            n = len(steps[j][2]) * P
            dve.wait_ge(A["hi"], i * J + (j + 1))
            dve.tensor_tensor(pt[j % npt][1][:, 0:n], slot(j % 4, 0, n), pt[j % npt][0][:, 0:n].bitcast(F32),
                              ALU.subtract).then_inc(A["lo"], 1)

        for j in range(J + 2):
            if j < J:
                h, b, tiles, nl, bt = steps[j]
                n = len(tiles) * P
                c = j % 8
                dve.wait_ge(A["s"], i * J + (j + 1))
                if l == 0:
                    a = 0 if b < 4 else 512
                    dve.reduce_max(nmax[:, c:c + 1], slot(j % 4, a, a + n), AX).then_inc(A["max"], 1)
                    dve.wait_ge(A["max"], i * J + (j + 1))
                    dve.tensor_scalar(nneg[:, c:c + 1], nmax[:, c:c + 1], rq[:, h * 6 + b:h * 6 + b + 1], -1.0,
                                      ALU.mult, ALU.mult).then_inc(A["neg"], 1)
                else:
                    if j == 0:
                        dve.wait_ge(A["bias"], i * 16 + 16)
                    dve.wait_ge(A["t"], i * J + (j + 1))
                    r = rq[:, b * 2 + h:b * 2 + h + 1]
                    dve.scalar_tensor_tensor(out=p[j % 2][:, 0:nl], in0=slot(j % 4, 0, nl), scalar=r,
                                             in1=biasb[:, h, bt * P:bt * P + nl], op0=ALU.mult, op1=ALU.add
                                             ).then_inc(A["sadd"], 1)
                    dve.tensor_scalar(p[j % 2][:, nl:n], slot(j % 4, 512, T), r, None, ALU.mult
                                      ).then_inc(A["sadd"], 1)
                    dve.wait_ge(A["sadd"], i * (2 * J) + (2 * j + 2))
                    dve.reduce_max(nmax[:, c:c + 1], p[j % 2][:, 0:n], AX).then_inc(A["max"], 1)
                    dve.wait_ge(A["max"], i * J + (j + 1))
                    dve.tensor_scalar(nneg[:, c:c + 1], nmax[:, c:c + 1], -1.0, None, ALU.mult
                                      ).then_inc(A["neg"], 1)
            if j >= 2:
                turned(j - 2)
            if j < J:
                dve.wait_ge(A["exp"], i * J + (j + 1))
                dve.reciprocal(rinv[:, c:c + 1], rsum[:, c:c + 1]).then_inc(A["inv"], 1)
            if l == 0 and 3 <= j <= 3 + 2 and nxt:
                pair_lo(dve, l, *nxt, ROLE_ORDER[j - 3])

    def att_pool(pool, l, i, nxt):
        A = a_sem[l]
        p = operands(l)[3]
        steps = steps_of(l)
        J = len(steps)
        for j in range(J):
            n = len(steps[j][2]) * P
            pool.wait_ge(A["inv"], i * J + (j + 1))
            pool.tensor_tensor(p[j % 2][:, 0:n], p[j % 2][:, 0:n],
                               rinv[:, j % 8:j % 8 + 1].broadcast_to([P, n]), ALU.mult).then_inc(A["p"], 1)
            if l == 1 and j >= 2 and nxt:
                ni, s, _ = nxt
                r, cols = ROLE_ORDER[j // 2 - 1], U // 2
                x = slice(j % 2 * cols, (j % 2 + 1) * cols)
                pool.wait_ge(hi_ready[r], ni + (AT["pr1"].u[r] + 1))
                ins = pool.tensor_tensor(wlo[r][:, x], raw[s][:, r, x], whi[r][:, x].bitcast(F32), ALU.subtract)
                if j % 2:
                    ins.then_inc(lo_ready[r], 1)

    def pairs(eng, l, body):
        name, n = ("pr0", PAIRS0) if l == 0 else ("pr1", PAIRS1)
        f = AT[name].f
        with eng.Fori(0, n // 2 - 1) as ii:
            body(ii * 2, (ii * 2 + 1, 1, ii + f[1]))
            body(ii * 2 + 1, (ii * 2 + 2, 0, ii + (f[0] + 1)))
        body(n - 2, (n - 1, 1, n // 2 - 1 + f[1]))
        body(n - 1, None)

    def items(eng, body):
        eng.wait_ge(e_sem["tab"], 1)
        with eng.Fori(0, ITEMS) as it:
            live = eng.value_load(tabi[0:1, 0, ds(it, 1)], min_val=0, max_val=1)
            wide = eng.value_load(tabi[0:1, 2, ds(it, 1)], min_val=0, max_val=1)
            with eng.If(live > 0):
                with eng.If(wide > 0):
                    body(it, BLK)
                with eng.Else():
                    body(it, P)
                eng.nop()
            eng.nop()

    def norm_act_first(act, nb):
        for k in range(KC):
            if k >= 2:
                act.wait_ge(nr[1], nb * 8 + (k - 1))
            act.activation(fn_sq[k % 2][:, :], res_lat(k), ACT.Square).then_inc(nr[0], 1)
        act.wait_ge(nr[1], nb * 8 + 8)
        act.activation(fn_rs[:, :], slot(3, 0, SEQ), ACT.Sqrt, bias=eps[:, 0:1], scale=1.0 / D).then_inc(nr[2], 1)

    def turned_hi(act, k):
        act.wait_ge(e_sem["xt"], k + 1)
        act.activation(xt[0][:, :, k * P:(k + 1) * P], bank(k % 4, 0, 512).rearrange("p (b c) -> p b c", b=4),
                       ACT.Copy).then_inc(e_sem["xthi"], 1)

    def y_part(J, part):
        if J == 2:
            return slot(part), part, 0, D
        return bank(part, 0, 512), 0, part * 512, part * 512 + 512

    GATHER_BANKS = (6, 7, 4)

    @block.tensor
    def _(pe):
        pe.sem_inc(m_tr, 3)
        for r in range(3):
            pe.sem_inc(used[r], USED0)
        for l in range(2):
            pe.sem_inc(a_sem[l]["t"], 2)
            pe.sem_inc(a_sem[l]["o"], NPT[l])

        def mods_pe(l):
            u = AT[("md0", "md1")[l]].u

            def turn_block(j, b):
                pe.wait_ge(m_row, j * 3 + (12 * l + b + 1 + 3))
                for n in range(4):
                    ins = pe.matmul(PS[:, 7, ds(j * 24 + (b * 4 + n) * 2, 2)], mrow[b][:, n * P:(n + 1) * P],
                                    hl_sum[:, :], start=True, stop=True)
                ins.then_inc(m_tr, 1)

            def turn(j, first=False):
                for b in range(3):
                    pe.wait_ge(m_row, j * 3 + (12 * l + b + 1))
                    for q in range(4):
                        t, r = (b * 4 + q) // 3, (b * 4 + q) % 3
                        pe.wait_ge(lo_ready[r], j * 4 + (LO0 + u[r] + t + 1))
                        for h in range(2):
                            for w in (whi, wlo):
                                ins = pe.matmul(bank(b, 0, 512), scond_hl[:, 2 * q + h, :],
                                                w[r][:, h * 512:(h + 1) * 512], start=q == 0 and h == 0 and w is whi,
                                                stop=q == 3 and h == 1 and w is wlo)
                        ins.then_inc(used[r], 1)
                    pe.drain().then_inc(m_blk, 1)
                    if b or not first:
                        turn_block(j, b - 1)

            turn(0, True)
            with pe.Fori(1, N_MOD // 4) as j:
                turn(j)
            turn_block(N_MOD // 4, -1)

        def linear(nm, subs, x, n, before):
            for m in range(subs):
                r, t = m % 3, m // 3
                pe.wait_ge(lin_evac, before + m + 1)
                pe.wait_ge(lo_ready[r], LO0 + AT[nm].u[r] + t + 1)
                for k in range(KC):
                    for a, b in pieces(n):
                        ins = mm3(pe, slot(m % 4, a, b), [w[r][:, k * P:(k + 1) * P] for w in (whi, wlo)],
                                  [h[:, k, a:b] for h in x], k == 0, k == KC - 1)
                ins.then_inc(used[r], 1)

        pe.wait_ge(s_const, 16 * len(CONSTS))
        pe.wait_ge(s_scond, 4)
        mods_pe(0)
        phase_end(pe, "mods0")
        norm_pe(pe, 0, T, sqb)
        phase_end(pe, "norm0")
        linear("ain", 6, xn, T, 0)
        phase_end(pe, "ain")
        SQ, SUM = c_sem[0], c_sem[1]
        pe.wait_ge(SQ, 2)
        for kc in range(2):
            for a, b in pieces(T):
                ins = pe.matmul(slot(0, a, b), ones[:, :], l0_sq[:, kc, a:b], start=kc == 0, stop=kc == 1)
        ins.then_inc(SUM, 1)
        pe.wait_ge(SQ, 3)
        for a, b in pieces(T):
            ins = pe.matmul(slot(1, a, b), ones[:, :], l0_x[:, 0, a:b], start=True, stop=True)
        ins.then_inc(SUM, 1)
        phase_end(pe, "lat")
        fa, fahi, falo, fev, fhi, flo = f_sem
        u4 = AT["four"].u
        pe.wait_ge(flo, 2)
        pe.wait_ge(lo_ready[0], LO0 + u4[0] + 1)
        for tb in range(6):
            if tb >= 4:
                pe.wait_ge(falo, tb - 3)
            for ch in range(2):
                ins = mm3(pe, slot(tb % 4, ch * 256, ch * 256 + 256), [t[:, ch, tb * P:(tb + 1) * P] for t in ff_hl],
                          [w[0][:, 0:256] for w in (whi, wlo)], True, True)
            ins.then_inc(fa, 1)
        pe.drain().then_inc(used[0], 1)
        pe.wait_ge(falo, 6)
        for u in range(4):
            r, t = (u + 1) % 3, (u + 1) // 3
            pe.wait_ge(lo_ready[r], LO0 + u4[r] + t + 1)
            for ch in range(2):
                for kb in range(2):
                    o = ch * 256 + (u // 2) * 128
                    ins = mm3(pe, slot(ch, 0, 512), [x[:, (u % 2) * 2 + kb, o:o + 128] for x in four_a],
                              [w[r][:, kb * 512:(kb + 1) * 512] for w in (whi, wlo)],
                              u == 0 and kb == 0, u == 3 and kb == 1)
            ins.then_inc(used[r], 1)
        pe.wait_ge(lo_ready[2], LO0 + u4[2] + 2)
        for ch in range(2):
            for u in range(2):
                for kb in range(2):
                    o = ch * 256 + u * 128
                    ins = mm3(pe, slot(ch, 512, 768), [x[:, 4 + kb, o:o + 128] for x in four_a],
                              [w[2][:, (u * 2 + kb) * 256:(u * 2 + kb + 1) * 256] for w in (whi, wlo)],
                              u == 0 and kb == 0, u == 1 and kb == 1)
        ins.then_inc(used[2], 1)
        phase_end(pe, "four")

        def queries0(i, h):
            for a, b in pieces(T):
                for kc in range(2):
                    o = (h * 2 + kc) * P
                    ins = mm3(pe, slot(1 + h, a, b), [w[0][:, o:o + P] for w in (whi, wlo)],
                              [x[:, kc, a:b] for x in cq], kc == 0, kc == 1)
            return ins

        def head0(i):
            A, u = a_sem[0], AT["pr0"].u
            pe.wait_ge(A["oev"], i * 12 + 2)
            pe.wait_ge(lo_ready[1], i + (u[1] + LO0 + 1))
            for a, b in pieces(T):
                ins = mm3(pe, slot(0, a, b), [w[1][:, 0:P] for w in (whi, wlo)], [x[:, a:b] for x in ckv],
                          True, True)
            ins.then_inc(used[1], 1)
            pe.wait_ge(lo_ready[0], i + (u[0] + LO0 + 1))
            queries0(i, 0).then_inc(A["qm"], 1)

        def pair0(i, nxt):
            A, u = a_sem[0], AT["pr0"].u
            pe.wait_ge(A["oev"], i * 12 + 4)
            pe.wait_ge(A["ksq"], i + 1)
            for a, b in pieces(T):
                pe.matmul(slot(3, a, b), ones64[:, :], sqk0[:, a:b], start=True, stop=False)
                ins = pe.matmul(slot(3, a, b), onesr[:, :], sqr[:, a:b], start=False, stop=True)
            ins.then_inc(A["ks"], 1)
            queries0(i, 1).then_inc(used[0], 1)
            pe.wait_ge(lo_ready[2], i + (u[2] + LO0 + 1))
            pe.wait_ge(A["kstd"], i + 1)
            for tb in range(6):
                ins = mm3(pe, slot(3, tb * P, (tb + 1) * P), [x[:, tb * P:(tb + 1) * P] for x in ckv],
                          [w[2][:, 0:P] for w in (whi, wlo)], True, True)
            for h in range(2):
                pe.wait_ge(A["qsq"], i * 2 + (h + 1))
                for b in range(6):
                    ins = pe.matmul(slot(3, 1000 + h * 6 + b, 1001 + h * 6 + b), sqq0[:, h, b * P:(b + 1) * P],
                                    ones96[:, 0:1], start=True, stop=True)
            ins.then_inc(used[2], 1)

            def before(j):
                if j == 0:
                    pe.wait_ge(A["kx"], i * 2 + 2)
                    pe.wait_ge(A["klo"], i * 2 + 1)
                    pe.wait_ge(A["qlo"], i * 2 + 1)
                if j == 2:
                    pe.wait_ge(A["qx"], i * 2 + 2)
                if j == 3:
                    pe.wait_ge(A["rqs"], i + 1)
                    pe.wait_ge(A["vlo"], i + 1)
                if j == 6:
                    pe.wait_ge(A["klo"], i * 2 + 2)
                    pe.wait_ge(A["qlo"], i * 2 + 2)

            att_pe(pe, 0, i, before, nxt, head0)

        head0(0)
        pairs(pe, 0, pair0)
        phase_end(pe, "att0")
        phase_end(pe, "split0")
        linear("out0", 8, mix0_hl, T, 6)
        phase_end(pe, "out0")

        n1 = NORM_AT["n1"]

        def block_pe(t, more):
            def between(c0):
                return lambda c: next_norm_pe(pe, t + (n1 + 1), c0 + c) if more else None

            ffn_pe(pe, "mlp", t * 22, AT["mlp"].u, BLK, "channels", True, False,
                   lambda: pe.wait_ge(y_evac, t + 1),
                   lambda k: pe.wait_ge(nr[7], t * 8 + (n1 * 8 + k + 1)), between(0),
                   more=True)
            ffn_pe(pe, "mlp", t * 22 + 11, AT["mlp"].u, BLK, "channels", False, True, lambda: None,
                   between=between(11), joined=True)

        norm_pe(pe, n1, BLK, fn_sq)
        with pe.Fori(0, 2) as t:
            block_pe(t, True)
        block_pe(2, False)
        phase_end(pe, "mlp")
        mods_pe(1)
        phase_end(pe, "mods1")
        norm_pe(pe, NORM_AT["n2"], T, sqb)
        phase_end(pe, "norm1")

        def project(r, slot_, n, ks):
            for k in ks:
                for a, b in pieces(n):
                    ins = mm3(pe, slot(slot_, a, b), [w[r][:, k * P:(k + 1) * P] for w in (whi, wlo)],
                              [x[:, k, a:b] for x in xn], k == 0, k == KC - 1)
            return ins

        def head1(i):
            A, u = a_sem[1], AT["pr1"].u
            pe.wait_ge(A["oev"], i * 8 + 2)
            pe.wait_ge(lo_ready[1], i + (u[1] + LO0 + 1))
            project(1, 1, T, range(KC)).then_inc(used[1], 1)

        def pair1(i, nxt):
            A, u = a_sem[1], AT["pr1"].u
            pe.wait_ge(A["oev"], i * 8 + 4)
            pe.wait_ge(lo_ready[0], i + (u[0] + LO0 + 1))
            project(0, 2, SEQ, range(2))
            pe.wait_ge(A["ksq"], i + 1)
            for a, b in pieces(T):
                ins = pe.matmul(slot(0, a, b), ones64[:, :], sq1[:, a:b], start=True, stop=True)
            ins.then_inc(A["ks"], 1)
            project(0, 2, SEQ, range(2, KC)).then_inc(used[0], 1)
            pe.wait_ge(lo_ready[2], i + (u[2] + LO0 + 1))
            project(2, 3, T, range(KC)).then_inc(used[2], 1)
            pe.wait_ge(A["qsq"], i + 1)
            for b in range(4):
                ins = pe.matmul(slot(2, 1000 + b * 2, 1002 + b * 2), sqq1[:, b * P:(b + 1) * P], half2[:, :],
                                start=True, stop=True)
            ins.then_inc(A["rq"], 1)

            def before(j):
                if j == 0:
                    pe.wait_ge(A["klo"], i + 1)
                    pe.wait_ge(A["qlo"], i + 1)
                if j == 1:
                    pe.wait_ge(A["vc"], i + 1)
                    for tb in range(6):
                        ins = pe.transpose(slot(3, tb * P, (tb + 1) * P), sq1[:, tb * P:(tb + 1) * P], ident[:, :])
                    ins.then_inc(A["vt"], 1)
                if j == 2:
                    pe.wait_ge(A["rqs"], i + 1)
                if j == 3:
                    pe.wait_ge(A["vlo"], i + 1)

            att_pe(pe, 1, i, before, nxt, head1)

        head1(0)
        pe.wait_ge(s_zero, 1)
        pairs(pe, 1, pair1)
        phase_end(pe, "att1")
        phase_end(pe, "split1")
        linear("out1", 8, mix1_hl, SEQ, 14)
        phase_end(pe, "out1")

        E = e_sem
        norm_pe(pe, NORM_AT["n3"], SEQ, fn_sq)
        pe.wait_ge(E["in"], 16 * len(E_CONSTS))
        for k in range(KC):
            pe.wait_ge(nr[5], (NORM_AT["n3"]) * 8 + k + 1)
            if k >= 4:
                pe.wait_ge(E["xtlo"], k - 3)
            for b in range(4):
                ins = pe.transpose(bank(k % 4, b * P, P), xfm[k % 2][:, b * P:(b + 1) * P], ident[:, :])
            for b in range(4):
                ins = pe.matmul(bank(5, b * 8, 8), xfm[k % 2][:, b * P:(b + 1) * P], wr[:, k, :],
                                start=k == 0 and b == 0, stop=k == KC - 1, skip_group_check=True)
            ins.then_inc(E["xt"], 1)
        pe.wait_ge(E["sel"], 1)
        for b in range(4):
            for b2 in range(b + 1):
                ins = pe.matmul(bank(4, b * 8, 8), (tri if b2 == b else ones)[:, :], seltok[:, b2, :],
                                start=b2 == 0, stop=b2 == b)
        for b2 in range(4):
            ins = pe.matmul(bank(4, 32, 8), ones[:, :], seltok[:, b2, :], start=b2 == 0, stop=b2 == 3)
        ins.then_inc(E["pos"], 1)
        phase_end(pe, "router")

        def gather(g, ks):
            pe.wait_ge(E["gm"], g + 1)
            for k in ks:
                pe.wait_ge(E["xlo"], g * 8 + (k + 1))
                for b in range(4):
                    for w in range(2):
                        ins = pe.matmul(bank(GATHER_BANKS[k % 3], 0, BLK), xt[w][:, b, k * P:(k + 1) * P], gm[:, b, :],
                                        start=b == 0 and w == 0, stop=b == 3 and w == 1)
                ins.then_inc(E["gmt"], 1)

        def item(it, N):
            J = N // P

            def between(c):
                if c == 0:
                    for j in range(J):
                        for b in range(4):
                            ins = pe.matmul(bank(5, j, 1), gm[:, b, j * P:(j + 1) * P].bitcast(F32),
                                            cmbi[:, b, ds(it, 1)], start=b == 0, stop=b == 3)
                    ins.then_inc(E["ws"], 1)
                    for j in range(J):
                        for b in range(4):
                            ins = pe.transpose(bank(7 - j, b * P, P), gm[:, b, j * P:(j + 1) * P].bitcast(F32),
                                               ident[:, :])
                    ins.then_inc(E["sc"], 1)
                    pe.wait_ge(E["wsc"], it + 1)
                if c == 1:
                    pe.wait_ge(E["gt"], it + 1)
                if c == EX_CHUNKS - 1:
                    gather(it + 1, range(3))

            ffn_pe(pe, "exp", it * EX_CHUNKS, AT["exp"].u, N, "slots", True, True,
                   lambda: pe.wait_ge(E["scev"], it * 8 + 4),
                   lambda k: pe.wait_ge(E["xlo"], it * 8 + max(9, k + 4)), between)
            gather(it + 1, range(3, KC))
            pe.wait_ge(E["ylo"], it * 2 + 2)
            for m in range(KC):
                pe.wait_ge(E["scev"], it * 8 + (m + 1))
                for j in range(J):
                    for w in range(2):
                        ins = pe.matmul(bank(m % 4, 0, 512), yhl[w][:, j, m * P:(m + 1) * P], gt[:, j, :],
                                        start=j == 0 and w == 0, stop=j == J - 1 and w == 1)
                ins.then_inc(E["sct"], 1)

        gather(0, range(KC))
        items(pe, item)
        phase_end(pe, "moe")

    @block.scalar
    def _(act):
        act.sem_inc(a_sem[0]["oev"], 4)
        act.sem_inc(a_sem[1]["oev"], 4)
        act.wait_ge(s_const, 16 * len(CONSTS))
        act.activation(scond[:, :, :], cond[:, :, :], ACT.Silu).then_inc(s_scond, 1)
        act.wait_ge(s_scond, 2)
        act.activation(scond_hl[:, :, 0:2], scond[:, :, :], ACT.Copy).then_inc(s_scond, 1)

        def mods_act(l):
            name = ("md0", "md1")[l]
            u, f = AT[name].u, AT[name].f

            def rows(j, b):
                act.wait_ge(m_blk, j * 3 + (12 * l + b + 1))
                act.wait_ge(m_tr, j * 3 + (12 * l + b + 1))
                act.activation(mrow[b][:, :], bank(b % 3, 0, 512), ACT.Copy).then_inc(m_row, 1)

            def turn(j, first=False):
                for b in range(3):
                    for q in range(4):
                        t, r = (b * 4 + q) // 3, (b * 4 + q) % 3
                        if q == 2 and (b or not first):
                            rows(j, b - 1)
                        hi_unit(act, r, (raw + [raw_m])[t][:, r, :], U, t, j + (f[t] + 1), j * 4 + (u[r] + t))

            turn(0, True)
            with act.Fori(1, N_MOD // 4) as j:
                turn(j)
            rows(N_MOD // 4, -1)

        mods_act(0)
        phase_end(act, "mods0")

        def linear_hi(nm, m):
            r, t = m % 3, m // 3
            hi_unit(act, r, raw[t][:, r, :], U, t, AT[nm].f[t] + 1, AT[nm].u[r] + t)

        def first_ain():
            for m in range(3):
                linear_hi("ain", m)

        norm_act(act, 0, res_all, T, sqb, rstd, zb, xfb, cols_all(0), lambda k: xn[0][:, k, :], first_ain)
        phase_end(act, "norm0")
        for m in range(6):
            if m + 3 < 6:
                linear_hi("ain", m + 3)
            act.wait_ge(used[m % 3], USED0 + AT["ain"].u[m % 3] + m // 3 + 1)
            act.activation(plat[:, m, :], slot(m % 4, 0, T), ACT.Copy).then_inc(lin_evac, 1)
        phase_end(act, "ain")
        SQ, SUM, STD, X, HI, LO, KR = c_sem
        for kc in range(2):
            act.activation(l0_sq[:, kc, :], plat[:, kc, :], ACT.Square).then_inc(SQ, 1)
        act.activation(l0_x[:, 0, :], plat[:, 2, :], ACT.Square).then_inc(SQ, 1)
        act.activation(sqr[:, :], plat[:, 3, :], ACT.Square)
        act.wait_ge(SUM, 1)
        act.activation(l0_rs[:, 0, :], slot(0, 0, T), ACT.Sqrt, bias=eps[:, 0:1], scale=1.0 / A_QR).then_inc(STD, 1)
        act.wait_ge(SUM, 2)
        act.activation(l0_rs[:, 1, :], slot(1, 0, T), ACT.Sqrt, bias=eps[:, 0:1], scale=1.0 / A_KVR).then_inc(STD, 1)
        for n, (dst, src) in enumerate(((cq[0][:, 0, :], l0_t[:, 0, :]), (cq[0][:, 1, :], l0_t[:, 1, :]),
                                        (ckv[0][:, :], l0_x[:, 1, :]))):
            act.wait_ge(X, n + 1)
            act.activation(dst, src, ACT.Copy).then_inc(HI, 1)
        phase_end(act, "lat")
        fa, fahi, falo, fev, fhi, flo = f_sem
        for ch in range(2):
            act.activation(ff_hl[0][:, ch, :], plat[:, 4 + ch, :], ACT.Copy).then_inc(fhi, 1)
        for m in range(3):
            linear_hi("four", m)
        for tb in range(6):
            act.wait_ge(fa, tb + 1)
            act.activation(four_a[0][:, tb, :], slot(tb % 4, 0, 512), ACT.Copy).then_inc(fahi, 1)
        for m in range(3, 6):
            linear_hi("four", m)
        act.wait_ge(used[2], USED0 + AT["four"].u[2] + 2)
        for ch in range(2):
            act.activation(mix0[:, 6 + ch, :], slot(ch, 0, T), ACT.Copy)
        phase_end(act, "four")

        def head0(i):
            A, u = a_sem[0], AT["pr0"].u
            act.wait_ge(used[1], i + (u[1] + USED0 + 1))
            act.activation(sqk0[:, :], slot(0, 0, T), ACT.Square).then_inc(A["ksq"], 1)

        def pair0(i, nxt):
            A, u = a_sem[0], AT["pr0"].u
            act.wait_ge(A["qm"], i + 1)
            act.activation(sqq0[:, 0, :], slot(1, 0, T), ACT.Square).then_inc(A["qsq"], 1)
            act.wait_ge(A["qx"], i * 2 + 1)
            act.activation(q0[0][:, 0, :], qx0[0][:, :], ACT.Copy).then_inc(A["qhi"], 1)
            act.wait_ge(A["ks"], i + 1)
            act.activation(rk0[:, :], slot(3, 0, T), ACT.Sqrt, bias=eps[:, 0:1], scale=1.0 / A_QK
                           ).then_inc(A["kstd"], 1)
            act.wait_ge(used[0], i + (u[0] + USED0 + 1))
            act.activation(sqq0[:, 1, :], slot(2, 0, T), ACT.Square).then_inc(A["qsq"], 1)
            act.wait_ge(used[2], i + (u[2] + USED0 + 1))
            act.activation(rqs[:, 0:12], slot(3, 1000, 1012), ACT.Sqrt, bias=eps[:, 1:2]).then_inc(A["rqs"], 1)
            act.activation(v0[0][:, :, :], slot(3, 0, T), ACT.Copy).then_inc(A["vhi"], 1)
            for h in range(2):
                act.wait_ge(A["kx"], i * 2 + (h + 1))
                if h == 0:
                    act.wait_ge(A["kd"], i + 1)
                act.activation(k0[0][:, h, :], kx0[h][:, :], ACT.Copy).then_inc(A["khi"], 1)
            act.wait_ge(A["qx"], i * 2 + 2)
            act.activation(q0[0][:, 1, :], qx0[1][:, :], ACT.Copy).then_inc(A["qhi"], 1)
            att_act(act, 0, i, nxt, head0)

        for r in ROLE_ORDER:
            pair_hi(act, 0, 0, 0, AT["pr0"].f[0], r)
        head0(0)
        pairs(act, 0, pair0)
        phase_end(act, "att0")
        for k in range(KC):
            act.activation(mix0_hl[0][:, k, :], mix0[:, k, :], ACT.Copy).then_inc(mx_hi, 1)
        phase_end(act, "split0")
        for m in range(8):
            linear_hi("out0", m)
        phase_end(act, "out0")
        n1 = NORM_AT["n1"]
        norm_act(act, n1, lambda k: res[:, k, 0:BLK], BLK, fn_sq, fn_rs, fn_z, fn_x,
                 lambda k: [(0, BLK, nscr[:, k, 0:1], nshr[:, k, 0:1])], lambda k: xg[0][:, k, :])

        def block_act(t, more):
            def between(c0):
                return lambda c: next_norm_act(act, t + (n1 + 1), t + 1, c0 + c) if more else None

            ffn_act(act, "mlp", t * 22, t * 2, AT["mlp"], BLK, between(0), raw + [raw_f], False, True)
            ffn_act(act, "mlp", t * 22 + 11, t * 2 + 1, AT["mlp"], BLK, between(11), raw + [raw_f], False, more)

        for r in range(2):
            hi_unit(act, r, raw[0][:, r, :], U, 0, AT["mlp"].f[0] + 1, AT["mlp"].u[r])
        with act.Fori(0, 2) as t:
            block_act(t, True)
            act.wait_ge(used[1], t * 22 + (AT["mlp"].u[1] + USED0 + 22))
            for k in range(KC):
                act.activation(xg[0][:, k, :], xs[:, k, :], ACT.Copy).then_inc(nr[6], 1)
        block_act(2, False)
        phase_end(act, "mlp")
        mods_act(1)
        phase_end(act, "mods1")

        def first_pair():
            for r in ROLE_ORDER:
                pair_hi(act, 1, 0, 0, AT["pr1"].f[0], r)

        norm_act(act, NORM_AT["n2"], res_all, T, sqb, rstd, zb, xfb, cols_all(1), lambda k: xn[0][:, k, :],
                 first_pair)
        phase_end(act, "norm1")

        def head1(i):
            A, u = a_sem[1], AT["pr1"].u
            act.wait_ge(used[1], i + (u[1] + USED0 + 1))
            act.activation(sq1[:, :], slot(1, 0, T), ACT.Square).then_inc(A["ksq"], 1)

        def pair1(i, nxt):
            A, u = a_sem[1], AT["pr1"].u
            act.wait_ge(A["ks"], i + 1)
            act.activation(rk1[:, :], slot(0, 0, T), ACT.Sqrt, bias=eps[:, 0:1], scale=1.0 / DH
                           ).then_inc(A["kstd"], 1)
            act.wait_ge(used[0], i + (u[0] + USED0 + 1))
            act.activation(sqq1[:, :], slot(2, 0, SEQ), ACT.Square).then_inc(A["qsq"], 1)
            act.wait_ge(A["kx"], i + 1)
            act.activation(k1[0][:, :], rk1[:, :], ACT.Copy).then_inc(A["khi"], 1)
            act.wait_ge(A["qx"], i + 1)
            for h in range(2):
                rows = slice(h * 64, h * 64 + 64)
                ins = act.activation(q1[0][rows, h, :], qx1[rows, :], ACT.Copy)
            ins.then_inc(A["qhi"], 1)
            act.wait_ge(used[2], i + (u[2] + USED0 + 1))
            act.activation(sq1[:, :], slot(3, 0, T), ACT.Copy).then_inc(A["vc"], 1)
            act.wait_ge(A["rq"], i + 1)
            act.activation(rqs[:, 0:8], slot(2, 1000, 1008), ACT.Sqrt, bias=eps[:, 2:3]).then_inc(A["rqs"], 1)
            act.wait_ge(A["vt"], i + 1)
            act.activation(v1[0][:, :, :], slot(3, 0, T), ACT.Copy).then_inc(A["vhi"], 1)
            att_act(act, 1, i, nxt, head1)

        head1(0)
        pairs(act, 1, pair1)
        phase_end(act, "att1")
        for k in range(KC):
            act.activation(mix1_hl[0][:, k, :], mix1[:, k, :], ACT.Copy).then_inc(mx_hi, 1)
        phase_end(act, "split1")
        for m in range(8):
            linear_hi("out1", m)
        phase_end(act, "out1")

        E = e_sem
        n3 = NORM_AT["n3"]
        norm_act_first(act, n3)
        for k in range(KC):
            act.wait_ge(nr[4], n3 * 8 + k + 1)
            if k >= 2:
                act.wait_ge(E["xt"], k - 1)
            a, b, scale, shift = cols_moe(k)[0]
            act.activation(xfm[k % 2][:, :], fn_z[k % 2][:, :], ACT.Identity, bias=shift, scale=scale
                           ).then_inc(nr[5], 1)
            if k >= 1:
                turned_hi(act, k - 1)
        turned_hi(act, KC - 1)
        act.wait_ge(E["exps"], 1)
        act.activation(wexp[:, :, :], wexp[:, :, :], ACT.Exp).then_inc(E["exps"], 1)
        phase_end(act, "router")

        def gathered_hi(g, ks):
            for k in ks:
                act.wait_ge(E["gmt"], g * 8 + (k + 1))
                act.activation(xg[0][:, k, :], bank(GATHER_BANKS[k % 3], 0, BLK), ACT.Copy).then_inc(E["xhi"], 1)

        def item(it, N):
            J = N // P

            def between(c):
                if c == 0:
                    act.wait_ge(E["sc"], it + 1)
                    for j in range(J):
                        ins = act.activation(gt[:, j, :], bank(7 - j, 0, 512), ACT.Copy)
                    ins.then_inc(E["gt"], 1)

            ffn_act(act, "exp", it * EX_CHUNKS, it, AT["exp"], N, between)
            gathered_hi(it + 1, range(3))
            act.wait_ge(used[2], it * EX_CHUNKS + (AT["exp"].u[2] + USED0 + EX_CHUNKS))
            for part in range(2):
                yb, j, a, b = y_part(J, part)
                act.activation(yx[part][:, a:b], yb, ACT.Copy, scale=wslot[:, j:j + 1]).then_inc(E["yx"], 1)
                act.wait_ge(E["yx"], it * 2 + (part + 1))
                act.activation(yhl[0][:, j, a:b], yx[part][:, a:b], ACT.Copy).then_inc(E["yhi"], 1)
            gathered_hi(it + 1, range(3, KC))

        gathered_hi(0, range(KC))
        items(act, item)
        phase_end(act, "moe")

    @block.vector
    def _(dve):
        for r in range(3):
            dve.sem_inc(lo_ready[r], LO0)
        dve.sem_inc(m_row, 3)
        for n in ("mlp", "exp"):
            dve.sem_inc(ff[n]["hm"], 2)
        dve.sem_inc(y_evac, 1)
        dve.sem_inc(e_sem["scev"], 4)
        dve.sem_inc(e_sem["xlo"], 3)
        dve.sem_inc(lin_evac, 4)
        chain = [0]

        def link(ins):
            chain[0] += 1
            ins.then_inc(s_chain, 1)
            dve.wait_ge(s_chain, chain[0])

        dve.wait_ge(s_const, 16 * len(CONSTS))

        dve.tensor_scalar(scond_hl[:, :, :], ones[:, :].unsqueeze(1).broadcast_to([P, KC, P]), 0.0, None, ALU.mult
                          ).then_inc(s_scond, 1)
        dve.wait_ge(s_scond, 3)
        dve.tensor_tensor(scond_hl[:, :, 2:4], scond[:, :, :], scond_hl[:, :, 0:2].bitcast(F32), ALU.subtract
                          ).then_inc(s_scond, 1)

        def mods_dve(l):
            u = AT[("md0", "md1")[l]].u
            with dve.Fori(0, N_MOD // 4) as j:
                for n in range(12):
                    t, r = n // 3, n % 3
                    lo_unit(dve, r, (raw + [raw_m])[t][:, r, :], U, j * 4 + (u[r] + t + 1))
            dve.wait_ge(m_tr, 12 * l + 12 + 3)
            link(dve.tensor_tensor(mods[:, l, :, :], bank(7, 0, 96).rearrange("p (s c) -> p s c", c=2),
                                   bmod[:, l, :].unsqueeze(2).broadcast_to([P, 48, 2]), ALU.add))
            for n in range(2):
                sc = mods[:, l, (3 * n + 1) * KC:(3 * n + 2) * KC, :]
                link(dve.tensor_scalar(nsc[:, l, n, :, :], sc, 1.0, None, ALU.add))
                link(dve.tensor_tensor(nsc[:, l, n, :, :], nsc[:, l, n, :, :],
                                       ng[:, l, n, :].unsqueeze(2).broadcast_to([P, KC, 2]), ALU.mult))

        mods_dve(0)
        phase_end(dve, "mods0")

        def linear_lo(nm, m):
            r, t = m % 3, m // 3
            lo_unit(dve, r, raw[t][:, r, :], U, AT[nm].u[r] + t + 1)

        def first_ain():
            for m in range(3):
                linear_lo("ain", m)

        norm_dve(dve, 0, res_all, T, rstd, zb, xfb, lambda k: xn[0][:, k, :], lambda k: xn[1][:, k, :], first_ain)
        phase_end(dve, "norm0")

        for m in range(3, 6):
            linear_lo("ain", m)
        phase_end(dve, "ain")
        SQ, SUM, STD, X, HI, LO, KR = c_sem
        link(dve.scalar_tensor_tensor(out=l0_x[64:128, 2, :], in0=plat[64:128, 3, :], scalar=gcol[64:128, 5:6],
                                      in1=ktab[64:128, :], op0=ALU.mult, op1=ALU.mult))
        link(dve.scalar_tensor_tensor(out=krope[64:128, :], in0=plat[0:64, 3, :], scalar=gcol[0:64, 5:6],
                                      in1=ktab[0:64, :], op0=ALU.mult, op1=ALU.mult))
        link(dve.tensor_tensor(krope[64:128, :], krope[64:128, :], l0_x[64:128, 2, :], ALU.add))
        link(dve.tensor_copy(krope[0:64, :], krope[64:128, :]))
        link(dve.tensor_scalar(csg[:, :], qtab[:, :], gcol[:, 3:4], None, ALU.mult))
        dve.wait_ge(STD, 1)
        link(dve.reciprocal(l0_rs[:, 0, :], l0_rs[:, 0, :]))
        dve.wait_ge(STD, 2)
        link(dve.reciprocal(l0_rs[:, 1, :], l0_rs[:, 1, :]))
        vals = ((plat[:, 0, :], 0, l0_rs[:, 0, :], l0_t[:, 0, :], cq[0][:, 0, :], cq[1][:, 0, :]),
                (plat[:, 1, :], 1, l0_rs[:, 0, :], l0_t[:, 1, :], cq[0][:, 1, :], cq[1][:, 1, :]),
                (plat[:, 2, :], 2, l0_rs[:, 1, :], l0_x[:, 1, :], ckv[0][:, :], ckv[1][:, :]))
        for src, g, rs, dst, hi, lo in vals:
            dve.scalar_tensor_tensor(out=dst, in0=src, scalar=gcol[:, g:g + 1], in1=rs, op0=ALU.mult,
                                     op1=ALU.mult).then_inc(X, 1)
        for n, (src, g, rs, dst, hi, lo) in enumerate(vals):
            dve.wait_ge(HI, n + 1)
            dve.tensor_tensor(lo, dst, hi.bitcast(F32), ALU.subtract).then_inc(LO, 1)
        phase_end(dve, "lat")
        fa, fahi, falo, fev, fhi, flo = f_sem
        for ch in range(2):
            dve.wait_ge(fhi, ch + 1)
            dve.tensor_tensor(ff_hl[1][:, ch, :], plat[:, 4 + ch, :], ff_hl[0][:, ch, :].bitcast(F32),
                              ALU.subtract).then_inc(flo, 1)
        for m in range(3):
            linear_lo("four", m)
        for tb in range(6):
            dve.wait_ge(fahi, tb + 1)
            dve.tensor_tensor(four_a[1][:, tb, :], slot(tb % 4, 0, 512), four_a[0][:, tb, :].bitcast(F32),
                              ALU.subtract).then_inc(falo, 1)
        for m in range(3, 6):
            linear_lo("four", m)
        phase_end(dve, "four")

        def pair0(i, nxt):
            A, u = a_sem[0], AT["pr0"].u

            def queries(h):
                dve.wait_ge(A["qsq"], i * 2 + (h + 1))
                dve.tensor_tensor(qx0[h][:, :], slot(1 + h, 0, T), csg[:, :], ALU.mult).then_inc(A["qx"], 1)

            dve.wait_ge(A["o"], i * 12 + NPT[0])
            queries(0)
            dve.wait_ge(A["kstd"], i + 1)
            dve.reciprocal(rk0[:, :], rk0[:, :]).then_inc(A["rk"], 1)
            dve.wait_ge(A["rk"], i + 1)
            for h in range(2):
                rows = slice(h * 64, h * 64 + 64)
                if h:
                    dve.wait_ge(A["kr"], i + 1)
                dve.scalar_tensor_tensor(out=kx0[h][0:64, :], in0=slot(0, 0, T)[rows, :], scalar=gcol[rows, 4:5],
                                         in1=rk0[rows, :], op0=ALU.mult, op1=ALU.mult).then_inc(A["kx"], 1)
                if h == 0:
                    dve.tensor_tensor(kx0[0][64:128, :], krope[0:64, :], rk0[0:64, :], ALU.mult).then_inc(A["kd"], 1)
            queries(1)
            for h in range(2):
                dve.wait_ge(A["khi"], i * 2 + (h + 1))
                dve.tensor_tensor(k0[1][:, h, :], kx0[h][:, :], k0[0][:, h, :].bitcast(F32), ALU.subtract
                                  ).then_inc(A["klo"], 1)
            dve.wait_ge(A["rqs"], i + 1)
            dve.reciprocal(rq[:, 0:12], rqs[:, 0:12]).then_inc(A["rqd"], 1)
            dve.wait_ge(A["vhi"], i + 1)
            dve.tensor_tensor(v0[1][:, :, :], slot(3, 0, T), v0[0][:, :, :].bitcast(F32), ALU.subtract
                              ).then_inc(A["vlo"], 1)
            dve.wait_ge(A["rqd"], i + 1)
            att_dve(dve, 0, i, nxt)

        for r in ROLE_ORDER:
            pair_lo(dve, 0, 0, 0, 0, r)
        pairs(dve, 0, pair0)
        phase_end(dve, "att0")
        for k in range(KC):
            dve.wait_ge(mx_hi, k + 1)
            dve.tensor_tensor(mix0_hl[1][:, k, :], mix0[:, k, :], mix0_hl[0][:, k, :].bitcast(F32), ALU.subtract)
        phase_end(dve, "split0")

        def out_dve(nm, l, parts):
            for m in range(3):
                linear_lo(nm, m)
            for m in range(8):
                dve.wait_ge(used[m % 3], USED0 + AT[nm].u[m % 3] + m // 3 + 1)
                for n, (a, b, s) in enumerate(parts):
                    ins = dve.scalar_tensor_tensor(out=res[:, m, a:b], in0=slot(m % 4, a, b),
                                                   scalar=mods[:, l, 2 * KC + m, s:s + 1], in1=res[:, m, a:b],
                                                   op0=ALU.mult, op1=ALU.add)
                ins.then_inc(lin_evac, 1)
                if m + 3 < 8:
                    linear_lo(nm, m + 3)

        out_dve("out0", 0, [(0, SEQ, 0), (SEQ, T, 1)])
        for dst, src in ((nscr, nsc[:, 0, 1, :, :]), (nshr, mods[:, 0, 3 * KC:4 * KC, :]),
                         (ngtr, mods[:, 0, 5 * KC:6 * KC, :])):
            for t, s in enumerate((0, 0, 1)):
                dve.tensor_copy(dst[:, :, t], src[:, :, s])
        phase_end(dve, "out0")
        n1 = NORM_AT["n1"]
        norm_dve(dve, n1, lambda k: res[:, k, 0:BLK], BLK, fn_rs, fn_z, fn_x,
                 lambda k: xg[0][:, k, :], lambda k: xg[1][:, k, :])

        def block_dve(t, more):
            def between(c0):
                return lambda c: next_norm_dve(dve, t + (n1 + 1), t + 1, c0 + c) if more else None

            def output():
                dve.wait_ge(used[2], t * 22 + (AT["mlp"].u[2] + USED0 + 22))
                for m in range(KC):
                    ins = dve.scalar_tensor_tensor(
                        out=res[:, m, ds(t * BLK, BLK)], in0=bank(m // 2, (m % 2) * BLK, BLK),
                        scalar=ngtr[:, m, ds(t, 1)], in1=res[:, m, ds(t * BLK, BLK)], op0=ALU.mult, op1=ALU.add)
                ins.then_inc(y_evac, 1)

            ffn_dve(dve, "mlp", t * 22, AT["mlp"], BLK, lambda c: None, between(0), raw + [raw_f], False, True)
            ffn_dve(dve, "mlp", t * 22 + 11, AT["mlp"], BLK, lambda c: None, between(11), raw + [raw_f], False, more)
            if more:
                for k in range(KC):
                    dve.wait_ge(nr[6], t * 8 + ((n1 + 1) * 8 + k + 1))
                    dve.tensor_tensor(xg[1][:, k, :], xs[:, k, :], xg[0][:, k, :].bitcast(F32), ALU.subtract
                                      ).then_inc(nr[7], 1)
            output()

        for r in range(2):
            lo_unit(dve, r, raw[0][:, r, :], U, AT["mlp"].u[r] + 1)
        with dve.Fori(0, 2) as t:
            block_dve(t, True)
        block_dve(2, False)
        phase_end(dve, "mlp")
        mods_dve(1)
        phase_end(dve, "mods1")

        def first_pair():
            for r in ROLE_ORDER:
                pair_lo(dve, 1, 0, 0, 0, r)

        norm_dve(dve, NORM_AT["n2"], res_all, T, rstd, zb, xfb, lambda k: xn[0][:, k, :], lambda k: xn[1][:, k, :],
                 first_pair)
        phase_end(dve, "norm1")
        for t in q1:
            dve.tensor_copy(t[64:128, 0, :].rearrange("p (a b) -> p a b", b=64),
                            ones64[64:128, 0:64].unsqueeze(1).broadcast_to([64, 8, 64]))
            ins = dve.tensor_copy(t[0:64, 1, :].rearrange("p (a b) -> p a b", b=64),
                                  ones64[0:64, 64:128].unsqueeze(1).broadcast_to([64, 8, 64]))
        ins.then_inc(s_zero, 1)

        dve.wait_ge(s_zero, 1)

        def pair1(i, nxt):
            A, u = a_sem[1], AT["pr1"].u
            dve.wait_ge(A["o"], i * 8 + NPT[1])
            dve.wait_ge(A["kstd"], i + 1)
            dve.reciprocal(rk1[:, :], rk1[:, :]).then_inc(A["rk"], 1)
            dve.wait_ge(A["rk"], i + 1)
            dve.scalar_tensor_tensor(out=rk1[:, :], in0=slot(1, 0, T), scalar=gcol[:, 7:8], in1=rk1[:, :],
                                     op0=ALU.mult, op1=ALU.mult).then_inc(A["kx"], 1)
            dve.wait_ge(A["qsq"], i + 1)
            dve.tensor_scalar(qx1[:, :], slot(2, 0, SEQ), gcol[:, 6:7], None, ALU.mult).then_inc(A["qx"], 1)
            dve.wait_ge(A["khi"], i + 1)
            dve.tensor_tensor(k1[1][:, :], rk1[:, :], k1[0][:, :].bitcast(F32), ALU.subtract).then_inc(A["klo"], 1)
            dve.wait_ge(A["qhi"], i + 1)
            for h in range(2):
                rows = slice(h * 64, h * 64 + 64)
                ins = dve.tensor_tensor(q1[1][rows, h, :], qx1[rows, :], q1[0][rows, h, :].bitcast(F32), ALU.subtract)
            ins.then_inc(A["qlo"], 1)
            dve.wait_ge(A["rqs"], i + 1)
            dve.reciprocal(rq[:, 0:8], rqs[:, 0:8]).then_inc(A["rqd"], 1)
            dve.wait_ge(A["vhi"], i + 1)
            dve.tensor_tensor(v1[1][:, :, :], slot(3, 0, T), v1[0][:, :, :].bitcast(F32), ALU.subtract
                              ).then_inc(A["vlo"], 1)
            dve.wait_ge(A["rqd"], i + 1)
            att_dve(dve, 1, i, nxt)

        pairs(dve, 1, pair1)
        phase_end(dve, "att1")
        for k in range(KC):
            dve.wait_ge(mx_hi, KC + k + 1)
            dve.tensor_tensor(mix1_hl[1][:, k, :], mix1[:, k, :], mix1_hl[0][:, k, :].bitcast(F32), ALU.subtract)
        phase_end(dve, "split1")
        out_dve("out1", 1, [(0, SEQ, 0)])
        phase_end(dve, "out1")

        E = e_sem
        n3 = NORM_AT["n3"]
        dve.wait_ge(nr[2], n3 + 1)
        link(dve.reciprocal(fn_rs[:, :], fn_rs[:, :]))

        def turned_lo(k):
            dve.wait_ge(E["xthi"], k + 1)
            dve.tensor_tensor(xt[1][:, :, k * P:(k + 1) * P], bank(k % 4, 0, 512).rearrange("p (b c) -> p b c", b=4),
                              xt[0][:, :, k * P:(k + 1) * P].bitcast(F32), ALU.subtract).then_inc(E["xtlo"], 1)

        for k in range(KC):
            if k >= 2:
                dve.wait_ge(nr[5], n3 * 8 + k - 1)
            dve.tensor_tensor(fn_z[k % 2][:, :], res_lat(k), fn_rs[:, :], ALU.mult).then_inc(nr[4], 1)
            if k >= 2:
                turned_lo(k - 2)
        turned_lo(KC - 2)
        turned_lo(KC - 1)

        dve.wait_ge(E["xt"], KC)
        dve.wait_ge(E["in"], 16 * len(E_CONSTS))
        link(dve.tensor_copy(lg[:, :, :], bank(5, 0, 32).rearrange("p (b e) -> p b e", b=4)))
        for b in range(4):
            mine = lg[:, b, :].unsqueeze(2).broadcast_to([P, 8, 8])
            other = lg[:, b, :].unsqueeze(1).broadcast_to([P, 8, 8])
            link(dve.tensor_tensor(r64[:, b, :, :], other, mine, ALU.is_gt))
            link(dve.tensor_tensor(r64b[:, b, :, :], other, mine, ALU.is_equal))
            link(dve.tensor_tensor(r64b[:, b, :, :], r64b[:, b, :, :], ltj[:, :, :], ALU.mult))
        link(dve.tensor_tensor(r64[:, :, :, :], r64[:, :, :, :], r64b[:, :, :, :], ALU.add))
        link(dve.reduce_sum(rank[:, :, :], r64[:, :, :, :], AX))
        dve.tensor_scalar(seltok[:, :, :], rank[:, :, :], 2.0, None, ALU.is_lt).then_inc(E["sel"], 1)
        link(dve.reduce_max(lmax[:, :], lg[:, :, :], AX))
        dve.tensor_tensor(wexp[:, :, :], lg[:, :, :], lmax[:, :].unsqueeze(2).broadcast_to([P, 4, 8]),
                          ALU.subtract).then_inc(E["exps"], 1)
        dve.wait_ge(E["exps"], 2)
        dve.wait_ge(E["sel"], 1)
        link(dve.tensor_tensor(wexp[:, :, :], wexp[:, :, :], seltok[:, :, :], ALU.mult))
        link(dve.reduce_sum(wsum[:, :], wexp[:, :, :], AX))
        link(dve.reciprocal(wsum[:, :], wsum[:, :]))
        link(dve.tensor_tensor(comb[:, :, :], wexp[:, :, :], wsum[:, :].unsqueeze(2).broadcast_to([P, 4, 8]), ALU.mult))
        dve.wait_ge(E["pos"], 1)
        link(dve.tensor_scalar(posn[:, :, :], bank(4, 0, 32).rearrange("p (b e) -> p b e", b=4), 1.0, None, ALU.add))
        link(dve.tensor_tensor(posn[:, :, :], posn[:, :, :], seltok[:, :, :], ALU.mult))
        link(dve.tensor_copy(cnts[:, :], bank(4, 32, 8)))
        link(dve.tensor_scalar(nit[:, :], cnts[:, :], 0.0, None, ALU.is_gt))
        link(dve.tensor_scalar(endi[:, :], cnts[:, :], float(BLK), None, ALU.is_gt))
        link(dve.tensor_tensor(nit[:, :], nit[:, :], endi[:, :], ALU.add))
        link(dve.tensor_tensor(r64[:, 0, :, :], nit[:, :].unsqueeze(1).broadcast_to([P, 8, 8]), ltj[:, :, :], ALU.mult))
        link(dve.reduce_sum(starti[:, :], r64[:, 0, :, :], AX))
        link(dve.tensor_tensor(endi[:, :], starti[:, :], nit[:, :], ALU.add))
        inum = itn[:, :].unsqueeze(2).broadcast_to([P, COLS, 8])
        link(dve.tensor_tensor(oneh[:, :, :], inum, starti[:, :].unsqueeze(1).broadcast_to([P, COLS, 8]), ALU.is_ge))
        link(dve.tensor_tensor(oneb[:, :, :], inum, endi[:, :].unsqueeze(1).broadcast_to([P, COLS, 8]), ALU.is_lt))
        link(dve.tensor_tensor(oneh[:, :, :], oneh[:, :, :], oneb[:, :, :], ALU.mult))

        def of_item(dst, vec):
            link(dve.tensor_tensor(oneb[:, :, :], oneh[:, :, :], vec[:, :].unsqueeze(1).broadcast_to([P, COLS, 8]),
                                   ALU.mult))
            link(dve.reduce_sum(dst, oneb[:, :, :], AX))

        link(dve.reduce_sum(tab[:, 0, :], oneh[:, :, :], AX))
        of_item(tab[:, 1, :], erow)
        of_item(tab[:, 3, :], starti)
        of_item(tab[:, 4, :], cnts)
        link(dve.tensor_tensor(tab[:, 5, :], itn[:, :], tab[:, 3, :], ALU.subtract))
        link(dve.tensor_scalar(tab[:, 5, :], tab[:, 5, :], float(BLK), None, ALU.mult))
        link(dve.tensor_tensor(tab[:, 4, :], tab[:, 4, :], tab[:, 5, :], ALU.subtract))
        link(dve.tensor_scalar(tab[:, 2, :], tab[:, 4, :], float(P), None, ALU.is_gt))
        link(dve.tensor_copy(tabi[:, :, :], tab[:, :, :]))
        for b in range(4):
            link(dve.tensor_tensor(oneb[:, :, :], oneh[:, :, :],
                                   posn[:, b, :].unsqueeze(1).broadcast_to([P, COLS, 8]), ALU.mult))
            link(dve.reduce_sum(posi[:, b, :], oneb[:, :, :], AX))
            link(dve.tensor_tensor(oneb[:, :, :], oneh[:, :, :],
                                   comb[:, b, :].unsqueeze(1).broadcast_to([P, COLS, 8]), ALU.mult))
            link(dve.reduce_sum(cmbi[:, b, :], oneb[:, :, :], AX))
            link(dve.tensor_tensor(posi[:, b, :], posi[:, b, :], tab[:, 5, :], ALU.subtract))
            link(dve.tensor_scalar(posi[:, b, :], posi[:, b, :], -1.0, None, ALU.add))
        dve.tensor_copy(cmbi[:, 0, 0:1], cmbi[:, 0, 0:1]).then_inc(E["tab"], 1)
        phase_end(dve, "router")

        def selection(g):
            for b in range(4):
                ins = dve.tensor_scalar(gm[:, b, :], iot[:, :], posi[:, b, ds(g, 1)], None, ALU.is_equal)
            ins.then_inc(E["gm"], 1)

        def gathered_lo(g, ks):
            for k in ks:
                dve.wait_ge(E["xhi"], g * 8 + (k + 1))
                dve.tensor_tensor(xg[1][:, k, :], bank(GATHER_BANKS[k % 3], 0, BLK), xg[0][:, k, :].bitcast(F32),
                                  ALU.subtract).then_inc(E["xlo"], 1)

        def item(it, N):
            J = N // P

            def mid(c):
                if c == 0:
                    dve.wait_ge(E["ws"], it + 1)
                    dve.tensor_copy(wslot[:, 0:J], bank(5, 0, J)).then_inc(E["wsc"], 1)

            def between(c):
                if c == 1:
                    dve.wait_ge(E["sc"], it + 1)
                    selection(it + 1)

            ffn_dve(dve, "exp", it * EX_CHUNKS, AT["exp"], N, mid, between, first=False)
            gathered_lo(it + 1, range(3))
            for part in range(2):
                yb, j, a, b = y_part(J, part)
                dve.wait_ge(E["yhi"], it * 2 + (part + 1))
                dve.tensor_tensor(yhl[1][:, j, a:b], yx[part][:, a:b], yhl[0][:, j, a:b].bitcast(F32), ALU.subtract
                                  ).then_inc(E["ylo"], 1)
            gathered_lo(it + 1, range(3, KC))
            for m in range(KC):
                dve.wait_ge(E["sct"], it * 8 + (m + 1))
                dve.scalar_tensor_tensor(out=res[:, m, 0:SEQ], in0=bank(m % 4, 0, 512),
                                         scalar=mods[:, 1, 5 * KC + m, 0:1], in1=res[:, m, 0:SEQ],
                                         op0=ALU.mult, op1=ALU.add).then_inc(E["scev"], 1)

        selection(0)
        gathered_lo(0, range(KC))
        items(dve, item)
        phase_end(dve, "moe")

    @block.gpsimd
    def _(pool):
        for name in ("mods0", "norm0", "ain", "lat", "four"):
            phase_end(pool, name)

        def pair0(i, nxt):
            A = a_sem[0]

            def queries_lo(h):
                pool.wait_ge(A["qhi"], i * 2 + (h + 1))
                pool.tensor_tensor(q0[1][:, h, :], qx0[h][:, :], q0[0][:, h, :].bitcast(F32), ALU.subtract
                                   ).then_inc(A["qlo"], 1)

            queries_lo(0)
            pool.wait_ge(A["rk"], i + 1)
            pool.tensor_tensor(kx0[1][:, :], krope[:, :], rk0[:, :], ALU.mult).then_inc(A["kr"], 1)
            queries_lo(1)
            att_pool(pool, 0, i, nxt)

        pairs(pool, 0, pair0)
        for name in ("att0", "split0", "out0", "mlp", "mods1", "norm1"):
            phase_end(pool, name)
        pairs(pool, 1, lambda i, nxt: att_pool(pool, 1, i, nxt))
        for name in ("att1", "split1", "out1", "router"):
            phase_end(pool, name)

        def item(it, N):
            for r in range(2):
                lo_unit(pool, r, raw[0][:, r, :], U, it * EX_CHUNKS + (AT["exp"].u[r] + 1))

        items(pool, item)
        phase_end(pool, "moe")


def _unit(w, m):
    k = w.shape[0] // P
    return w[:, m * P:(m + 1) * P].reshape(k, P, P).transpose(1, 0, 2).reshape(P, k * P)


def _swap(n):
    return np.arange(n) ^ 1


def layout(x, c, ctx, c_ctx, w_mod, b_mod, norm_g, a_w_in, a_g_cq, a_g_ckv, a_w_uq, a_w_ukv, a_g_q, a_g_k,
           a_w_out, f_w_gate, f_w_up, f_w_down, c_w_in, c_g_q, c_g_k, c_rpb, c_w_out, m_w_router, m_w_gate,
           m_w_up, m_w_down):
    f = np.float32
    order = np.arange(SEQ).reshape(ROWS, GRID_W).T.reshape(-1)
    a = {}
    tok = np.concatenate([x[0][order], ctx[0]], axis=0)
    a["xT"] = tok.T.reshape(KC, P, T).transpose(1, 0, 2)
    a["cond"] = np.stack([c[0], c_ctx], axis=-1).reshape(KC, P, 2).transpose(1, 0, 2)
    a["bmod"] = b_mod.reshape(2, 48, P).transpose(2, 0, 1)
    a["ng"] = norm_g.reshape(2, 2, KC, P).transpose(3, 0, 1, 2)
    g = np.ones((P, 8), f)
    sw = _swap(A_ROPE)
    g[:, 0:2] = a_g_cq[0].reshape(2, P).T
    g[:, 2] = a_g_ckv[0]
    g[0:96, 3] = a_g_q[0]
    g[96:128, 3] = a_g_q[0][64:][sw]
    g[:, 4] = np.tile(a_g_k[0][0:64], 2)
    rope = a_g_k[0][64:]
    g[:, 5] = np.concatenate([rope[sw], rope[sw], rope, rope])
    g[:, 6] = np.tile(c_g_q[0], 2)
    g[:, 7] = np.tile(c_g_k[0], 2)
    a["gcol"] = g
    a["ident"] = np.eye(P, dtype=f)
    a["ones"] = np.ones((P, P), f)
    o96 = np.zeros((P, P), f)
    o96[0:96] = 1
    a["ones96"] = o96
    o64 = np.zeros((P, P), f)
    o64[0:64, 0:64] = 1
    o64[64:, 64:] = 1
    a["ones64"] = o64
    onr = np.zeros((P, P), f)
    onr[64:96] = 1
    a["onesr"] = onr
    h2 = np.zeros((P, 2), f)
    h2[0:64, 0] = 1
    h2[64:, 1] = 1
    a["half2"] = h2
    hl = np.zeros((P, 2), f)
    hl[[0, 2], 0] = 1
    hl[[1, 3], 1] = 1
    a["hl_sum"] = hl
    a["eps"] = np.tile(np.array([EPS, A_QK * EPS, DH * EPS], f), (P, 1))
    inv = 10000.0 ** (-np.arange(8, dtype=np.float64) / 8)
    ang = np.concatenate([(order // GRID_W)[:, None] * inv, (order % GRID_W)[:, None] * inv], axis=1)
    cos = np.ones((A_ROPE, T))
    sin = np.zeros((A_ROPE, T))
    cos[:, 0:SEQ] = np.repeat(np.cos(ang).T, 2, axis=0)
    sin[:, 0:SEQ] = np.repeat(np.sin(ang).T, 2, axis=0) * np.tile([-1.0, 1.0], 16)[:, None]
    a["qtab"] = np.concatenate([np.ones((64, T)), cos, sin]).astype(f)
    a["ktab"] = np.concatenate([sin, sin, cos, cos]).astype(f)
    rows = []

    def triple(*units):
        t = np.zeros((P, 3, U), f)
        for n, u in enumerate(units):
            t[:, n, 0:u.shape[1]] = u
        rows.append(t.reshape(P, 3 * U))

    def triples(units):
        for n in range(0, len(units), 3):
            triple(*units[n:n + 3])

    def mod_units(w):
        return [np.concatenate([w[(2 * q + h) * P:(2 * q + h + 1) * P, b * 512:(b + 1) * 512] for h in range(2)],
                               axis=1) for b in range(12) for q in range(4)]

    triples(mod_units(w_mod[0]))
    w = a_w_in[0]
    kr = w[:, 384:416]
    w_in = np.concatenate([w[:, 0:384], kr[:, sw], kr[:, sw], kr, kr, w[:, 416:672]], axis=1)
    triples([_unit(w_in, m) for m in range(6)])
    uq = a_w_uq[0].reshape(A_QR, A_HEADS, A_QK)
    uq = np.concatenate([uq, uq[:, :, 64:][:, :, sw]], axis=2)
    ukv = a_w_ukv[0].reshape(A_KVR, A_HEADS, 128)
    for i in range(PAIRS0):
        q = np.concatenate([uq[kc * P:(kc + 1) * P, 2 * i + h] for h in range(2) for kc in range(2)], axis=1)
        ka, kb = ukv[:, 2 * i, 0:64], ukv[:, 2 * i + 1, 0:64]
        v = np.concatenate([ukv[:, 2 * i, 64:], ukv[:, 2 * i + 1, 64:]], axis=1)
        triple(q, np.concatenate([ka, kb], axis=1), v)
    triples([_unit(a_w_out[0], m) for m in range(8)])
    for cch in range(FF_CHUNKS):
        triple(_unit(f_w_gate[0], cch), _unit(f_w_up[0], cch), f_w_down[0][cch * P:(cch + 1) * P])
    triples(mod_units(w_mod[1]))
    for i in range(PAIRS1):
        triple(*[_unit(c_w_in[0][:, s * D:(s + 1) * D], i) for s in range(3)])
    triples([_unit(c_w_out[0], m) for m in range(8)])
    for e in range(EXPERTS):
        for cch in range(EX_CHUNKS):
            triple(_unit(m_w_gate[0, e], cch), _unit(m_w_up[0, e], cch), m_w_down[0, e][cch * P:(cch + 1) * P])
    a["stream"] = np.stack(rows)
    assert a["stream"].shape[0] == TR_END
    units = []
    ch = 2 * np.pi * np.outer(np.arange(64), np.arange(64)) / 64
    z = np.zeros((64, 64))
    units.append(np.concatenate([np.block([[fn(ch), z], [z, fn(ch)]]) for fn in (np.cos, np.sin)], axis=1))
    th = 2 * np.pi * ((order[:, None] * order[None, :]) % SEQ) / SEQ
    for fn, sign in ((np.cos, 1), (np.sin, -1)):
        m = sign * fn(th) / np.sqrt(SEQ * 64)
        for u in range(2):
            units.append(np.concatenate([m[(2 * u + kb) * P:(2 * u + kb + 1) * P] for kb in range(2)], axis=1))
    tc = np.arange(CTX)
    th = 2 * np.pi * ((tc[:, None] * tc[None, :]) % CTX) / CTX
    units.append(np.concatenate([s * fn(th)[kb * P:(kb + 1) * P] / np.sqrt(CTX * 64)
                                 for fn, s in ((np.cos, 1), (np.sin, -1)) for kb in range(2)], axis=1))
    fo = np.zeros((2, P, 3, U), f)
    for n, u in enumerate(units):
        fo[n // 3, :, n % 3, 0:u.shape[1]] = u
    a["fourier"] = fo.reshape(2, P, 3 * U)
    qi = np.arange(P)
    tiles = []
    for b, kbs in ((0, (0, 1)), (1, (0, 1, 2)), (3, (2, 3))):
        cq_, rq_ = b * 16 + qi // 8, qi % 8
        start = np.clip(cq_ - WIN_C // 2, 0, GRID_W - WIN_C)
        for kb in kbs:
            ck, rk = kb * 16 + qi // 8, qi % 8
            inside = (ck[None, :] >= start[:, None]) & (ck[None, :] < start[:, None] + WIN_C)
            dr = rk[None, :] - rq_[:, None] + WIN_R - 1
            dc = np.clip(ck[None, :] - cq_[:, None] + WIN_C - 1, 0, 2 * WIN_C - 2)
            t = c_rpb[0][:, dr, dc]
            tiles.append(np.where(inside[None], t, f(-BIG)))
    bias = np.concatenate(tiles, axis=2)
    a["bias"] = bias.reshape(PAIRS1, 2, P, BIAS_TILES * P).transpose(0, 2, 1, 3)
    a["wr"] = m_w_router[0].reshape(KC, P, 8).transpose(1, 0, 2)
    a["tri"] = np.triu(np.ones((P, P), f), 1)
    a["iot"] = np.tile(np.arange(BLK, dtype=f), (P, 1))
    a["ltj"] = np.tile(np.tril(np.ones((8, 8), f), -1), (P, 1, 1))
    a["itn"] = np.tile(np.arange(COLS, dtype=f), (P, 1))
    a["erow"] = np.tile(TR_EXP + EX_CHUNKS * np.arange(8, dtype=f), (P, 1))
    return {k: np.ascontiguousarray(v, dtype=f) for k, v in a.items()}, order


def kernel(**inputs):
    import concourse.bacc as bacc
    from concourse.bass_utils import run_bass_kernel_spmd as run

    arrays, order = layout(**{k: np.asarray(v) for k, v in inputs.items()})
    nc = bacc.Bacc("TRN2", target_bir_lowering=False, num_devices=1)
    io = {n: nc.dram_tensor(n, v.shape, F32, kind="ExternalInput").ap() for n, v in arrays.items()}
    io["out"] = nc.dram_tensor("out", (P, KC, SEQ), F32, kind="ExternalOutput").ap()
    build(nc, io)
    r = run(nc, [arrays], core_ids=[0])
    y = r.results[0]["out"].transpose(1, 0, 2).reshape(D, SEQ)
    out = np.empty((1, SEQ, D), y.dtype)
    out[0, order] = y.T
    return out
```
